# Optimizing a Trainium2 kernel written in Bass

```python
import jax, jax.numpy as jnp
from jax import lax
import numpy as np

D_MODEL = 2048
BATCH = 1
SEQ = 512
DEPTH = 1

HEAD_DIM = 128
GDN_HEADS = 8
GDN_WIDTH = GDN_HEADS * HEAD_DIM
GDN_CONV = 4
GDN_CHUNK = 64
MOBA_HEADS = 8
MOBA_WIDTH = MOBA_HEADS * HEAD_DIM
MOBA_BLOCK = 256
MOBA_TOPK = 3
MOBA_QCHUNK = 32
ROPE_THETA = 10000.0
EPS = 1e-6
N_BRANCH = 2

SPLIT_SIZES = [3 * GDN_WIDTH, GDN_WIDTH, GDN_HEADS, GDN_HEADS,
               3 * MOBA_WIDTH, MOBA_WIDTH, N_BRANCH * D_MODEL]
SPLIT_POINTS = [int(s) for s in np.cumsum(SPLIT_SIZES)[:-1]]
IN_COLS = int(sum(SPLIT_SIZES))

kernel_name = "hybrid_gdn_moba_gated_merge"

def rms_norm(x, w):
    xf = x.astype(jnp.float32)
    y = xf * lax.rsqrt(jnp.mean(xf * xf, axis=-1, keepdims=True) + EPS) * w.astype(jnp.float32)
    return y.astype(x.dtype)

def l2_norm(x):
    xf = x.astype(jnp.float32)
    return xf * lax.rsqrt(jnp.sum(xf * xf, axis=-1, keepdims=True) + EPS)

def causal_depthwise_conv(x, w):
    k_width, ch = w.shape
    return lax.conv_general_dilated(
        x, w[:, None, :].astype(x.dtype), window_strides=(1,), padding=[(k_width - 1, 0)],
        dimension_numbers=("NWC", "WIO", "NWC"), feature_group_count=ch)

def rope(x):
    t_len, d = x.shape[1], x.shape[3]
    inv_freq = ROPE_THETA ** (-jnp.arange(0, d, 2, dtype=jnp.float32) / d)
    ang = jnp.arange(t_len, dtype=jnp.float32)[:, None] * inv_freq[None, :]
    cos = jnp.cos(ang)[None, :, None, :]
    sin = jnp.sin(ang)[None, :, None, :]
    xf = x.astype(jnp.float32)
    x1, x2 = xf[..., : d // 2], xf[..., d // 2:]
    return jnp.concatenate([x1 * cos - x2 * sin, x2 * cos + x1 * sin], axis=-1).astype(x.dtype)

def gated_delta_rule(q, k, v, g, beta):
    b_sz, t_len, n_h, d_k = q.shape
    d_v = v.shape[-1]
    c = GDN_CHUNK
    n_c = t_len // c

    def to_chunks(t):
        return t.astype(jnp.float32).reshape(b_sz, n_c, c, n_h, -1).transpose(1, 0, 3, 2, 4)

    q = to_chunks(q) * (d_k ** -0.5)
    k = to_chunks(k)
    v = to_chunks(v)
    g = g.astype(jnp.float32).reshape(b_sz, n_c, c, n_h).transpose(1, 0, 3, 2)
    beta = beta.astype(jnp.float32).reshape(b_sz, n_c, c, n_h).transpose(1, 0, 3, 2)

    cum_g = jnp.cumsum(g, axis=-1)
    causal = jnp.tril(jnp.ones((c, c), dtype=bool))
    strict = jnp.tril(jnp.ones((c, c), dtype=bool), k=-1)
    decay_mat = jnp.exp(jnp.where(causal, cum_g[..., :, None] - cum_g[..., None, :], -jnp.inf))

    kk = jnp.einsum("nbhid,nbhjd->nbhij", k, k)
    a_mat = jnp.where(strict, beta[..., :, None] * kk * decay_mat, 0.0)
    eye = jnp.eye(c, dtype=jnp.float32)
    rhs = jnp.concatenate([v * beta[..., None], k * (beta * jnp.exp(cum_g))[..., None]], axis=-1)
    sol = lax.linalg.triangular_solve(eye + a_mat, rhs, left_side=True, lower=True,
                                      unit_diagonal=True)
    u, w = sol[..., :d_v], sol[..., d_v:]

    qk = jnp.einsum("nbhid,nbhjd->nbhij", q, k) * decay_mat
    q_dec = q * jnp.exp(cum_g)[..., None]
    k_dec = k * jnp.exp(cum_g[..., -1:] - cum_g)[..., None]
    g_last = jnp.exp(cum_g[..., -1])

    def step(state, xs):
        q_c, k_c, u_c, w_c, qk_c, gl_c = xs
        v_new = u_c - jnp.einsum("bhcd,bhde->bhce", w_c, state)
        o_c = jnp.einsum("bhcd,bhde->bhce", q_c, state) + jnp.einsum("bhij,bhje->bhie", qk_c, v_new)
        state = state * gl_c[..., None, None] + jnp.einsum("bhcd,bhce->bhde", k_c, v_new)
        return state, o_c

    s0 = jnp.zeros((b_sz, n_h, d_k, d_v), jnp.float32)
    _, o = lax.scan(step, s0, (q_dec, k_dec, u, w, qk, g_last))
    return o.transpose(1, 0, 3, 2, 4).reshape(b_sz, t_len, n_h, d_v)

def moba_attention(q, k, v):
    b_sz, t_len, n_h, d = q.shape
    bs = MOBA_BLOCK
    n_blk = -(-t_len // bs)
    pad = n_blk * bs - t_len
    n_sel = max(1, min(MOBA_TOPK, n_blk - 1))
    qc = MOBA_QCHUNK
    n_qc = t_len // qc
    scale = d ** -0.5

    q = q.transpose(0, 2, 1, 3)
    k = jnp.pad(k.transpose(0, 2, 1, 3), ((0, 0), (0, 0), (0, pad), (0, 0)))
    v = jnp.pad(v.transpose(0, 2, 1, 3), ((0, 0), (0, 0), (0, pad), (0, 0)))
    k_blocks = k.reshape(b_sz, n_h, n_blk, bs, d)
    v_blocks = v.reshape(b_sz, n_h, n_blk, bs, d)
    k_mean = jnp.mean(k_blocks.astype(jnp.float32), axis=3)

    q_blk = jnp.arange(t_len) // bs
    gate = jnp.einsum("bhtd,bhnd->bhtn", q.astype(jnp.float32), k_mean)
    gate = jnp.where(jnp.arange(n_blk)[None, :] < q_blk[:, None], gate, -jnp.inf)
    _, sel = lax.top_k(gate, n_sel)

    bi = jnp.arange(b_sz)[:, None, None, None]
    hi = jnp.arange(n_h)[None, :, None, None]

    def attend(args):
        q_c, sel_c, start = args
        pos = start + jnp.arange(qc)
        blk = start // bs
        k_own = lax.dynamic_slice_in_dim(k, blk * bs, bs, axis=2)
        v_own = lax.dynamic_slice_in_dim(v, blk * bs, bs, axis=2)
        s_own = jnp.einsum("bhqd,bhkd->bhqk", q_c, k_own).astype(jnp.float32) * scale
        s_own = jnp.where((blk * bs + jnp.arange(bs))[None, :] <= pos[:, None], s_own, -jnp.inf)
        k_sel = k_blocks[bi, hi, sel_c]
        v_sel = v_blocks[bi, hi, sel_c]
        s_sel = jnp.einsum("bhqd,bhqnkd->bhqnk", q_c, k_sel).astype(jnp.float32) * scale
        valid = jnp.arange(n_sel) < blk
        s_sel = jnp.where(valid[None, None, None, :, None], s_sel, -jnp.inf)
        s_sel = s_sel.reshape(b_sz, n_h, qc, n_sel * bs)
        p = jax.nn.softmax(jnp.concatenate([s_sel, s_own], axis=-1), axis=-1)
        p_sel = p[..., : n_sel * bs].reshape(b_sz, n_h, qc, n_sel, bs).astype(v.dtype)
        p_own = p[..., n_sel * bs:].astype(v.dtype)
        return (jnp.einsum("bhqnk,bhqnkd->bhqd", p_sel, v_sel)
                + jnp.einsum("bhqk,bhkd->bhqd", p_own, v_own))

    q_chunks = q.reshape(b_sz, n_h, n_qc, qc, d).transpose(2, 0, 1, 3, 4)
    sel_chunks = sel.reshape(b_sz, n_h, n_qc, qc, n_sel).transpose(2, 0, 1, 3, 4)
    starts = jnp.arange(n_qc, dtype=jnp.int32) * qc
    o = lax.map(attend, (q_chunks, sel_chunks, starts))
    return o.transpose(1, 0, 3, 2, 4).reshape(b_sz, t_len, n_h, d)

def setup_inputs(seed: int = 0) -> dict:
    key = jax.random.key(seed)
    ks = jax.random.split(key, 14)
    f32 = jnp.float32
    x = jax.random.normal(ks[0], (BATCH, SEQ, D_MODEL), f32)
    norm_w = 1.0 + 0.02 * jax.random.normal(ks[1], (DEPTH, D_MODEL), f32)
    w_in = jax.random.normal(ks[2], (DEPTH, D_MODEL, IN_COLS), f32) * D_MODEL ** -0.5
    gdn_conv_w = jax.random.normal(ks[3], (DEPTH, GDN_CONV, 3 * GDN_WIDTH), f32) * GDN_CONV ** -0.5
    gdn_a_log = jnp.log(jax.random.uniform(ks[4], (DEPTH, GDN_HEADS), f32, 1.0, 16.0))
    dt = jnp.exp(jax.random.uniform(ks[5], (DEPTH, GDN_HEADS), f32, np.log(1e-3), np.log(1e-1)))
    gdn_dt_bias = dt + jnp.log(-jnp.expm1(-dt))
    gdn_norm_w = 1.0 + 0.02 * jax.random.normal(ks[6], (DEPTH, HEAD_DIM), f32)
    moba_q_norm_w = 1.0 + 0.02 * jax.random.normal(ks[7], (DEPTH, HEAD_DIM), f32)
    moba_k_norm_w = 1.0 + 0.02 * jax.random.normal(ks[8], (DEPTH, HEAD_DIM), f32)
    w_out_gdn = jax.random.normal(ks[9], (DEPTH, GDN_WIDTH, D_MODEL), f32) * GDN_WIDTH ** -0.5
    w_out_moba = jax.random.normal(ks[10], (DEPTH, MOBA_WIDTH, D_MODEL), f32) * MOBA_WIDTH ** -0.5
    w_o = jax.random.normal(ks[11], (DEPTH, D_MODEL, D_MODEL), f32) * D_MODEL ** -0.5
    return {"x": x, "norm_w": norm_w, "w_in": w_in, "gdn_conv_w": gdn_conv_w,
            "gdn_a_log": gdn_a_log, "gdn_dt_bias": gdn_dt_bias, "gdn_norm_w": gdn_norm_w,
            "moba_q_norm_w": moba_q_norm_w, "moba_k_norm_w": moba_k_norm_w,
            "w_out_gdn": w_out_gdn, "w_out_moba": w_out_moba, "w_o": w_o}

def reference(x, norm_w, w_in, gdn_conv_w, gdn_a_log, gdn_dt_bias, gdn_norm_w,
              moba_q_norm_w, moba_k_norm_w, w_out_gdn, w_out_moba, w_o):
    b_sz, t_len, _ = x.shape
    for l in range(DEPTH):
        h = rms_norm(x, norm_w[l])
        proj = jnp.einsum("btd,dc->btc", h, w_in[l])
        gdn_qkv, gdn_z, gdn_b, gdn_a, moba_qkv, moba_z, gates = jnp.split(proj, SPLIT_POINTS, axis=-1)

        qkv = jax.nn.silu(causal_depthwise_conv(gdn_qkv, gdn_conv_w[l]))
        qa, ka, va = jnp.split(qkv, 3, axis=-1)
        qa = l2_norm(qa.reshape(b_sz, t_len, GDN_HEADS, HEAD_DIM))
        ka = l2_norm(ka.reshape(b_sz, t_len, GDN_HEADS, HEAD_DIM))
        va = va.reshape(b_sz, t_len, GDN_HEADS, HEAD_DIM)
        beta = jax.nn.sigmoid(gdn_b.astype(jnp.float32))
        g = -jnp.exp(gdn_a_log[l].astype(jnp.float32)) * jax.nn.softplus(
            gdn_a.astype(jnp.float32) + gdn_dt_bias[l].astype(jnp.float32))
        oa = gated_delta_rule(qa, ka, va, g, beta)
        oa = rms_norm(oa, gdn_norm_w[l]).astype(x.dtype)
        oa = oa.reshape(b_sz, t_len, GDN_WIDTH) * jax.nn.silu(gdn_z)
        y_gdn = jnp.einsum("btc,cd->btd", oa, w_out_gdn[l])

        qb, kb, vb = jnp.split(moba_qkv, 3, axis=-1)
        qb = rope(rms_norm(qb.reshape(b_sz, t_len, MOBA_HEADS, HEAD_DIM), moba_q_norm_w[l]))
        kb = rope(rms_norm(kb.reshape(b_sz, t_len, MOBA_HEADS, HEAD_DIM), moba_k_norm_w[l]))
        vb = vb.reshape(b_sz, t_len, MOBA_HEADS, HEAD_DIM)
        ob = moba_attention(qb, kb, vb).reshape(b_sz, t_len, MOBA_WIDTH) * jax.nn.silu(moba_z)
        y_moba = jnp.einsum("btc,cd->btd", ob, w_out_moba[l])

        g_gdn, g_moba = jnp.split(gates, N_BRANCH, axis=-1)
        merged = jax.nn.sigmoid(g_gdn) * y_gdn + jax.nn.sigmoid(g_moba) * y_moba
        x = x + jnp.einsum("btd,de->bte", merged, w_o[l])
    return x


_drawn_inputs = setup_inputs


def setup_inputs(seed=0):
    import zlib

    import numpy as np

    out = dict(_drawn_inputs(seed))
    spreads = {}
    factors = {'norm_w': 5.157, 'gdn_norm_w': 8.0, 'moba_q_norm_w': 8.0, 'moba_k_norm_w': 8.0}
    for name, (base, spread) in spreads.items():
        noise = np.random.default_rng([zlib.crc32(name.encode()), seed]).standard_normal(out[name].shape)
        drawn = base * np.exp(spread * noise) if base else spread * noise
        out[name] = __import__('jax').numpy.asarray(drawn.astype(out[name].dtype))
    for name, factor in factors.items():
        out[name] = (out[name] * factor).astype(out[name].dtype)
    return out
```

```python
from contextlib import ExitStack

import numpy as np

import concourse.bass as bass
from concourse import mybir

F32 = mybir.dt.float32
F32R = mybir.dt.float32r
ALU = mybir.AluOpType
ACT = mybir.ActivationFunctionType
AX_X = mybir.AxisListType.X

P = 128
D = 2048
T = 512
NT = T // P
KT = D // P
H = 8
W = H * P
EPS = 1e-6
NEG = -1e30
LEAST = -43.0
COL_GDN = 0
COL_BETA = 4 * W
COL_MOBA = COL_BETA + 2 * H
COL_GATE = COL_MOBA + 4 * W
IN_COLS = COL_GATE + 2 * D
SCALE = float(P) ** -0.5
LNSCALE = float(np.log(SCALE))

STRIPES = (("gk", COL_GDN + W), ("gq", COL_GDN), ("gv", COL_GDN + 2 * W), ("gz", COL_GDN + 3 * W),
           ("bk", COL_MOBA + W), ("bq", COL_MOBA), ("bv", COL_MOBA + 2 * W), ("bz", COL_MOBA + 3 * W))
NW = len(STRIPES)
N1 = NW * H
N2 = N1 + 4
N3 = N2 + 3 * KT - 4
BA_G = 11
OCH = 2 * H * T // D
MCH = KT * T // D

(C_ID, C_TRIU, C_DMASK, C_CMASK, C_STRICT, C_M16, C_L32, C_L64, C_L128) = range(9)
NCONST = 9
(HC_G, HC_CG, HC_B, HC_NB, HC_BE, HC_KD, HC_GL) = range(7)
NHC = 7
R_CONV, R_NW, R_GW, R_QW, R_KW = 0, 96, 112, 113, 114

SEMS = """
 consts rows_loaded rows_set rows_T rows_ready ab_loaded x_loaded0 x_loaded1 x_sq x_ln x_rstd x_scaled
 x_T x_evac x_hi x_lo w16_loaded w16_hi w16_lo ba_mm ba_step cg_mm hc_set ones_set pads
 raw_loaded0 raw_loaded1 y_loaded0 y_loaded1 hi_ready lo_ready win_done win_evac
 hcol cgrow_mm cg_arg cg_eg cg_dt cg_dts
 conv clampd sig silu sqd ss_mm rn_ln rn norm
 kT_mm kbe kdec kk_mm kkd qk_mm qkd qdec UT_mm Ln LT_mm Ud Ld X1 L32m L64m L128m
 n1_mm L2 U2 n2_mm X2 L4 U4 n3_mm X4 L8 n4_mm X8 ma_mm Y XT mb_mm X
 vT_mm vb wT_mm nwT vn_mm vn st_mm st o_mm o_sq o_ss o_ln o_rn o_1 o_2 o_out
 zclamp zsig zs
 b_sq b_ss b_ln b_rn b_n b_cos b_sinlo b_sinhi b_rope bvT_mm bvT
 s_mm s_mask s_max s_nmax s_exp s_rec s_norm pT_mm pT pv_mm ob ob_out
 g_evac g_sig ya yb mg mg_out
 act_loaded0 act_loaded1 act_hi act_lo
 p3_done resid x3_loaded out_stored
""".split()


def hybrid_layer(nc, x, norm_w, w_in, gdn_conv_w, gdn_a_log, gdn_dt_bias, gdn_norm_w, moba_q_norm_w,
                 moba_k_norm_w, w_out_gdn, w_out_moba, w_o, consts, rope, out):
    xs = x[0]
    outs = out[0]
    w_in3 = w_in[0].rearrange("(k p) c -> p k c", p=P)
    wg3 = w_out_gdn[0].rearrange("(k p) c -> p k c", p=P)
    wm3 = w_out_moba[0].rearrange("(k p) c -> p k c", p=P)
    wo3 = w_o[0].rearrange("(k p) c -> p k c", p=P)
    o_dram = nc.dram_tensor("branch_outputs", (2 * H, P, T), F32, kind="Internal").ap()
    m_dram = nc.dram_tensor("merged", (KT, P, T), F32, kind="Internal").ap()

    ctx = ExitStack()
    with ctx:
        def sb(name, shape, dt=F32, at=ctx):
            return at.enter_context(nc.sbuf_tensor(name, shape, dt))

        s = {n: ctx.enter_context(nc.semaphore(n)) for n in SEMS}
        bank = [ctx.enter_context(nc.psum_tensor(f"bank{i}", [P, 512], F32)) for i in range(8)]
        PJ = bank[0:2]
        G0, G1, G2 = bank[2:5]
        A0, A1, A2 = bank[5:8]

        h_hi = sb("h_hi", [P, KT, T], F32R)
        h_lo = sb("h_lo", [P, KT, T], F32R)
        raw = [sb(f"w_raw{i}", [P, D]) for i in range(2)]
        w_hi = [sb(f"w_hi{i}", [P, D], F32R) for i in range(2)]
        w_lo = [sb(f"w_lo{i}", [P, D], F32R) for i in range(2)]
        ones = sb("ones", [P, P])
        mean = sb("mean", [P, P])
        chan = sb("chan", [P, P])
        hc = sb("hc", [P, H, NHC, NT])
        eps = sb("eps", [P, 1])
        lnscale = sb("lnscale", [P, 1])
        sg = sb("sg", [P, 2, 2, T])
        mgt = sb("mgt", [P, 2, T])

        area = ExitStack()
        tmp = ExitStack()
        xt = sb("x_tiles", [P, 2, D], at=tmp)
        xsq = sb("x_square", [P, D], at=tmp)
        ssx = sb("x_stats", [P, NT], at=tmp)
        rsx = sb("x_rstd", [P, NT], at=tmp)
        htmp = sb("h_tmp", [P, 2, 512], at=tmp)
        w16 = sb("w16", [P, KT, 2 * H], at=tmp)
        w16h = sb("w16h", [P, KT, 2 * H], F32R, at=tmp)
        w16l = sb("w16l", [P, KT, 2 * H], F32R, at=tmp)
        rows = sb("rows", [P, P], at=tmp)
        alog = sb("alog", [P, H], at=tmp)
        dtb = sb("dtb", [P, H], at=tmp)
        ba = sb("ba", [P, 6, NT, H], at=tmp)
        tmp.close()

        rawc = {k: sb(f"raw_{k}", [P, T + 4], at=area) for k in ("gk", "gq", "gv")}
        cv = {k: sb(f"conv_{k}", [P, T], at=area) for k in ("gk", "gq", "gv")}
        dT = sb("decayT", [P, T], at=area)
        w0_, w1_, w2_, w3_, w4_ = [sb(f"work{i}", [P, T], at=area) for i in range(5)]
        xa = sb("inv_a", [P, T], at=area)
        xb = sb("inv_b", [P, T], at=area)
        lm = [sb(f"lower{i}", [P, T], at=area) for i in range(3)]
        kbe = sb("k_beta_decay", [P, T], at=area)
        kdec = sb("k_decay", [P, T], at=area)
        vb = sb("v_beta", [P, T], at=area)
        qdec = sb("q_decay", [P, T], at=area)
        qkT = sb("qkT", [P, T], at=area)
        st = [sb(f"state{i}", [P, P], at=area) for i in range(2)]
        zA = sb("zA", [P, T], at=area)
        zB = sb("zB", [P, T], at=area)
        zt = sb("z_tmp", [P, T], at=area)
        pt = sb("pt", [P, 4, T], at=area)
        bv = sb("bv", [P, T], at=area)
        pr1 = sb("probs1", [P, T], at=area)
        kr = sb("k_rope", [P, T], at=area)
        qr = sb("q_rope", [P, T], at=area)
        vT = sb("vT", [P, T], at=area)
        stat = sb("softmax_stats", [P, 4, NT], at=area)
        hcol = sb("hcol", [P, NHC, NT], at=area)
        cst = sb("cst", [P, NCONST, P], at=area)
        cossin = sb("cossin", [P, 2, T], at=area)
        area.close()

        late = ExitStack()
        o_hi = sb("o_hi", [P, 2 * H, T], F32R, at=late)
        o_lo = sb("o_lo", [P, 2 * H, T], F32R, at=late)
        act_raw = sb("act_raw", [P, 2, D], at=late)
        late.close()
        last = ExitStack()
        x3 = sb("x_residual", [P, NT, 512], at=last)
        y3 = sb("out_tiles", [P, NT, 512], at=last)
        last.close()

        ident, triu = cst[:, C_ID, :], cst[:, C_TRIU, :]
        cos, sin = cossin[:, 0, :], cossin[:, 1, :]
        Eg, L2, Yt = w2_, w2_, w2_
        dTs, L4, nwT = w0_, w0_, w0_
        Up, U2, XTt = w1_, w1_, w1_
        Ud, U4, vn = w3_, w3_, w3_
        Ld, L8, o1 = w4_, w4_, w4_
        Ln = lm[0]
        probs = [bv, pr1]
        dest = {"gk": rawc["gk"][:, 4:], "gq": rawc["gq"][:, 4:], "gv": rawc["gv"][:, 4:], "gz": zA[:],
                "bk": pt[:, 0, :], "bq": pt[:, 1, :], "bv": bv[:], "bz": zB[:]}

        def tile4(t):
            return slice(t * P, (t + 1) * P)

        def q4(ap):
            return ap[:].rearrange("p (t c) -> p t c", t=NT)

        def over(ap):
            return ap.unsqueeze(1).broadcast_to([P, NT, P])

        def hcb(kind):
            return hcol[:, kind, :].unsqueeze(2).broadcast_to([P, NT, P])

        block = ctx.enter_context(nc.Block())

        @block.sync
        def _(sp):
            sp.dma_start(xt[:, 0, :], xs[0:P, :]).then_inc(s["x_loaded0"], 16)
            sp.dma_start(xt[:, 1, :], xs[P:2 * P, :]).then_inc(s["x_loaded1"], 16)
            sp.dma_start(cst[:], consts).then_inc(s["consts"], 16)
            sp.dma_start(cossin[:], rope).then_inc(s["consts"], 16)
            sp.wait_ge(s["rows_set"], 1)
            for row, src in ((R_CONV, gdn_conv_w[0].rearrange("j (c p) -> (j c) p", p=P)),
                             (R_NW, norm_w[0].rearrange("(c p) -> c p", p=P)),
                             (R_GW, gdn_norm_w), (R_QW, moba_q_norm_w), (R_KW, moba_k_norm_w)):
                sp.dma_start(rows[row:row + src.shape[0], :], src).then_inc(s["rows_loaded"], 16)
            sp.dma_start(w16[:], w_in3[:, :, COL_BETA:COL_BETA + 2 * H]).then_inc(s["w16_loaded"], 16)
            sp.dma_start(alog[:], gdn_a_log.broadcast_to([P, H])).then_inc(s["ab_loaded"], 16)
            sp.dma_start(dtb[:], gdn_dt_bias.broadcast_to([P, H])).then_inc(s["ab_loaded"], 16)


            loaded = (s["raw_loaded0"], s["raw_loaded1"])

            def slot_free(n):
                sp.wait_ge(s["lo_ready"], n - 1)

            def load(n, slot, src):
                sp.dma_start(raw[slot][:].rearrange("p (k c) -> p k c", k=src.shape[1]), src)\
                    .then_inc(loaded[slot], 16)

            def head_loads(i):
                for w, (_, col) in enumerate(STRIPES):
                    if w == 0:
                        sp.wait_ge(s["lo_ready"], i * NW)
                    elif w > 1:
                        slot_free(i * NW + w)
                    load(i * NW + w, w % 2, w_in3[:, :, bass.ds(i * P + col, P)])

            for w in range(2):
                load(w, w, w_in3[:, :, STRIPES[w][1]:STRIPES[w][1] + P])
            sp.wait_ge(s["x_T"], 4)
            sp.dma_start(xt[:, 0, :], xs[2 * P:3 * P, :]).then_inc(s["x_loaded0"], 16)
            sp.wait_ge(s["x_T"], 8)
            sp.dma_start(xt[:, 1, :], xs[3 * P:4 * P, :]).then_inc(s["x_loaded1"], 16)
            for w in range(2, NW):
                slot_free(w)
                load(w, w % 2, w_in3[:, :, STRIPES[w][1]:STRIPES[w][1] + P])
            with sp.Fori(1, H) as i:
                head_loads(i)

            def gate_load(n, slot, j, which):
                slot_free(n)
                load(n, slot, w_in3[:, :, bass.ds(j * P + (COL_GATE + which * D), P)])

            def y_load(n, slot, j):
                slot_free(n)
                half = raw[slot][:].rearrange("p (b k c) -> p b k c", b=2, k=H)
                sp.dma_start(half[:, 0], wg3[:, :, bass.ds(j * P, P)]).then_inc(loaded[slot], 16)
                sp.dma_start(half[:, 1], wm3[:, :, bass.ds(j * P, P)]).then_inc((s["y_loaded0"], s["y_loaded1"])[slot], 16)

            for c in range(4):
                gate_load(N1 + c, c % 2, c // 2, c % 2)
            with sp.Fori(0, (KT - 2) // 2) as jj:
                j = jj * 2
                for u in range(2):
                    n = j * 3 + (N2 + 3 * u)
                    y_load(n, u % 2, j + u)
                    gate_load(n + 1, (u + 1) % 2, j + (u + 2), 0)
                    gate_load(n + 2, u % 2, j + (u + 2), 1)
            for u in range(2):
                y_load(N2 + 3 * (KT - 2) + u, u, KT - 2 + u)

            def wo_load(n, slot, eb, kc):
                slot_free(n)
                load(n, slot, wo3[:, 4 * kc:4 * kc + 4, bass.ds(eb * 512, 512)])

            with sp.Fori(0, D // 512) as eb:
                for kc in range(4):
                    wo_load(eb * 4 + (N3 + kc), kc % 2, eb, kc)
                    if kc == 1:
                        sp.wait_ge(s["win_done"], N3)
                        sp.wait_ge(s["resid"], eb * NT + 1)
                        sp.dma_start(x3[:], xs.rearrange("(t p) d -> p t d", p=P)[:, :, bass.ds(eb * 512, 512)])\
                            .then_inc(s["x3_loaded"], 16)

        @block.gpsimd
        def _(pool):
            pool.memset(rows[:], 0.0).then_inc(s["rows_set"], 1)
            for tile, value in ((ones, 1.0), (mean, 1.0 / P), (eps, EPS), (lnscale, LNSCALE)):
                pool.memset(tile[:], value).then_inc(s["ones_set"], 1)
            pool.wait_ge(s["x_lo"], NT * 4)
            pool.wait_ge(s["hc_set"], 7)
            for k in ("gk", "gq", "gv"):
                pool.memset(rawc[k][:, 0:4], 0.0).then_inc(s["pads"], 1)

            def head(h, p):
                pool.wait_ge(s["cg_dt"], h + 1)
                pool.wait_ge(s["vn_mm"], 4 * h)
                pool.tensor_tensor(q4(dTs), q4(dT), over(cst[:, C_STRICT, :]), ALU.mult).then_inc(s["cg_dts"], 1)
                if p is not None:
                    pool.wait_ge(s["ob"], h)
                    pool.dma_start(o_dram[bass.ds(p + H, 1)].rearrange("o p t -> p (o t)"), pr1[:])\
                        .then_inc(s["ob_out"], 16)
                pool.wait_ge(s["Ln"], h + 1)
                pool.wait_ge(s["ma_mm"], 3 * h)
                pool.tensor_tensor(q4(lm[1]), q4(Ln), over(cst[:, C_L32, :]), ALU.mult).then_inc(s["L32m"], 1)
                pool.tensor_tensor(q4(lm[2]), q4(Ln), over(cst[:, C_L64, :]), ALU.mult).then_inc(s["L64m"], 1)
                pool.wait_ge(s["Ld"], h + 1)
                pool.wait_ge(s["LT_mm"], h + 1)
                pool.tensor_tensor(q4(Ln), q4(Ln), over(cst[:, C_L128, :]), ALU.mult).then_inc(s["L128m"], 1)
                for c, r in ((0, kr), (1, qr)):
                    pool.wait_ge(s["b_n"], 2 * h + c + 1)
                    pool.wait_ge(s["s_mm"], 4 * h)
                    pool.tensor_tensor(r[:], pt[:, c, :], cos, ALU.mult).then_inc(s["b_cos"], 1)
                pool.wait_ge(s["o_2"], h + 1)
                pool.dma_start(o_dram[bass.ds(h, 1)].rearrange("o p t -> p (o t)"), o1[:]).then_inc(s["o_out"], 16)

            head(0, None)
            with pool.Fori(1, H) as i:
                head(i, i - 1)
            pool.wait_ge(s["ob"], H)
            pool.dma_start(o_dram[2 * H - 1], pr1[:]).then_inc(s["ob_out"], 16)

            pool.wait_ge(s["o_out"], 16 * H)
            pool.wait_ge(s["ob_out"], 16 * H)
            act_loaded = (s["act_loaded0"], s["act_loaded1"])
            def act_load(c, dram, first):
                if c >= 2:
                    pool.wait_ge(s["act_lo"], c - 1)
                pool.dma_start(act_raw[:, c % 2, :].rearrange("p (k t) -> p k t", t=T),
                               dram[4 * first:4 * first + 4].rearrange("k p t -> p k t"))\
                    .then_inc(act_loaded[c % 2], 16)
            for c in range(OCH):
                act_load(c, o_dram, c)

            def store_merged(j, u, wait):
                pool.wait_ge(s["mg"], wait)
                pool.dma_start(m_dram[bass.ds(j, 1)].rearrange("o p t -> p (o t)"), mgt[:, u, :])\
                    .then_inc(s["mg_out"], 16)

            with pool.Fori(0, (KT - 2) // 2) as jj:
                j = jj * 2
                for u in range(2):
                    store_merged(j + u, u, j + (u + 1))
            pool.wait_ge(s["mg_out"], 16 * (KT - 2))
            for c in range(MCH - 1):
                act_load(OCH + c, m_dram, c)
            for u in range(2):
                store_merged(KT - 2 + u, u, KT - 1 + u)
            pool.wait_ge(s["mg_out"], 16 * KT)
            act_load(OCH + MCH - 1, m_dram, MCH - 1)

            with pool.Fori(0, D // 512) as eb:
                for t in range(NT):
                    pool.wait_ge(s["resid"], eb * NT + (t + 2))
                    pool.dma_start(outs[t * P:(t + 1) * P, bass.ds(eb * 512, 512)], y3[:, t, :])\
                        .then_inc(s["out_stored"], 16)
            pool.wait_ge(s["out_stored"], 16 * NT * (D // 512))

        @block.tensor
        def _(pe):
            def products(slot, k0, k1):
                for k in range(k0, k1):
                    c = slice(k * P, (k + 1) * P)
                    pe.matmul(PJ[slot][:], w_hi[slot][:, c], h_hi[:, k, :], start=(k == 0), stop=False,
                              skip_group_check=True)
                    pe.matmul(PJ[slot][:], w_hi[slot][:, c], h_lo[:, k, :], start=False, stop=False,
                              skip_group_check=True)
                    mm = pe.matmul(PJ[slot][:], w_lo[slot][:, c], h_hi[:, k, :], start=False, stop=(k == KT - 1),
                                   skip_group_check=True)
                if k1 == KT:
                    mm.then_inc(s["win_done"], 1)

            def window(n, slot, k0, k1):
                if k0 == 0:
                    pe.wait_ge(s["lo_ready"], n + 1)
                    if not (isinstance(n, int) and n < 2):
                        pe.wait_ge(s["win_evac"], n - 1)
                products(slot, k0, k1)

            def four(ps, lhsT, rhs):
                for t in range(NT):
                    mm = pe.matmul(ps[:, tile4(t)], lhsT[:, tile4(t)], rhs[:, tile4(t)], start=True, stop=True)
                return mm

            def turn(ps, src):
                for t in range(NT):
                    mm = pe.transpose(ps[:, tile4(t)], src[:, tile4(t)], ident)
                return mm

            def cgrow(h):
                pe.wait_ge(s["hcol"], h + 1)
                pe.wait_ge(s["st"], 3 * h)
                for t in range(NT):
                    mm = pe.matmul(G2[:, tile4(t)], hcol[:, HC_G, t:t + 1].broadcast_to([P, P]), triu,
                                   start=True, stop=True)
                mm.then_inc(s["cgrow_mm"], 1)

            def ss(h, c):
                pe.wait_ge(s["sqd"], 2 * h + c + 1)
                pe.wait_ge((s["o_1"], s["o_ln"])[c], h)
                pe.matmul((G0, G1)[c][:], ones[:], rawc[("gk", "gq")[c]][:, 4:], start=True, stop=True)\
                    .then_inc(s["ss_mm"], 1)

            def kT(h):
                pe.wait_ge(s["norm"], 2 * h + 1)
                turn(G0, cv["gk"]).then_inc(s["kT_mm"], 1)

            def kk(h):
                pe.wait_ge(s["cg_eg"], h + 1)
                four(G2, cv["gk"], cv["gk"]).then_inc(s["kk_mm"], 1)

            def qk(h):
                pe.wait_ge(s["norm"], 2 * h + 2)
                four(G1, cv["gk"], cv["gq"]).then_inc(s["qk_mm"], 1)

            def UT(h):
                pe.wait_ge(s["kkd"], h + 1)
                pe.wait_ge(s["kdec"], h + 1)
                turn(G0, Up).then_inc(s["UT_mm"], 1)

            def LT(h):
                pe.wait_ge(s["Ln"], h + 1)
                turn(G2, Ln).then_inc(s["LT_mm"], 1)

            def n1(h):
                pe.wait_ge(s["Ud"], h + 1)
                pe.wait_ge(s["Ld"], h + 1)
                pe.wait_ge(s["qkd"], h + 1)
                four(G0, Ud, Ld)
                four(G1, Ld, Ud).then_inc(s["n1_mm"], 1)

            def n2(h):
                pe.wait_ge(s["L2"], h + 1)
                pe.wait_ge(s["U2"], h + 1)
                pe.wait_ge(s["X1"], h + 1)
                four(G0, U2, L2)
                four(G1, L2, U2)
                four(G2, L2, xa).then_inc(s["n2_mm"], 1)

            def n3(h):
                pe.wait_ge(s["X2"], h + 1)
                pe.wait_ge(s["L4"], h + 1)
                pe.wait_ge(s["U4"], h + 1)
                four(G0, U4, L4)
                four(G2, L4, xb).then_inc(s["n3_mm"], 1)

            def n4(h):
                pe.wait_ge(s["X4"], h + 1)
                pe.wait_ge(s["L8"], h + 1)
                four(G2, L8, xa).then_inc(s["n4_mm"], 1)

            def vTs(h):
                pe.wait_ge(s["silu"], 3 * h + 3)
                pe.wait_ge(s["U4"], h + 1)
                turn(G1, cv["gv"]).then_inc(s["vT_mm"], 1)

            def ma(h, k):
                src = (xb, xa, xb)[k]
                if k == 0:
                    pe.wait_ge(s["X8"], h + 1)
                    pe.wait_ge(s["L8"], h + 1)
                    pe.wait_ge(s["vb"], h + 1)
                else:
                    pe.wait_ge(s["X"], 3 * h + k)
                pe.wait_ge((s["L32m"], s["L64m"], s["L128m"])[k], h + 1)
                four(G0, (lm[1], lm[2], lm[0])[k], src)
                turn(G1, src).then_inc(s["ma_mm"], 1)

            def mb(h, k):
                pe.wait_ge(s["Y"], 3 * h + k + 1)
                pe.wait_ge(s["XT"], 3 * h + k + 1)
                four(G2, XTt, Yt).then_inc(s["mb_mm"], 1)

            def wT(h):
                pe.wait_ge(s["kbe"], h + 1)
                pe.wait_ge(s["X"], 3 * h + 3)
                four(G0, kbe, xa).then_inc(s["wT_mm"], 1)

            def vnew(h, t):
                if t == 0:
                    pe.wait_ge(s["vb"], h + 1)
                else:
                    pe.wait_ge(s["vn"], 4 * h + t)
                mm = pe.matmul(G1[:, :P], xa[:, tile4(t)], vb[:, tile4(t)], start=True, stop=(t == 0))
                if t > 0:
                    pe.wait_ge(s["nwT"], h + 1)
                    pe.wait_ge(s["st"], 3 * h + t)
                    mm = pe.matmul(G1[:, :P], nwT[:, tile4(t)], st[(t - 1) % 2][:], start=False, stop=True)
                mm.then_inc(s["vn_mm"], 1)

            def outs_(h, t):
                pe.wait_ge(s["vn"], 4 * h + t + 1)
                if t < NT - 1:
                    pe.wait_ge(s["kdec"], h + 1)
                    pe.matmul(G2[:, :P], kdec[:, tile4(t)], vn[:, tile4(t)], start=True, stop=True)\
                        .then_inc(s["st_mm"], 1)
                if t == 0:
                    pe.wait_ge(s["nwT"], h + 1)
                    pe.wait_ge(s["qkd"], h + 1)
                    pe.wait_ge(s["qdec"], h + 1)
                else:
                    pe.matmul(G0[:, tile4(t)], st[(t - 1) % 2][:], qdec[:, tile4(t)], start=True, stop=False)
                pe.matmul(G0[:, tile4(t)], vn[:, tile4(t)], qkT[:, tile4(t)], start=(t == 0), stop=True)\
                    .then_inc(s["o_mm"], 1)

            def gnorm(h):
                pe.wait_ge(s["o_sq"], h + 1)
                pe.matmul(G1[:], mean[:], kbe[:], start=True, stop=True).then_inc(s["o_ss"], 1)

            def b_ss(h, c):
                pe.wait_ge(s["b_sq"], 2 * h + c + 1)
                if c == 0:
                    pe.wait_ge(s["pT"], 4 * h)
                pe.matmul(A2[:], mean[:], pt[:, 2, :], start=True, stop=True).then_inc(s["b_ss"], 1)

            def bvTs(h):
                pe.wait_ge(s["win_evac"], NW * h + 7)
                pe.wait_ge(s["b_ln"], 2 * h + 2)
                turn(A2, bv).then_inc(s["bvT_mm"], 1)

            def scores(h, t):
                pe.wait_ge(s["b_rope"], 2 * h + 2)
                if t >= 2:
                    pe.wait_ge(s["s_exp"], 4 * h + t - 1)
                n = (t + 1) * P
                pe.matmul((A0, A1)[t % 2][:, :n], qr[:, tile4(t)], kr[:, :n], start=True, stop=True)\
                    .then_inc(s["s_mm"], 1)

            def pTs(h, t):
                pe.wait_ge(s["s_norm"], 4 * h + t + 1)
                if t == 0:
                    pe.wait_ge(s["bvT"], h + 1)
                else:
                    pe.wait_ge(s["pT"], 4 * h + t)
                for k in range(t + 1):
                    mm = pe.transpose(A2[:, tile4(k)], probs[t % 2][:, tile4(k)], ident)
                mm.then_inc(s["pT_mm"], 1)

            def pv(h):
                pe.wait_ge(s["pT"], 4 * h + 4)
                for k in range(NT):
                    mm = pe.matmul(A0[:, k * P:], vT[:, tile4(k)], pt[:, k, k * P:],
                                   start=(k == 0), stop=(k == NT - 1))
                mm.then_inc(s["pv_mm"], 1)

            def head(h, p):
                def win(w, a, b):
                    window(h * NW + w, w % 2, a, b)
                win(0, 0, 4)
                cgrow(h)
                if p is not None:
                    scores(p, 0)
                    win(0, 4, 8)
                    scores(p, 1)
                    win(0, 8, 11)
                    pTs(p, 0)
                    scores(p, 2)
                    win(0, 11, 16)
                    pTs(p, 1)
                    scores(p, 3)
                    win(1, 0, 4)
                    pTs(p, 2)
                    win(1, 4, 8)
                    pTs(p, 3)
                    win(1, 8, 11)
                    pv(p)
                else:
                    win(0, 4, 16)
                    win(1, 0, 11)
                win(1, 11, 16)
                ss(h, 0)
                win(2, 0, 6)
                kT(h)
                kk(h)
                win(2, 6, 16)
                ss(h, 1)
                win(3, 0, 4)
                UT(h)
                win(3, 4, 7)
                LT(h)
                qk(h)
                win(3, 7, 11)
                n1(h)
                win(3, 11, 14)
                n2(h)
                win(3, 14, 16)
                win(4, 0, 3)
                n3(h)
                win(4, 3, 6)
                n4(h)
                win(4, 6, 8)
                vTs(h)
                win(4, 8, 11)
                ma(h, 0)
                win(4, 11, 14)
                mb(h, 0)
                win(4, 14, 16)
                win(5, 0, 3)
                ma(h, 1)
                win(5, 3, 6)
                mb(h, 1)
                win(5, 6, 8)
                b_ss(h, 0)
                win(5, 8, 10)
                ma(h, 2)
                win(5, 10, 13)
                mb(h, 2)
                win(5, 13, 16)
                wT(h)
                vnew(h, 0)
                win(6, 0, 4)
                outs_(h, 0)
                win(6, 4, 6)
                vnew(h, 1)
                win(6, 6, 8)
                outs_(h, 1)
                win(6, 8, 10)
                vnew(h, 2)
                b_ss(h, 1)
                win(6, 10, 12)
                outs_(h, 2)
                win(6, 12, 14)
                vnew(h, 3)
                win(6, 14, 16)
                outs_(h, 3)
                win(7, 0, 4)
                gnorm(h)
                bvTs(h)
                win(7, 4, 16)

            pe.wait_ge(s["consts"], 32)
            pe.wait_ge(s["rows_loaded"], 80)
            pe.transpose(A0[:, :P], rows[:], ident).then_inc(s["rows_T"], 1)
            for t in range(NT):
                pe.wait_ge(s["x_scaled"], t + 1)
                for q in range(4):
                    g = 4 * t + q
                    if g >= 2:
                        pe.wait_ge(s["x_evac"], g - 1)
                    for k in range(4):
                        mm = pe.transpose(PJ[g % 2][:, tile4(k)], xt[:, t % 2, (4 * q + k) * P:(4 * q + k + 1) * P], ident)
                    mm.then_inc(s["x_T"], 1)
            pe.wait_ge(s["x_lo"], NT * 4)
            pe.wait_ge(s["w16_lo"], 1)
            for t in range(NT):
                ps = A1[:, t * 2 * H:(t + 1) * 2 * H]
                for k in range(KT):
                    pe.matmul(ps, h_hi[:, k, tile4(t)], w16h[:, k, :], start=(k == 0), stop=False)
                    pe.matmul(ps, h_hi[:, k, tile4(t)], w16l[:, k, :], start=False, stop=False)
                    mm = pe.matmul(ps, h_lo[:, k, tile4(t)], w16h[:, k, :], start=False, stop=(k == KT - 1))
            mm.then_inc(s["ba_mm"], 1)
            pe.wait_ge(s["ba_step"], BA_G)
            pe.matmul(A2[:, :NT * H], triu, ba[:, 5, :, :].rearrange("p t h -> p (t h)"), start=True, stop=True)
            pe.matmul(A2[:, NT * H:2 * NT * H], ones[:], ba[:, 5, :, :].rearrange("p t h -> p (t h)"),
                      start=True, stop=True).then_inc(s["cg_mm"], 1)

            head(0, None)
            with pe.Fori(1, H) as i:
                head(i, i - 1)

            def gate(n, slot, a, b):
                if a == 0:
                    pe.wait_ge(s["lo_ready"], n + 1)
                products(slot, a, b)

            last = H - 1
            pe.wait_ge(s["win_evac"], N1 - 1)
            gate(N1, 0, 0, 4)
            scores(last, 0)
            gate(N1, 0, 4, 8)
            scores(last, 1)
            gate(N1, 0, 8, 11)
            pTs(last, 0)
            scores(last, 2)
            gate(N1, 0, 11, 16)
            pTs(last, 1)
            scores(last, 3)
            pe.wait_ge(s["win_evac"], N1)
            gate(N1 + 1, 1, 0, 4)
            pTs(last, 2)
            gate(N1 + 1, 1, 4, 8)
            pTs(last, 3)
            gate(N1 + 1, 1, 8, 11)
            pv(last)
            gate(N1 + 1, 1, 11, 16)
            for c in range(2):
                pe.wait_ge(s["g_evac"], c + 1)
                gate(N1 + 2 + c, c, 0, 16)

            ybank = ((G0, G1), (A0, A1))

            def y(n, slot, u):
                pe.wait_ge(s["lo_ready"], n + 1)
                for b in range(2):
                    ps = ybank[u][b]
                    for k in range(H):
                        c = slice((b * H + k) * P, (b * H + k + 1) * P)
                        o = b * H + k
                        pe.matmul(ps[:], w_hi[slot][:, c], o_hi[:, o, :], start=(k == 0), stop=False)
                        pe.matmul(ps[:], w_hi[slot][:, c], o_lo[:, o, :], start=False, stop=False)
                        mm = pe.matmul(ps[:], w_lo[slot][:, c], o_hi[:, o, :], start=False, stop=(k == H - 1))
                mm.then_inc(s["win_done"], 1)

            pe.wait_ge(s["act_lo"], OCH)
            with pe.Fori(0, (KT - 2) // 2) as jj:
                j = jj * 2
                for u in range(2):
                    n = j * 3 + (N2 + 3 * u)
                    y(n, u, u)
                    pe.wait_ge(s["g_evac"], 2 * j + (2 * u + 4))
                    gate(n + 1, (u + 1) % 2, 0, 16)
                    gate(n + 2, u, 0, 16)
            for u in range(2):
                pe.wait_ge(s["yb"], KT - 2)
                y(N2 + 3 * (KT - 2) + u, u, u)

            def p3(n, slot, kc, banks):
                pe.wait_ge(s["lo_ready"], n + 1)
                for t in range(NT):
                    for k in range(4):
                        kt = 4 * kc + k
                        c = slice(k * 512, (k + 1) * 512)
                        pe.matmul(banks[t][:], h_hi[:, kt, tile4(t)], w_hi[slot][:, c],
                                  start=(kt == 0), stop=False)
                        pe.matmul(banks[t][:], h_hi[:, kt, tile4(t)], w_lo[slot][:, c], start=False, stop=False)
                        mm = pe.matmul(banks[t][:], h_lo[:, kt, tile4(t)], w_hi[slot][:, c],
                                       start=False, stop=(kt == KT - 1))
                    if kc == 3 and t < NT - 1:
                        mm.then_inc(s["p3_done"], 1)
                mm.then_inc(s["win_done"], 1)

            pe.wait_ge(s["yb"], KT)
            with pe.Fori(0, D // 512, 2) as eb:
                for e in range(2):
                    pe.wait_ge(s["resid"], eb * NT + 1)
                    for kc in range(4):
                        pe.wait_ge(s["act_lo"], OCH + kc + 1)
                        p3(eb * 4 + (N3 + 4 * e + kc), kc % 2, kc, (bank[0:4], bank[4:8])[e])

        @block.scalar
        def _(act):
            loaded = (s["raw_loaded0"], s["raw_loaded1"])
            act.preload_act_table_set("natural_log_exp_and_others")

            def split(n, slot, at, halves=None):
                if not (isinstance(n, int) and n < 2):
                    act.wait_ge(s["win_done"], n - 1)
                act.wait_ge(loaded[slot], 16 * at)
                if halves is not None:
                    act.wait_ge((s["y_loaded0"], s["y_loaded1"])[slot], 16 * halves)
                act.activation(w_hi[slot][:], raw[slot][:], ACT.Copy).then_inc(s["hi_ready"], 1)

            def sigmoid(ap, sem, n):
                act.activation(ap, ap, ACT.Exp, scale=-1.0).then_inc(sem, 1)
                act.wait_ge(sem, n + 1)
                act.activation(ap, ap, ACT.Ln, bias=1.0).then_inc(sem, 1)
                act.wait_ge(sem, n + 2)
                act.activation(ap, ap, ACT.Exp, scale=-1.0).then_inc(sem, 1)

            def evac(h, w):
                name = STRIPES[w][0]
                act.wait_ge(s["win_done"], h * NW + w + 1)
                if not (isinstance(h, int) and h == 0):
                    if name in ("gk", "gq"):
                        act.wait_ge(s["norm"], 2 * h + w - 1)
                    elif name == "gv":
                        act.wait_ge(s["silu"], 3 * h)
                    elif name == "gz":
                        act.wait_ge(s["o_2"], h)
                    elif name == "bk":
                        act.wait_ge(s["pv_mm"], h)
                    elif name == "bv":
                        act.wait_ge(s["pT_mm"], 4 * h)
                act.activation(dest[name], PJ[w % 2][:], ACT.Copy).then_inc(s["win_evac"], 1)

            def cgrow(h):
                act.wait_ge(s["cg_arg"], 4 * h + 4)
                act.wait_ge(s["mb_mm"], 3 * h)
                act.activation(Eg[:], G2[:], ACT.Exp).then_inc(s["cg_eg"], 1)
                act.activation(dT[:], dT[:], ACT.Exp).then_inc(s["cg_dt"], 1)

            def silu(h, c):
                act.wait_ge(s["clampd"], 3 * h + c + 1)
                sigmoid(rawc[("gk", "gq", "gv")[c]][:, 4:], s["sig"], 9 * h + 3 * c)

            def sq(h, c):
                k = ("gk", "gq")[c]
                act.wait_ge(s["silu"], 3 * h + c + 1)
                act.activation(rawc[k][:, 4:], cv[k][:], ACT.Square).then_inc(s["sqd"], 1)

            def rnorm(h, c):
                r = rawc[("gk", "gq")[c]][:, 4:]
                act.wait_ge(s["ss_mm"], 2 * h + c + 1)
                act.activation(r, (G0, G1)[c][:], ACT.Ln, bias=eps[:, 0:1]).then_inc(s["rn_ln"], 1)
                act.wait_ge(s["rn_ln"], 2 * h + c + 1)
                if c == 0:
                    act.activation(r, r, ACT.Exp, scale=-0.5).then_inc(s["rn"], 1)
                else:
                    act.activation(r, r, ACT.Exp, scale=-0.5, bias=lnscale[:, 0:1]).then_inc(s["rn"], 1)

            def n1(h):
                act.wait_ge(s["n1_mm"], h + 1)
                act.wait_ge(s["qdec"], h + 1)
                act.activation(L2[:], G0[:], ACT.Copy).then_inc(s["L2"], 1)

            def n2(h):
                act.wait_ge(s["n2_mm"], h + 1)
                act.activation(L4[:], G0[:], ACT.Copy).then_inc(s["L4"], 1)
                act.activation(U4[:], G1[:], ACT.Copy).then_inc(s["U4"], 1)

            def n3(h):
                act.wait_ge(s["n3_mm"], h + 1)
                act.activation(L8[:], G0[:], ACT.Copy).then_inc(s["L8"], 1)

            def ma(h, k):
                act.wait_ge(s["ma_mm"], 3 * h + k + 1)
                act.activation(Yt[:], G0[:], ACT.Copy).then_inc(s["Y"], 1)

            def wT(h):
                act.wait_ge(s["wT_mm"], h + 1)
                act.activation(nwT[:], G0[:], ACT.Copy, scale=-1.0).then_inc(s["nwT"], 1)

            def vnew(h, t):
                act.wait_ge(s["vn_mm"], 4 * h + t + 1)
                act.activation(vn[:, tile4(t)], G1[:, :P], ACT.Copy).then_inc(s["vn"], 1)

            def gnorm(h):
                act.wait_ge(s["o_mm"], 4 * h + 4)
                act.activation(kbe[:], G0[:], ACT.Square).then_inc(s["o_sq"], 1)
                act.wait_ge(s["o_ss"], h + 1)
                act.activation(kbe[:], G1[:], ACT.Ln, bias=eps[:, 0:1]).then_inc(s["o_ln"], 1)
                act.wait_ge(s["o_ln"], h + 1)
                act.activation(kbe[:], kbe[:], ACT.Exp, scale=-0.5).then_inc(s["o_rn"], 1)

            def zsig(h, b):
                act.wait_ge(s["zclamp"], 2 * h + b + 1)
                sigmoid(zt[:], s["zsig"], 6 * h + 3 * b)

            def b_norm(h, c):
                act.wait_ge(s["win_evac"], NW * h + 5 + c)
                if c == 0:
                    act.wait_ge(s["pv_mm"], h)
                else:
                    act.wait_ge(s["b_n"], 2 * h + 1)
                act.activation(pt[:, 2, :], pt[:, c, :], ACT.Square).then_inc(s["b_sq"], 1)
                act.wait_ge(s["b_ss"], 2 * h + c + 1)
                act.activation(pt[:, 2, :], A2[:], ACT.Ln, bias=eps[:, 0:1]).then_inc(s["b_ln"], 1)
                act.wait_ge(s["b_ln"], 2 * h + c + 1)
                act.activation(pt[:, 2, :], pt[:, 2, :], ACT.Exp, scale=-0.5).then_inc(s["b_rn"], 1)

            def softmax(h, t):
                act.wait_ge(s["s_nmax"], 4 * h + t + 1)
                if t >= 2:
                    act.wait_ge(s["pT_mm"], 4 * h + t - 1)
                elif t == 0:
                    act.wait_ge(s["bvT_mm"], h + 1)
                n = (t + 1) * P
                act.activation(probs[t % 2][:, :n], (A0, A1)[t % 2][:, :n], ACT.Exp, scale=SCALE,
                               bias=stat[:, 1, t:t + 1], accum_out=stat[:, 2, t:t + 1]).then_inc(s["s_exp"], 1)

            def pTc(h, t):
                act.wait_ge(s["pT_mm"], 4 * h + t + 1)
                act.activation(pt[:, 0:t + 1, tile4(t)],
                               A2[:, :(t + 1) * P].rearrange("p (k c) -> p k c", c=P), ACT.Copy).then_inc(s["pT"], 1)

            def at(i, w):
                return i * (NW // 2) + (w // 2 + 1)

            def split_next(i, w):
                if w + 1 < NW:
                    split(i * NW + (w + 1), (w + 1) % 2, at(i, w + 1))
                else:
                    split(i * NW + NW, 0, i * (NW // 2) + (NW // 2 + 1))

            def head(h, p):
                if p is not None:
                    evac(p, NW - 1)
                split_next(h, 0)
                cgrow(h)
                if p is not None:
                    softmax(p, 0)
                    zsig(p, 1)
                    softmax(p, 1)
                    pTc(p, 0)
                    softmax(p, 2)
                    pTc(p, 1)
                    softmax(p, 3)
                evac(h, 0)
                split_next(h, 1)
                if p is not None:
                    pTc(p, 2)
                    pTc(p, 3)
                silu(h, 0)
                sq(h, 0)
                evac(h, 1)
                split_next(h, 2)
                rnorm(h, 0)
                silu(h, 1)
                sq(h, 1)
                evac(h, 2)
                split_next(h, 3)
                rnorm(h, 1)
                n1(h)
                n2(h)
                silu(h, 2)
                evac(h, 3)
                split_next(h, 4)
                n3(h)
                zsig(h, 0)
                ma(h, 0)
                evac(h, 4)
                split_next(h, 5)
                ma(h, 1)
                b_norm(h, 0)
                ma(h, 2)
                wT(h)
                evac(h, 5)
                split_next(h, 6)
                vnew(h, 0)
                vnew(h, 1)
                b_norm(h, 1)
                vnew(h, 2)
                vnew(h, 3)
                evac(h, 6)
                split_next(h, 7)
                if p is not None:
                    act.wait_ge(s["ob_out"], 16 * h)
                gnorm(h)

            act.wait_ge(s["ones_set"], 4)
            for t in range(NT):
                act.wait_ge((s["x_loaded0"], s["x_loaded1"])[t % 2], 16 * (t // 2 + 1))
                if t > 0:
                    act.wait_ge(s["x_sq"], t)
                act.activation(xsq[:], xt[:, t % 2, :], ACT.Square, accum_out=ssx[:, t:t + 1]).then_inc(s["x_sq"], 1)
                act.wait_ge(s["x_sq"], t + 1)
                act.activation(rsx[:, t:t + 1], ssx[:, t:t + 1], ACT.Ln, scale=1.0 / D, bias=eps[:, 0:1])\
                    .then_inc(s["x_ln"], 1)
                act.wait_ge(s["x_ln"], t + 1)
                act.activation(rsx[:, t:t + 1], rsx[:, t:t + 1], ACT.Exp, scale=-0.5).then_inc(s["x_rstd"], 1)
                for q in range(4):
                    g = 4 * t + q
                    act.wait_ge(s["x_evac"], g + 1)
                    act.activation(h_hi[:, 4 * q:4 * q + 4, tile4(t)],
                                   htmp[:, g % 2, :].rearrange("p (k c) -> p k c", c=P), ACT.Copy)\
                        .then_inc(s["x_hi"], 1)
                if t == 1:
                    act.wait_ge(s["w16_loaded"], 16)
                    act.activation(w16h[:], w16[:], ACT.Copy).then_inc(s["w16_hi"], 1)
                    split(0, 0, 1)
            act.wait_ge(s["ab_loaded"], 32)
            act.wait_ge(s["ba_step"], 2)
            sigmoid(ba[:, 0], s["ba_step"], 2)
            act.wait_ge(s["ba_step"], 5)
            act.activation(ba[:, 2], ba[:, 1], ACT.Abs).then_inc(s["ba_step"], 1)
            act.wait_ge(s["ba_step"], 6)
            act.activation(ba[:, 2], ba[:, 2], ACT.Exp, scale=-1.0).then_inc(s["ba_step"], 1)
            act.wait_ge(s["ba_step"], 7)
            act.activation(ba[:, 2], ba[:, 2], ACT.Ln, bias=1.0).then_inc(s["ba_step"], 1)
            act.activation(alog[:], alog[:], ACT.Exp).then_inc(s["ba_step"], 1)
            act.wait_ge(s["ba_step"], BA_G + 3)
            act.activation(ba[:, 3], ba[:, 3], ACT.Exp).then_inc(s["ba_step"], 1)
            act.activation(ba[:, 4], ba[:, 1], ACT.Exp).then_inc(s["ba_step"], 1)
            act.activation(ba[:, 2], ba[:, 2], ACT.Exp).then_inc(s["ba_step"], 1)
            act.wait_ge(s["hc_set"], 7)

            head(0, None)
            with act.Fori(1, H) as i:
                head(i, i - 1)

            last = H - 1
            evac(last, NW - 1)
            split(N1 + 1, 1, (N1 + 1) // 2 + 1)
            softmax(last, 0)
            zsig(last, 1)
            softmax(last, 1)
            pTc(last, 0)
            softmax(last, 2)
            pTc(last, 1)
            softmax(last, 3)
            split(N1 + 2, 0, (N1 + 2) // 2 + 1)
            pTc(last, 2)
            pTc(last, 3)

            def gate_sigmoid(u, which, count):
                act.wait_ge(s["g_evac"], count + 1)
                sigmoid(sg[:, u, which, :], s["g_sig"], 3 * count)

            def act_split(c, dst, first):
                act.wait_ge((s["act_loaded0"], s["act_loaded1"])[c % 2], 16 * (c // 2 + 1))
                act.activation(dst[:, first:first + 4, :].rearrange("p k t -> p (k t)"), act_raw[:, c % 2, :],
                               ACT.Copy).then_inc(s["act_hi"], 1)

            gate_sigmoid(0, 0, 0)
            split(N1 + 3, 1, (N1 + 3) // 2 + 1)
            gate_sigmoid(0, 1, 1)
            split(N2, 0, N2 // 2 + 1, 1)
            gate_sigmoid(1, 0, 2)
            for c in range(OCH):
                act_split(c, o_hi, 4 * c)

            with act.Fori(0, (KT - 2) // 2) as jj:
                for u in range(2):
                    def nth(k):
                        c = 3 * u + k
                        return jj * 6 + (N2 + c), c % 2, jj * 3 + ((N2 + c) // 2 + 1)
                    split(*nth(1))
                    gate_sigmoid((u + 1) % 2, 1, 4 * jj + (2 * u + 3))
                    split(*nth(2))
                    split(*nth(3), jj + (u + 1))
                    gate_sigmoid(u, 0, 4 * jj + (2 * u + 4))
            n = N3 - 2
            split(n + 1, 1, (n + 1) // 2 + 1, KT // 2)
            gate_sigmoid(1, 1, 2 * KT - 1)
            act.wait_ge(s["win_done"], N3 - 2)
            for c in range(MCH - 1):
                act_split(OCH + c, h_hi, 4 * c)
            split(N3, 0, N3 // 2 + 1)
            split(N3 + 1, 1, (N3 + 1) // 2 + 1)
            act_split(OCH + MCH - 1, h_hi, 4 * (MCH - 1))
            with act.Fori(0, 3) as eb:
                for k in range(2, 6):
                    split(eb * 4 + (N3 + k), k % 2, eb * 2 + ((N3 + k) // 2 + 1))
            for k in range(14, 16):
                split(N3 + k, k % 2, (N3 + k) // 2 + 1)

        @block.vector
        def _(dve):
            def split(n, slot):
                dve.wait_ge(s["hi_ready"], n + 1)
                dve.tensor_tensor(w_lo[slot][:], raw[slot][:], w_hi[slot][:].bitcast(F32), ALU.subtract)\
                    .then_inc(s["lo_ready"], 1)

            def columns(h):
                dve.tensor_copy(hcol[:].rearrange("p k t -> p (k t)"),
                                hc[:, bass.ds(h, 1), :, :].rearrange("p h k t -> p (h k t)")).then_inc(s["hcol"], 1)

            def cgrow(h):
                dve.wait_ge(s["cgrow_mm"], h + 1)
                dve.wait_ge(s["cg_dts"], h)
                for t in range(NT):
                    dve.scalar_tensor_tensor(dT[:, tile4(t)], G2[:, tile4(t)], hcol[:, HC_CG, t:t + 1],
                                             cst[:, C_DMASK, :], ALU.subtract, ALU.add).then_inc(s["cg_arg"], 1)

            def conv(h, c):
                name, col = (("gk", H), ("gq", 0), ("gv", 2 * H))[c]
                r, y = rawc[name], cv[name]
                dve.wait_ge(s["win_evac"], h * NW + c + 1)
                dve.wait_ge((s["qk_mm"], s["qk_mm"], s["vT_mm"])[c], h)

                def tap(j):
                    return chan[:, bass.ds(h + (R_CONV + 3 * H * j + col), 1)]

                n = 12 * h + 4 * c
                dve.tensor_scalar(y[:], r[:, 4:4 + T], tap(3), None, ALU.mult).then_inc(s["conv"], 1)
                for j in range(3):
                    dve.wait_ge(s["conv"], n + j + 1)
                    dve.scalar_tensor_tensor(y[:], r[:, 1 + j:1 + j + T], tap(j), y[:], ALU.mult, ALU.add)\
                        .then_inc(s["conv"], 1)
                dve.wait_ge(s["conv"], n + 4)
                dve.tensor_scalar(r[:, 4:], y[:], LEAST, None, ALU.max).then_inc(s["clampd"], 1)

            def silu(h, c):
                name = ("gk", "gq", "gv")[c]
                dve.wait_ge(s["sig"], 9 * h + 3 * c + 3)
                dve.tensor_tensor(cv[name][:], cv[name][:], rawc[name][:, 4:], ALU.mult).then_inc(s["silu"], 1)

            def norm(h, c):
                name = ("gk", "gq")[c]
                dve.wait_ge(s["rn"], 2 * h + c + 1)
                dve.tensor_tensor(cv[name][:], cv[name][:], rawc[name][:, 4:], ALU.mult).then_inc(s["norm"], 1)

            def kT(h):
                dve.wait_ge(s["kT_mm"], h + 1)
                dve.wait_ge(s["wT_mm"], h)
                dve.wait_ge(s["o_rn"], h)
                dve.tensor_tensor(q4(kbe), q4(G0), hcb(HC_BE), ALU.mult).then_inc(s["kbe"], 1)
                dve.wait_ge(s["st_mm"], 3 * h)
                dve.tensor_tensor(q4(kdec), q4(G0), hcb(HC_KD), ALU.mult).then_inc(s["kdec"], 1)

            def kk(h):
                dve.wait_ge(s["kk_mm"], h + 1)
                dve.wait_ge(s["cg_dts"], h + 1)
                dve.wait_ge(s["mb_mm"], 3 * h)
                dve.tensor_tensor(Up[:], G2[:], dTs[:], ALU.mult).then_inc(s["kkd"], 1)

            def UT(h):
                dve.wait_ge(s["UT_mm"], h + 1)
                dve.wait_ge(s["ma_mm"], 3 * h)
                dve.tensor_tensor(q4(Ln), q4(G0), hcb(HC_NB), ALU.mult).then_inc(s["Ln"], 1)

            def LT(h):
                dve.wait_ge(s["LT_mm"], h + 1)
                dve.wait_ge(s["o_mm"], 4 * h)
                dve.tensor_tensor(q4(Ud), q4(G2), over(cst[:, C_M16, :]), ALU.mult).then_inc(s["Ud"], 1)
                dve.wait_ge(s["o_out"], 16 * h)
                dve.tensor_tensor(q4(Ld), q4(Ln), over(cst[:, C_M16, :]), ALU.mult).then_inc(s["Ld"], 1)
                dve.wait_ge(s["Ud"], h + 1)
                dve.wait_ge(s["vn_mm"], 4 * h)
                dve.tensor_tensor(q4(xa), q4(Ud), over(ident), ALU.add).then_inc(s["X1"], 1)

            def qk(h):
                dve.wait_ge(s["cg_dt"], h + 1)
                dve.wait_ge(s["qk_mm"], h + 1)
                dve.tensor_tensor(qkT[:], G1[:], dT[:], ALU.mult).then_inc(s["qkd"], 1)
                dve.wait_ge(s["cg_eg"], h + 1)
                dve.wait_ge(s["norm"], 2 * h + 2)
                dve.tensor_tensor(qdec[:], cv["gq"][:], Eg[:], ALU.mult).then_inc(s["qdec"], 1)

            def n1(h):
                dve.wait_ge(s["n1_mm"], h + 1)
                dve.tensor_copy(U2[:], G1[:]).then_inc(s["U2"], 1)

            def n2(h):
                dve.wait_ge(s["n2_mm"], h + 1)
                dve.wait_ge(s["X1"], h + 1)
                dve.tensor_tensor(xb[:], G2[:], xa[:], ALU.add).then_inc(s["X2"], 1)

            def n3(h):
                dve.wait_ge(s["n3_mm"], h + 1)
                dve.wait_ge(s["X2"], h + 1)
                dve.tensor_tensor(xa[:], G2[:], xb[:], ALU.add).then_inc(s["X4"], 1)

            def n4(h):
                dve.wait_ge(s["n4_mm"], h + 1)
                dve.wait_ge(s["X4"], h + 1)
                dve.tensor_tensor(xb[:], G2[:], xa[:], ALU.add).then_inc(s["X8"], 1)

            def vTs(h):
                dve.wait_ge(s["vT_mm"], h + 1)
                dve.tensor_tensor(q4(vb), q4(G1), hcb(HC_B), ALU.mult).then_inc(s["vb"], 1)

            def ma(h, k):
                dve.wait_ge(s["ma_mm"], 3 * h + k + 1)
                dve.tensor_copy(XTt[:], G1[:]).then_inc(s["XT"], 1)

            def mb(h, k):
                a, b = ((xb, xa), (xa, xb), (xb, xa))[k]
                dve.wait_ge(s["mb_mm"], 3 * h + k + 1)
                if k == 0:
                    dve.wait_ge(s["X8"], h + 1)
                else:
                    dve.wait_ge(s["X"], 3 * h + k)
                dve.tensor_tensor(b[:], G2[:], a[:], ALU.add).then_inc(s["X"], 1)

            def state(h, t):
                dve.wait_ge(s["st_mm"], 3 * h + t + 1)
                if t == 0:
                    dve.tensor_copy(st[0][:], G2[:, :P]).then_inc(s["st"], 1)
                else:
                    dve.wait_ge(s["st"], 3 * h + t)
                    dve.scalar_tensor_tensor(st[t % 2][:], st[(t - 1) % 2][:], hcol[:, HC_GL, t:t + 1], G2[:, :P],
                                             ALU.mult, ALU.add).then_inc(s["st"], 1)

            def gnorm(h):
                dve.wait_ge(s["o_rn"], h + 1)
                dve.scalar_tensor_tensor(o1[:], G0[:], chan[:, R_GW:R_GW + 1], kbe[:], ALU.mult, ALU.mult)\
                    .then_inc(s["o_1"], 1)
                dve.wait_ge(s["o_1"], h + 1)
                dve.wait_ge(s["zs"], 2 * h + 1)
                dve.tensor_tensor(o1[:], o1[:], zA[:], ALU.mult).then_inc(s["o_2"], 1)

            def zclamp(h, b):
                dve.wait_ge(s["win_evac"], h * NW + (4, 8)[b])
                dve.tensor_scalar(zt[:], (zA, zB)[b][:], LEAST, None, ALU.max).then_inc(s["zclamp"], 1)

            def zmul(h, b):
                z = (zA, zB)[b]
                dve.wait_ge(s["zsig"], 6 * h + 3 * b + 3)
                dve.tensor_tensor(z[:], z[:], zt[:], ALU.mult).then_inc(s["zs"], 1)

            def b_norm(h, c):
                r, w = ((kr, R_KW), (qr, R_QW))[c]
                x_ = pt[:, c, :]
                lo, hi = slice(0, P // 2), slice(P // 2, P)
                dve.wait_ge(s["b_rn"], 2 * h + c + 1)
                dve.scalar_tensor_tensor(x_, x_, chan[:, w:w + 1], pt[:, 2, :], ALU.mult, ALU.mult)\
                    .then_inc(s["b_n"], 1)
                dve.wait_ge(s["b_n"], 2 * h + c + 1)
                if c == 0:
                    dve.wait_ge(s["pv_mm"], h)
                dve.tensor_tensor(pt[lo, 3, :], pt[hi, c, :], cossin[hi, 1, :], ALU.mult).then_inc(s["b_sinlo"], 1)
                dve.tensor_tensor(pt[hi, 3, :], pt[lo, c, :], cossin[lo, 1, :], ALU.mult).then_inc(s["b_sinhi"], 1)
                dve.wait_ge(s["b_sinlo"], 2 * h + c + 1)
                dve.wait_ge(s["b_sinhi"], 2 * h + c + 1)
                dve.wait_ge(s["b_cos"], 2 * h + c + 1)
                dve.tensor_tensor(r[:], r[:], pt[:, 3, :], ALU.add).then_inc(s["b_rope"], 1)

            def bvTs(h):
                dve.wait_ge(s["bvT_mm"], h + 1)
                dve.wait_ge(s["pv_mm"], h)
                dve.tensor_copy(vT[:], A2[:]).then_inc(s["bvT"], 1)

            def softmax_max(h, t):
                ps = (A0, A1)[t % 2]
                dve.wait_ge(s["s_mm"], 4 * h + t + 1)
                dve.tensor_tensor(ps[:, tile4(t)], ps[:, tile4(t)], cst[:, C_CMASK, :], ALU.add)\
                    .then_inc(s["s_mask"], 1)
                dve.wait_ge(s["s_mask"], 4 * h + t + 1)
                dve.tensor_reduce(stat[:, 0, t:t + 1], ps[:, :(t + 1) * P], AX_X, ALU.max).then_inc(s["s_max"], 1)
                dve.wait_ge(s["s_max"], 4 * h + t + 1)
                dve.tensor_scalar(stat[:, 1, t:t + 1], stat[:, 0, t:t + 1], -SCALE, None, ALU.mult)\
                    .then_inc(s["s_nmax"], 1)

            def softmax_norm(h, t):
                pr = probs[t % 2][:, :(t + 1) * P]
                dve.wait_ge(s["s_exp"], 4 * h + t + 1)
                dve.reciprocal(stat[:, 3, t:t + 1], stat[:, 2, t:t + 1]).then_inc(s["s_rec"], 1)
                dve.wait_ge(s["s_rec"], 4 * h + t + 1)
                dve.tensor_scalar(pr, pr, stat[:, 3, t:t + 1], None, ALU.mult).then_inc(s["s_norm"], 1)

            def attn_out(h):
                dve.wait_ge(s["pv_mm"], h + 1)
                dve.wait_ge(s["zs"], 2 * h + 2)
                dve.tensor_tensor(pr1[:], A0[:], zB[:], ALU.mult).then_inc(s["ob"], 1)

            def head(h, p):
                n = h * NW
                columns(h)
                split(n + 1, 1)
                cgrow(h)
                if p is not None:
                    softmax_max(p, 0)
                    zclamp(p, 1)
                    softmax_max(p, 1)
                    softmax_norm(p, 0)
                    zmul(p, 1)
                    softmax_max(p, 2)
                    softmax_norm(p, 1)
                    softmax_max(p, 3)
                    softmax_norm(p, 2)
                    softmax_norm(p, 3)
                split(n + 2, 0)
                conv(h, 0)
                silu(h, 0)
                if p is not None:
                    attn_out(p)
                split(n + 3, 1)
                norm(h, 0)
                conv(h, 1)
                kT(h)
                kk(h)
                silu(h, 1)
                split(n + 4, 0)
                norm(h, 1)
                UT(h)
                LT(h)
                qk(h)
                n1(h)
                conv(h, 2)
                n2(h)
                silu(h, 2)
                split(n + 5, 1)
                n3(h)
                zclamp(h, 0)
                n4(h)
                vTs(h)
                ma(h, 0)
                zmul(h, 0)
                mb(h, 0)
                split(n + 6, 0)
                ma(h, 1)
                mb(h, 1)
                b_norm(h, 0)
                ma(h, 2)
                mb(h, 2)
                split(n + 7, 1)
                state(h, 0)
                state(h, 1)
                b_norm(h, 1)
                state(h, 2)
                split(n + 8, 0)
                bvTs(h)
                gnorm(h)

            dve.wait_ge(s["rows_T"], 1)
            dve.tensor_copy(chan[:], A0[:, :P]).then_inc(s["rows_ready"], 1)
            dve.wait_ge(s["rows_ready"], 1)
            for t in range(NT):
                dve.wait_ge(s["x_rstd"], t + 1)
                dve.tensor_scalar(xt[:, t % 2, :], xt[:, t % 2, :], rsx[:, t:t + 1], None, ALU.mult)\
                    .then_inc(s["x_scaled"], 1)
                for q in range(4):
                    g = 4 * t + q
                    dve.wait_ge(s["x_T"], g + 1)
                    if g >= 2:
                        dve.wait_ge(s["x_hi"], g - 1)
                        dve.wait_ge(s["x_lo"], g - 1)
                    dve.tensor_tensor(htmp[:, g % 2, :].rearrange("p (k c) -> p k c", c=P), q4(PJ[g % 2]),
                                      chan[:, R_NW + 4 * q:R_NW + 4 * q + 4].unsqueeze(2).broadcast_to([P, 4, P]),
                                      ALU.mult).then_inc(s["x_evac"], 1)
                    dve.wait_ge(s["x_hi"], g + 1)
                    dve.tensor_tensor(h_lo[:, 4 * q:4 * q + 4, tile4(t)],
                                      htmp[:, g % 2, :].rearrange("p (k c) -> p k c", c=P),
                                      h_hi[:, 4 * q:4 * q + 4, tile4(t)].bitcast(F32), ALU.subtract)\
                        .then_inc(s["x_lo"], 1)
            dve.wait_ge(s["w16_hi"], 1)
            dve.tensor_tensor(w16l[:], w16[:], w16h[:].bitcast(F32), ALU.subtract).then_inc(s["w16_lo"], 1)
            split(0, 0)
            dve.wait_ge(s["ba_mm"], 1)
            dve.wait_ge(s["ab_loaded"], 32)
            ab = A1[:, :NT * 2 * H].rearrange("p (t c) -> p t c", t=NT)
            dve.tensor_scalar(ba[:, 0], ab[:, :, 0:H], LEAST, None, ALU.max).then_inc(s["ba_step"], 1)
            dve.tensor_tensor(ba[:, 1], ab[:, :, H:2 * H], dtb[:].unsqueeze(1).broadcast_to([P, NT, H]), ALU.add)\
                .then_inc(s["ba_step"], 1)
            dve.wait_ge(s["ba_step"], 9)
            dve.scalar_tensor_tensor(ba[:, 3], ba[:, 1], 0.0, ba[:, 2], ALU.max, ALU.add).then_inc(s["ba_step"], 1)
            dve.wait_ge(s["ba_step"], 10)
            dve.scalar_tensor_tensor(ba[:, 5], ba[:, 3], -1.0, alog[:].unsqueeze(1).broadcast_to([P, NT, H]),
                                     ALU.mult, ALU.mult).then_inc(s["ba_step"], 1)
            dve.wait_ge(s["cg_mm"], 1)
            cg = A2[:, :NT * H].rearrange("p (t h) -> p t h", t=NT)
            gl = A2[:, NT * H:2 * NT * H].rearrange("p (t h) -> p t h", t=NT)
            dve.tensor_copy(ba[:, 1], cg).then_inc(s["ba_step"], 1)
            dve.tensor_copy(ba[:, 2], gl).then_inc(s["ba_step"], 1)
            dve.wait_ge(s["ba_step"], 13)
            dve.tensor_tensor(ba[:, 3], ba[:, 2], ba[:, 1], ALU.subtract).then_inc(s["ba_step"], 1)
            dve.wait_ge(s["ba_step"], 17)
            dve.tensor_tensor(ba[:, 4], ba[:, 4], ba[:, 0], ALU.mult).then_inc(s["ba_step"], 1)
            dve.wait_ge(s["ba_step"], 18)
            for kind, b in ((HC_G, 5), (HC_CG, 1), (HC_B, 0), (HC_BE, 4), (HC_KD, 3), (HC_GL, 2)):
                dve.tensor_copy(hc[:, :, kind, :], ba[:, b].rearrange("p t h -> p h t")).then_inc(s["hc_set"], 1)
            dve.tensor_scalar(hc[:, :, HC_NB, :], ba[:, 0].rearrange("p t h -> p h t"), -1.0, None, ALU.mult)\
                .then_inc(s["hc_set"], 1)
            dve.wait_ge(s["hc_set"], 7)
            dve.wait_ge(s["pads"], 3)

            head(0, None)
            with dve.Fori(1, H) as i:
                head(i, i - 1)

            def gate_evac(n, slot, u, which):
                dve.wait_ge(s["win_done"], n + 1)
                dve.tensor_scalar(sg[:, u, which, :], PJ[slot][:], LEAST, None, ALU.max).then_inc(s["g_evac"], 1)

            def act_split(c, src, dst, first):
                dve.wait_ge(s["act_hi"], c + 1)
                dve.tensor_tensor(dst[:, first:first + 4, :].rearrange("p k t -> p (k t)"), act_raw[:, c % 2, :],
                                  src[:, first:first + 4, :].rearrange("p k t -> p (k t)").bitcast(F32),
                                  ALU.subtract).then_inc(s["act_lo"], 1)

            def merge(n, u, j):
                dve.wait_ge(s["win_done"], n + 1)
                dve.wait_ge(s["g_sig"], 6 * j + 6)
                a, b = ((G0, G1), (A0, A1))[u]
                dve.tensor_tensor(sg[:, u, 0, :], a[:], sg[:, u, 0, :], ALU.mult).then_inc(s["ya"], 1)
                dve.tensor_tensor(sg[:, u, 1, :], b[:], sg[:, u, 1, :], ALU.mult).then_inc(s["yb"], 1)
                dve.wait_ge(s["ya"], j + 1)
                dve.wait_ge(s["yb"], j + 1)
                dve.tensor_tensor(mgt[:, u, :], sg[:, u, 0, :], sg[:, u, 1, :], ALU.add).then_inc(s["mg"], 1)

            last = H - 1
            split(N1 + 1, 1)
            softmax_max(last, 0)
            zclamp(last, 1)
            softmax_max(last, 1)
            softmax_norm(last, 0)
            zmul(last, 1)
            softmax_max(last, 2)
            softmax_norm(last, 1)
            softmax_max(last, 3)
            softmax_norm(last, 2)
            softmax_norm(last, 3)
            gate_evac(N1, 0, 0, 0)
            split(N1 + 2, 0)
            attn_out(last)
            gate_evac(N1 + 1, 1, 0, 1)
            split(N1 + 3, 1)
            gate_evac(N1 + 2, 0, 1, 0)
            split(N2, 0)
            for c in range(OCH):
                act_split(c, o_hi, o_lo, 4 * c)
            with dve.Fori(0, (KT - 2) // 2) as jj:
                j = jj * 2
                for u in range(2):
                    n = j * 3 + (N2 + 3 * u)
                    gate_evac(n - 1, (u + 1) % 2, (u + 1) % 2, 1)
                    split(n + 1, (u + 1) % 2)
                    split(n + 2, u)
                    merge(n, u, j + u)
                    split(n + 3, (u + 1) % 2)
                    dve.wait_ge(s["mg"], j + (u + 1))
                    gate_evac(n + 1, (u + 1) % 2, u, 0)
                dve.wait_ge(s["mg_out"], 16 * (j + 2))
            gate_evac(N3 - 3, 1, 1, 1)
            split(N3 - 1, 1)
            for c in range(MCH - 1):
                act_split(OCH + c, h_hi, h_lo, 4 * c)
            merge(N3 - 2, 0, KT - 2)
            split(N3, 0)
            merge(N3 - 1, 1, KT - 1)
            split(N3 + 1, 1)
            act_split(OCH + MCH - 1, h_hi, h_lo, 4 * (MCH - 1))

            def residual(eb):
                dve.wait_ge(s["x3_loaded"], 16 * (eb + 1))
                dve.wait_ge(s["out_stored"], 16 * NT * eb)
                for t in range(NT):
                    if t < NT - 1:
                        dve.wait_ge(s["p3_done"], eb * (NT - 1) + (t + 1))
                    else:
                        dve.wait_ge(s["win_done"], eb * 4 + (N3 + 4))
                    dve.tensor_tensor(y3[:, t, :], bank[4 * (eb % 2) + t][:], x3[:, t, :], ALU.add).then_inc(s["resid"], 1)

            dve.sem_inc(s["resid"], 1)
            for eb in range(D // 512):
                for k in range(4 * eb + 2, min(4 * eb + 6, 16)):
                    split(N3 + k, k % 2)
                residual(eb)


_INS = ["x", "norm_w", "w_in", "gdn_conv_w", "gdn_a_log", "gdn_dt_bias", "gdn_norm_w", "moba_q_norm_w",
        "moba_k_norm_w", "w_out_gdn", "w_out_moba", "w_o"]


def shape_constants():
    r, c = np.arange(P)[:, None], np.arange(P)[None, :]
    cst = np.zeros((P, NCONST, P), np.float32)
    cst[:, C_ID] = r == c
    cst[:, C_TRIU] = r <= c
    cst[:, C_DMASK] = np.where(r <= c, 0.0, NEG)
    cst[:, C_CMASK] = np.where(c <= r, 0.0, NEG)
    cst[:, C_STRICT] = r < c
    cst[:, C_M16] = r // 16 == c // 16
    for col, b in ((C_L32, 16), (C_L64, 32), (C_L128, 64)):
        cst[:, col] = (r // b == c // b + 1) & (r // (2 * b) == c // (2 * b))
    freq = np.float32(10000.0) ** (-np.arange(0, P, 2, dtype=np.float32) / np.float32(P))
    ang = np.arange(T, dtype=np.float32)[None, :] * freq.astype(np.float32)[:, None]
    rope = np.empty((P, 2, T), np.float32)
    rope[:P // 2, 0] = rope[P // 2:, 0] = np.cos(ang)
    rope[:P // 2, 1] = np.sin(ang)
    rope[P // 2:, 1] = -np.sin(ang)
    return cst, rope


def kernel(**inputs):
    import concourse.bacc as _bacc
    from concourse.bass_utils import run_bass_kernel_spmd as _run

    nc = _bacc.Bacc("TRN2", target_bir_lowering=False, num_devices=1)
    arrays, args = {}, []
    for name in _INS:
        arrays[f"in_{name}_dram"] = np.ascontiguousarray(inputs[name])
    arrays["const_masks"], arrays["const_rope"] = shape_constants()
    for name, a in arrays.items():
        args.append(nc.dram_tensor(name, a.shape, mybir.dt.from_np(a.dtype), kind="ExternalInput").ap())
    args.append(nc.dram_tensor("out_0_dram", (1, T, D), F32, kind="ExternalOutput").ap())
    hybrid_layer(nc, *args)
    r = _run(nc, [arrays], core_ids=[0])
    return r.results[0]["out_0_dram"]
```

```python
from contextlib import ExitStack

import numpy as np

import concourse.bass as bass
from concourse import mybir

F32 = mybir.dt.float32
F32R = mybir.dt.float32r
ALU = mybir.AluOpType
ACT = mybir.ActivationFunctionType
AX_X = mybir.AxisListType.X

P = 128
D = 2048
T = 512
NT = T // P
KT = D // P
H = 8
W = H * P
EPS = 1e-6
NEG = -1e30
LEAST = -43.0
COL_GDN = 0
COL_BETA = 4 * W
COL_MOBA = COL_BETA + 2 * H
COL_GATE = COL_MOBA + 4 * W
IN_COLS = COL_GATE + 2 * D
SCALE = float(P) ** -0.5
LNSCALE = float(np.log(SCALE))

STRIPES = (("gk", COL_GDN + W), ("gq", COL_GDN), ("gv", COL_GDN + 2 * W), ("gz", COL_GDN + 3 * W),
           ("bk", COL_MOBA + W), ("bq", COL_MOBA), ("bv", COL_MOBA + 2 * W), ("bz", COL_MOBA + 3 * W))
NW = len(STRIPES)
N1 = NW * H
N2 = N1 + 4
N3 = N2 + 3 * KT - 4
BA_G = 11
X_SPLIT = 3 * D // 4
OCH = 2 * H * T // D
MCH = KT * T // D

(C_ID, C_TRIU, C_DMASK, C_CMASK, C_STRICT, C_M16, C_L32, C_L64) = range(8)
NCONST = 8
(HC_G, HC_CG, HC_B, HC_NB, HC_NBE, HC_KD, HC_GL) = range(7)
NHC = 7
R_CONV, R_GW, R_QW, R_KW = 0, 96, 97, 98

SEMS = """
 ident_loaded consts rope_loaded nw_loaded rows_loaded rows_set rows_T rows_ready ab_loaded
 x_loaded0 x_loaded1 x_loaded2 x_loaded3 x_sq x_ln x_rstd x_rs x_scaled_a x_scaled_b
 x_T x_hi x_lo w16_loaded w16_hi w16_lo ba_mm ba_copied ba_T ab_sum ba_step cg_mm hc_set ones_set pads
 raw_loaded0 raw_loaded1 y_loaded0 y_loaded1 hi_ready lo_ready win_done win_evac
 hcol cgrow_mm cg_arg cg_eg cg_dt cg_dts
 conv clampd sig silu sqd ss_mm rn_ln rn norm
 kT_mm kdec kk_mm kkd qk_mm qkd qdec UT_mm Ln LT_mm Ud Ld X1 L32m L64m
 n1_mm L2 U2 n2_mm X2 L4 U4 n3_mm X4 L8 n4_mm X8 ma_mm Y XT mb_mm X
 vT_mm vb ks_mm vbk vn_mm vn st_mm st o_mm o_sq o_ss o_ln o_rn o_1 o_2 o_out
 zclamp zsig zs
 b_sq b_ss b_ln b_rn b_n b_cos b_sinlo b_sinhi b_rope bvT_mm bvT
 s_mm s_mask s_max s_nmax s_exp s_rec s_norm pT_mm pT pv_mm ob ob_out
 g_evac g_sig ya yb mg mg_out
 act_loaded0 act_loaded1 act_hi act_lo last_hi last_lo
 p3_done resid x3_loaded out_stored
""".split()


def hybrid_layer(nc, x, norm_w, w_in, gdn_conv_w, gdn_a_log, gdn_dt_bias, gdn_norm_w, moba_q_norm_w,
                 moba_k_norm_w, w_out_gdn, w_out_moba, w_o, consts, rope, out):
    xs = x[0]
    outs = out[0]
    w_in3 = w_in[0].rearrange("(k p) c -> p k c", p=P)
    wg3 = w_out_gdn[0].rearrange("(k p) c -> p k c", p=P)
    wm3 = w_out_moba[0].rearrange("(k p) c -> p k c", p=P)
    wo3 = w_o[0].rearrange("(k p) c -> p k c", p=P)
    o_dram = nc.dram_tensor("branch_outputs", (2 * H, P, T), F32, kind="Internal").ap()
    m_dram = nc.dram_tensor("merged", (KT, P, T), F32, kind="Internal").ap()

    ctx = ExitStack()
    with ctx:
        def sb(name, shape, dt=F32, at=ctx):
            return at.enter_context(nc.sbuf_tensor(name, shape, dt))

        s = {n: ctx.enter_context(nc.semaphore(n)) for n in SEMS}
        bank = [ctx.enter_context(nc.psum_tensor(f"bank{i}", [P, 512], F32)) for i in range(8)]
        PJ = bank[0:2]
        G0, G1, G2 = bank[2:5]
        A0, A1, A2 = bank[5:8]

        h_hi = sb("h_hi", [P, KT, T], F32R)
        h_lo = sb("h_lo", [P, KT, T], F32R)
        raw = [sb(f"w_raw{i}", [P, D]) for i in range(2)]
        w_hi = [sb(f"w_hi{i}", [P, D], F32R) for i in range(2)]
        w_lo = [sb(f"w_lo{i}", [P, D], F32R) for i in range(2)]
        ones = sb("ones", [P, P])
        mean = sb("mean", [P, P])
        chan = sb("chan", [P, P])
        hc = sb("hc", [P, H, NHC, NT])
        eps = sb("eps", [P, 1])
        lnscale = sb("lnscale", [P, 1])
        sg = sb("sg", [P, 2, 2, T])
        mgt = sb("mgt", [P, 2, T])
        baT = sg[:4 * H, 0, 0, :]
        ab = mgt[:, 1, P:P + NT * 2 * H].rearrange("p (t c) -> p t c", t=NT)
        ba = mgt[:, 0, :6 * NT * H].rearrange("p (b t h) -> p b t h", b=6, t=NT)
        alog, dtb = mgt[:, 1, 0:H], mgt[:, 1, H:2 * H]
        ssx, rsx = mgt[:, 1, 2 * H:2 * H + NT], mgt[:, 1, 2 * H + NT:2 * H + 2 * NT]

        area = ExitStack()
        tmp = ExitStack()
        w16 = sb("w16", [P, KT, 2 * H], at=tmp)
        w16s = sb("w16_split", [P, KT, 2, 2 * H], F32R, at=tmp)
        rows = sb("rows", [P, P], at=tmp)
        xt = sb("x_tiles", [P, NT, D], at=tmp)
        nw = sb("norm_w_rows", [P, D], at=tmp)
        xsq = sb("x_square", [P, D], at=tmp)
        tmp.close()

        rawc = {k: sb(f"raw_{k}", [P, T + 4], at=area) for k in ("gk", "gq", "gv")}
        cv = {k: sb(f"conv_{k}", [P, T], at=area) for k in ("gk", "gq", "gv")}
        dT = sb("decayT", [P, T], at=area)
        w0_, w1_, w2_, w3_, w4_ = [sb(f"work{i}", [P, T], at=area) for i in range(5)]
        xa = sb("inv_a", [P, T], at=area)
        xb = sb("inv_b", [P, T], at=area)
        lm = [sb(f"lower{i}", [P, T], at=area) for i in range(3)]
        onorm = sb("out_norm", [P, T], at=area)
        kdec = sb("k_decay", [P, T], at=area)
        vb = sb("v_beta", [P, T], at=area)
        qdec = sb("q_decay", [P, T], at=area)
        qkT = sb("qkT", [P, T], at=area)
        st = [sb(f"state{i}", [P, P], at=area) for i in range(2)]
        zA = sb("zA", [P, T], at=area)
        hcol = sb("hcol", [P, NHC, NT], at=area)
        cossin = sb("cossin", [P, 2, T], at=area)
        zB = sb("zB", [P, T], at=area)
        zt = sb("z_tmp", [P, T], at=area)
        pt = sb("pt", [P, 4, T], at=area)
        bv = sb("bv", [P, T], at=area)
        pr1 = sb("probs1", [P, T], at=area)
        kr = sb("k_rope", [P, T], at=area)
        qr = sb("q_rope", [P, T], at=area)
        vT = sb("vT", [P, T], at=area)
        stat = sb("softmax_stats", [P, 4, NT], at=area)
        cst = sb("cst", [P, NCONST, P], at=area)
        area.close()

        late = ExitStack()
        act_raw = sb("act_raw", [P, 2, D], at=ctx)
        o_split = sb("o_split", [P, OCH, 2, 4, T], F32R, at=late)
        late.close()
        x3 = sb("x_residual", [P, NT, 512], at=ctx)
        y3 = sb("out_tiles", [P, NT, 512], at=ctx)

        def o_hi(o):
            return o_split[:, o // 4, 0, o % 4, :]

        def o_lo(o):
            return o_split[:, o // 4, 1, o % 4, :]

        ident, triu = cst[:, C_ID, :], cst[:, C_TRIU, :]
        cos, sin = cossin[:, 0, :], cossin[:, 1, :]
        Eg, L2, Yt = w2_, w2_, w2_
        dTs, L4 = w0_, w0_
        Up, U2, XTt = w1_, w1_, w1_
        Ud, U4, vn = w3_, w3_, w3_
        Ld, L8, o1 = w4_, w4_, w4_
        Ln = lm[0]
        probs = [bv, pr1]
        dest = {"gk": rawc["gk"][:, 4:], "gq": rawc["gq"][:, 4:], "gv": rawc["gv"][:, 4:], "gz": zA[:],
                "bk": pt[:, 0, :], "bq": pt[:, 1, :], "bv": bv[:], "bz": zB[:]}

        def tile4(t):
            return slice(t * P, (t + 1) * P)

        def tile4h(t):
            return slice(t * P, t * P + P // 2), slice(t * P + P // 2, (t + 1) * P)

        def corner(ap, half):
            return q4(ap)[:P // 2, :, half * P // 2:(half + 1) * P // 2]

        def q4(ap):
            return ap[:].rearrange("p (t c) -> p t c", t=NT)

        def over(ap):
            return ap.unsqueeze(1).broadcast_to([P, NT, P])

        def hcb(kind):
            return hcol[:, kind, :].unsqueeze(2).broadcast_to([P, NT, P])

        block = ctx.enter_context(nc.Block())

        @block.sync
        def _(sp):
            x_loaded = (s["x_loaded0"], s["x_loaded1"], s["x_loaded2"], s["x_loaded3"])

            def load_x(t):
                sp.dma_start(xt[:, t, :], xs[t * P:(t + 1) * P, :]).then_inc(x_loaded[t], 16)

            load_x(0)
            sp.dma_start(nw[:], norm_w.broadcast_to([P, D])).then_inc(s["nw_loaded"], 16)
            sp.dma_start(cst[:, C_ID, :], consts[:, C_ID, :]).then_inc(s["ident_loaded"], 16)
            load_x(1)
            load_x(2)
            sp.dma_start(w16[:], w_in3[:, :, COL_BETA:COL_BETA + 2 * H]).then_inc(s["w16_loaded"], 16)
            load_x(3)

            loaded = (s["raw_loaded0"], s["raw_loaded1"])

            def slot_free(n):
                sp.wait_ge(s["lo_ready"], n - 1)

            def load(n, slot, src):
                sp.dma_start(raw[slot][:].rearrange("p (k c) -> p k c", k=src.shape[1]), src)\
                    .then_inc(loaded[slot], 16)

            def head_loads(i):
                for w, (_, col) in enumerate(STRIPES):
                    if w == 0:
                        sp.wait_ge(s["lo_ready"], i * NW)
                    elif w > 1:
                        slot_free(i * NW + w)
                    load(i * NW + w, w % 2, w_in3[:, :, bass.ds(i * P + col, P)])

            load(0, 0, w_in3[:, :, STRIPES[0][1]:STRIPES[0][1] + P])
            sp.wait_ge(s["rows_set"], 1)
            for row, src in ((R_CONV, gdn_conv_w[0].rearrange("j (c p) -> (j c) p", p=P)),
                             (R_GW, gdn_norm_w), (R_QW, moba_q_norm_w), (R_KW, moba_k_norm_w)):
                sp.dma_start(rows[row:row + src.shape[0], :], src).then_inc(s["rows_loaded"], 16)
            sp.dma_start(alog, gdn_a_log.broadcast_to([P, H])).then_inc(s["ab_loaded"], 16)
            sp.dma_start(dtb, gdn_dt_bias.broadcast_to([P, H])).then_inc(s["ab_loaded"], 16)
            load(1, 1, w_in3[:, :, STRIPES[1][1]:STRIPES[1][1] + P])
            sp.dma_start(cst[:, C_ID + 1:, :], consts[:, C_ID + 1:, :]).then_inc(s["consts"], 16)
            sp.wait_ge(s["x_T"], 4 * NT)
            sp.dma_start(cossin[:], rope).then_inc(s["rope_loaded"], 16)
            for w in range(2, NW):
                slot_free(w)
                load(w, w % 2, w_in3[:, :, STRIPES[w][1]:STRIPES[w][1] + P])
            with sp.Fori(1, H) as i:
                head_loads(i)

            def gate_load(n, slot, j, which):
                slot_free(n)
                load(n, slot, w_in3[:, :, bass.ds(j * P + (COL_GATE + which * D), P)])

            def y_load(n, slot, j):
                slot_free(n)
                half = raw[slot][:].rearrange("p (b k c) -> p b k c", b=2, k=H)
                sp.dma_start(half[:, 0], wg3[:, :, bass.ds(j * P, P)]).then_inc(loaded[slot], 16)
                sp.dma_start(half[:, 1], wm3[:, :, bass.ds(j * P, P)]).then_inc((s["y_loaded0"], s["y_loaded1"])[slot], 16)

            for c in range(4):
                gate_load(N1 + c, c % 2, c // 2, c % 2)
            with sp.Fori(0, (KT - 2) // 2) as jj:
                j = jj * 2
                for u in range(2):
                    n = j * 3 + (N2 + 3 * u)
                    y_load(n, u % 2, j + u)
                    gate_load(n + 1, (u + 1) % 2, j + (u + 2), 0)
                    gate_load(n + 2, u % 2, j + (u + 2), 1)
            for u in range(2):
                y_load(N2 + 3 * (KT - 2) + u, u, KT - 2 + u)

            def wo_load(n, slot, eb, kc):
                slot_free(n)
                load(n, slot, wo3[:, 4 * kc:4 * kc + 4, bass.ds(eb * 512, 512)])

            with sp.Fori(0, D // 512) as eb:
                for kc in range(4):
                    wo_load(eb * 4 + (N3 + kc), kc % 2, eb, kc)
                    if kc == 1:
                        sp.wait_ge(s["win_done"], N3)
                        sp.wait_ge(s["resid"], eb * NT + (NT + 1))
                        sp.dma_start(x3[:], xs.rearrange("(t p) d -> p t d", p=P)[:, :, bass.ds(eb * 512, 512)])\
                            .then_inc(s["x3_loaded"], 16)

        @block.gpsimd
        def _(pool):
            pool.memset(rows[:], 0.0).then_inc(s["rows_set"], 1)
            for tile, value in ((ones, 1.0), (mean, 1.0 / P), (eps, EPS), (lnscale, LNSCALE)):
                pool.memset(tile[:], value).then_inc(s["ones_set"], 1)
            pool.wait_ge(s["nw_loaded"], 16)
            for t in range(NT):
                part = xt[:, t, X_SPLIT:]
                pool.wait_ge(s["x_rstd"], t + 1)
                pool.tensor_scalar(part, part, rsx[:, t:t + 1], None, ALU.mult).then_inc(s["x_rs"], 1)
                pool.wait_ge(s["x_rs"], t + 1)
                pool.tensor_tensor(part, part, nw[:, X_SPLIT:], ALU.mult).then_inc(s["x_scaled_b"], 1)
            pool.wait_ge(s["ba_mm"], 1)
            for k in ("gk", "gq", "gv"):
                pool.memset(rawc[k][:, 0:4], 0.0).then_inc(s["pads"], 1)

            def head(h, p):
                pool.wait_ge(s["cg_dt"], h + 1)
                pool.wait_ge(s["n3_mm"], h)
                pool.tensor_tensor(q4(dTs), q4(dT), over(cst[:, C_STRICT, :]), ALU.mult).then_inc(s["cg_dts"], 1)
                if p is not None:
                    pool.wait_ge(s["ob"], h)
                    pool.dma_start(o_dram[bass.ds(p + H, 1)].rearrange("o p t -> p (o t)"), pr1[:])\
                        .then_inc(s["ob_out"], 16)
                pool.wait_ge(s["Ln"], h + 1)
                pool.wait_ge(s["ma_mm"], 3 * h)
                pool.tensor_tensor(q4(lm[1]), q4(Ln), over(cst[:, C_L32, :]), ALU.mult).then_inc(s["L32m"], 1)
                pool.tensor_tensor(q4(lm[2]), q4(Ln), over(cst[:, C_L64, :]), ALU.mult).then_inc(s["L64m"], 1)
                pool.wait_ge(s["rope_loaded"], 16)
                for c, r in ((0, kr), (1, qr)):
                    pool.wait_ge(s["b_n"], 2 * h + c + 1)
                    pool.wait_ge(s["s_mm"], 4 * h)
                    pool.tensor_tensor(r[:], pt[:, c, :], cos, ALU.mult).then_inc(s["b_cos"], 1)
                pool.wait_ge(s["o_2"], h + 1)
                pool.dma_start(o_dram[bass.ds(h, 1)].rearrange("o p t -> p (o t)"), o1[:]).then_inc(s["o_out"], 16)

            head(0, None)
            with pool.Fori(1, H) as i:
                head(i, i - 1)

            act_loaded = (s["act_loaded0"], s["act_loaded1"])

            def act_load(c, dram, first, count=4):
                if c >= 2:
                    pool.wait_ge(s["act_lo"], c - 1)
                pool.dma_start(act_raw[:, c % 2, :count * T].rearrange("p (k t) -> p k t", t=T),
                               dram[first:first + count].rearrange("k p t -> p k t"))\
                    .then_inc(act_loaded[c % 2], 16)

            pool.wait_ge(s["o_out"], 16 * H)
            for c in range(2):
                act_load(c, o_dram, 4 * c)
            pool.wait_ge(s["ob"], H)
            pool.dma_start(o_dram[2 * H - 1], pr1[:]).then_inc(s["ob_out"], 16)
            pool.wait_ge(s["ob_out"], 16 * H)
            for c in range(2, OCH):
                act_load(c, o_dram, 4 * c)

            def store_merged(j, u, wait):
                pool.wait_ge(s["mg"], wait)
                pool.dma_start(m_dram[bass.ds(j, 1)].rearrange("o p t -> p (o t)"), mgt[:, u, :])\
                    .then_inc(s["mg_out"], 16)

            with pool.Fori(0, (KT - 2) // 2) as jj:
                j = jj * 2
                for u in range(2):
                    store_merged(j + u, u, j + (u + 1))
            pool.wait_ge(s["mg_out"], 16 * (KT - 2))
            for c in range(MCH):
                act_load(OCH + c, m_dram, 4 * c, 4 if c < MCH - 1 else 2)

            with pool.Fori(0, D // 512) as eb:
                for t in range(NT):
                    pool.wait_ge(s["resid"], eb * NT + (NT + t + 2))
                    pool.dma_start(outs[t * P:(t + 1) * P, bass.ds(eb * 512, 512)], y3[:, t, :])\
                        .then_inc(s["out_stored"], 16)
            pool.wait_ge(s["out_stored"], 16 * NT * (D // 512))

        @block.tensor
        def _(pe):
            def products(slot, k0, k1):
                for k in range(k0, k1):
                    c = slice(k * P, (k + 1) * P)
                    pe.matmul(PJ[slot][:], w_hi[slot][:, c], h_hi[:, k, :], start=(k == 0), stop=False,
                              skip_group_check=True)
                    pe.matmul(PJ[slot][:], w_hi[slot][:, c], h_lo[:, k, :], start=False, stop=False,
                              skip_group_check=True)
                    mm = pe.matmul(PJ[slot][:], w_lo[slot][:, c], h_hi[:, k, :], start=False, stop=(k == KT - 1),
                                   skip_group_check=True)
                if k1 == KT:
                    mm.then_inc(s["win_done"], 1)

            def products_half(slot, half):
                tok = slice(half * T // 2, (half + 1) * T // 2)
                for k in range(KT):
                    c = slice(k * P, (k + 1) * P)
                    pe.matmul(PJ[slot][:, tok], w_hi[slot][:, c], h_hi[:, k, tok], start=(k == 0), stop=False)
                    pe.matmul(PJ[slot][:, tok], w_hi[slot][:, c], h_lo[:, k, tok], start=False, stop=False)
                    mm = pe.matmul(PJ[slot][:, tok], w_lo[slot][:, c], h_hi[:, k, tok], start=False,
                                   stop=(k == KT - 1))
                return mm

            def window(n, slot, k0, k1):
                if k0 == 0:
                    pe.wait_ge(s["lo_ready"], n + 1)
                    if not (isinstance(n, int) and n < 2):
                        pe.wait_ge(s["win_evac"], n - 1)
                products(slot, k0, k1)

            def four(ps, lhsT, rhs):
                for t in range(NT):
                    mm = pe.matmul(ps[:, tile4(t)], lhsT[:, tile4(t)], rhs[:, tile4(t)], start=True, stop=True)
                return mm

            def turn(ps, src):
                for t in range(NT):
                    mm = pe.transpose(ps[:, tile4(t)], src[:, tile4(t)], ident)
                return mm

            def cgrow(h):
                pe.wait_ge(s["hcol"], h + 1)
                pe.wait_ge(s["st"], 3 * h)
                for t in range(NT):
                    mm = pe.matmul(G2[:, tile4(t)], hcol[:, HC_G, t:t + 1].broadcast_to([P, P]), triu,
                                   start=True, stop=True)
                mm.then_inc(s["cgrow_mm"], 1)

            def ss(h, c):
                pe.wait_ge(s["sqd"], 2 * h + c + 1)
                pe.wait_ge((s["o_1"], s["o_ln"])[c], h)
                pe.matmul((G0, G1)[c][:], ones[:], rawc[("gk", "gq")[c]][:, 4:], start=True, stop=True)\
                    .then_inc(s["ss_mm"], 1)

            def kT(h):
                pe.wait_ge(s["norm"], 2 * h + 1)
                turn(G0, cv["gk"]).then_inc(s["kT_mm"], 1)

            def kk(h):
                pe.wait_ge(s["cg_eg"], h + 1)
                four(G2, cv["gk"], cv["gk"]).then_inc(s["kk_mm"], 1)

            def qk(h):
                pe.wait_ge(s["norm"], 2 * h + 2)
                four(G1, cv["gk"], cv["gq"]).then_inc(s["qk_mm"], 1)

            def UT(h):
                pe.wait_ge(s["kkd"], h + 1)
                pe.wait_ge(s["kdec"], h + 1)
                turn(G0, Up).then_inc(s["UT_mm"], 1)

            def LT(h):
                pe.wait_ge(s["Ln"], h + 1)
                turn(G2, Ln).then_inc(s["LT_mm"], 1)

            def n1(h):
                pe.wait_ge(s["Ud"], h + 1)
                pe.wait_ge(s["Ld"], h + 1)
                pe.wait_ge(s["qkd"], h + 1)
                four(G0, Ud, Ld)
                four(G1, Ld, Ud).then_inc(s["n1_mm"], 1)

            def n2(h):
                pe.wait_ge(s["L2"], h + 1)
                pe.wait_ge(s["U2"], h + 1)
                pe.wait_ge(s["X1"], h + 1)
                four(G0, U2, L2)
                four(G1, L2, U2)
                four(G2, L2, xa).then_inc(s["n2_mm"], 1)

            def n3(h):
                pe.wait_ge(s["X2"], h + 1)
                pe.wait_ge(s["L4"], h + 1)
                pe.wait_ge(s["U4"], h + 1)
                four(G0, U4, L4)
                four(G2, L4, xb).then_inc(s["n3_mm"], 1)

            def n4(h):
                pe.wait_ge(s["X4"], h + 1)
                pe.wait_ge(s["L8"], h + 1)
                four(G2, L8, xa).then_inc(s["n4_mm"], 1)

            def vTs(h):
                pe.wait_ge(s["silu"], 3 * h + 3)
                pe.wait_ge(s["U4"], h + 1)
                turn(G1, cv["gv"]).then_inc(s["vT_mm"], 1)

            def ma(h, k):
                src = (xb, xa, xb)[k]
                if k == 0:
                    pe.wait_ge(s["X8"], h + 1)
                    pe.wait_ge(s["L8"], h + 1)
                    pe.wait_ge(s["vb"], h + 1)
                elif k == 1:
                    pe.wait_ge(s["X"], 3 * h + k)
                if k < 2:
                    pe.wait_ge((s["L32m"], s["L64m"])[k], h + 1)
                    four(G0, lm[k + 1], src)
                    mm = turn(G1, src)
                else:
                    for t in range(NT):
                        a, b = tile4h(t)
                        pe.matmul(G0[:P // 2, b], Ln[P // 2:, a], src[P // 2:, b], start=True, stop=True)
                    for t in range(NT):
                        a, b = tile4h(t)
                        mm = pe.transpose(G1[:P // 2, a], src[:P // 2, a], ident[:P // 2, :P // 2])
                mm.then_inc(s["ma_mm"], 1)

            def mb(h, k):
                if k < 2:
                    pe.wait_ge(s["Y"], 3 * h + k + 1)
                    pe.wait_ge(s["XT"], 3 * h + k + 1)
                    mm = four(G2, XTt, Yt)
                else:
                    for t in range(NT):
                        a, b = tile4h(t)
                        mm = pe.matmul(G2[:P // 2, b], XTt[:P // 2, a], Yt[:P // 2, b], start=True, stop=True)
                mm.then_inc(s["mb_mm"], 1)

            def kS(h, t):
                pe.wait_ge(s["st"], 3 * h + t)
                pe.matmul(G1[:, :P], cv["gk"][:, tile4(t)], st[(t - 1) % 2][:], start=True, stop=True)\
                    .then_inc(s["ks_mm"], 1)

            def vnew(h, t):
                if t == 0:
                    pe.wait_ge(s["vb"], h + 1)
                    pe.wait_ge(s["X"], 3 * h + 3)
                else:
                    pe.wait_ge(s["vbk"], 3 * h + t)
                pe.matmul(G1[:, :P], xb[:, tile4(t)], vb[:, tile4(t)], start=True, stop=True).then_inc(s["vn_mm"], 1)

            def outs_(h, t):
                pe.wait_ge(s["vn"], 4 * h + t + 1)
                if t < NT - 1:
                    pe.wait_ge(s["kdec"], h + 1)
                    pe.matmul(G2[:, :P], kdec[:, tile4(t)], vn[:, tile4(t)], start=True, stop=True)\
                        .then_inc(s["st_mm"], 1)
                if t == 0:
                    pe.wait_ge(s["qkd"], h + 1)
                    pe.wait_ge(s["qdec"], h + 1)
                else:
                    pe.matmul(G0[:, tile4(t)], st[(t - 1) % 2][:], qdec[:, tile4(t)], start=True, stop=False)
                pe.matmul(G0[:, tile4(t)], vn[:, tile4(t)], qkT[:, tile4(t)], start=(t == 0), stop=True)\
                    .then_inc(s["o_mm"], 1)

            def gnorm(h):
                pe.wait_ge(s["o_sq"], h + 1)
                pe.matmul(G1[:], mean[:], onorm[:], start=True, stop=True).then_inc(s["o_ss"], 1)

            def b_ss(h, c):
                pe.wait_ge(s["b_sq"], 2 * h + c + 1)
                if c == 0:
                    pe.wait_ge(s["pT"], 4 * h)
                pe.matmul(A2[:], mean[:], pt[:, 2, :], start=True, stop=True).then_inc(s["b_ss"], 1)

            def bvTs(h):
                pe.wait_ge(s["win_evac"], NW * h + 7)
                pe.wait_ge(s["b_ln"], 2 * h + 2)
                turn(A2, bv).then_inc(s["bvT_mm"], 1)

            def scores(h, t):
                pe.wait_ge(s["b_rope"], 2 * h + 2)
                if t >= 2:
                    pe.wait_ge(s["s_exp"], 4 * h + t - 1)
                n = (t + 1) * P
                pe.matmul((A0, A1)[t % 2][:, :n], qr[:, tile4(t)], kr[:, :n], start=True, stop=True)\
                    .then_inc(s["s_mm"], 1)

            def pTs(h, t):
                pe.wait_ge(s["s_norm"], 4 * h + t + 1)
                if t == 0:
                    pe.wait_ge(s["bvT"], h + 1)
                else:
                    pe.wait_ge(s["pT"], 4 * h + t)
                for k in range(t + 1):
                    mm = pe.transpose(A2[:, tile4(k)], probs[t % 2][:, tile4(k)], ident)
                mm.then_inc(s["pT_mm"], 1)

            def pv(h):
                pe.wait_ge(s["pT"], 4 * h + 4)
                for k in range(NT):
                    mm = pe.matmul(A0[:, k * P:], vT[:, tile4(k)], pt[:, k, k * P:],
                                   start=(k == 0), stop=(k == NT - 1))
                mm.then_inc(s["pv_mm"], 1)

            def head(h, p):
                def win(w, a, b):
                    window(h * NW + w, w % 2, a, b)
                if p is not None:
                    win(0, 0, 4)
                    cgrow(h)
                    scores(p, 0)
                    win(0, 4, 8)
                    scores(p, 1)
                    win(0, 8, 11)
                    pTs(p, 0)
                    scores(p, 2)
                    win(0, 11, 16)
                    pTs(p, 1)
                    scores(p, 3)
                    win(1, 0, 4)
                    pTs(p, 2)
                    win(1, 4, 8)
                    pTs(p, 3)
                    win(1, 8, 11)
                    pv(p)
                    win(1, 11, 16)
                else:
                    beta_alpha_T()
                    win(1, 0, 7)
                    cumulate()
                    win(1, 7, 14)
                    cgrow(h)
                    win(1, 14, 16)
                ss(h, 0)
                win(2, 0, 6)
                kT(h)
                kk(h)
                win(2, 6, 11)
                ss(h, 1)
                UT(h)
                win(2, 11, 15)
                LT(h)
                win(2, 15, 16)
                win(3, 0, 1)
                qk(h)
                win(3, 1, 4)
                n1(h)
                win(3, 4, 7)
                n2(h)
                win(3, 7, 10)
                n3(h)
                win(3, 10, 13)
                n4(h)
                win(3, 13, 16)
                vTs(h)
                win(4, 0, 2)
                ma(h, 0)
                win(4, 2, 5)
                mb(h, 0)
                win(4, 5, 8)
                ma(h, 1)
                win(4, 8, 11)
                mb(h, 1)
                win(4, 11, 13)
                pe.wait_ge(s["X"], 3 * h + 2)
                win(4, 13, 14)
                ma(h, 2)
                win(4, 14, 16)
                pe.wait_ge(s["Y"], 3 * h + 3)
                pe.wait_ge(s["XT"], 3 * h + 3)
                win(5, 0, 1)
                mb(h, 2)
                win(5, 1, 4)
                vnew(h, 0)
                win(5, 4, 7)
                outs_(h, 0)
                b_ss(h, 0)
                win(5, 7, 9)
                kS(h, 1)
                win(5, 9, 11)
                vnew(h, 1)
                win(5, 11, 14)
                outs_(h, 1)
                win(5, 14, 16)
                kS(h, 2)
                win(6, 0, 2)
                vnew(h, 2)
                win(6, 2, 4)
                outs_(h, 2)
                b_ss(h, 1)
                win(6, 4, 7)
                kS(h, 3)
                win(6, 7, 10)
                vnew(h, 3)
                win(6, 10, 13)
                outs_(h, 3)
                win(6, 13, 16)
                gnorm(h)
                win(7, 0, 4)
                bvTs(h)
                win(7, 4, 16)

            def beta_alpha(half):
                tok = slice(half * T // 2, (half + 1) * T // 2)
                for k in range(KT):
                    wk = w16s[:, k, :, :].rearrange("p b c -> p (b c)")
                    pe.matmul(A1[:4 * H, tok], wk, h_hi[:, k, tok], start=(k == 0), stop=False)
                    mm = pe.matmul(A1[:4 * H, tok], wk, h_lo[:, k, tok], start=False, stop=(k == KT - 1))
                return mm

            def beta_alpha_T():
                pe.wait_ge(s["ba_copied"], 1)
                for t in range(NT):
                    mm = pe.transpose(A0[:, t * 4 * H:(t + 1) * 4 * H], baT[:, tile4(t)], ident[:4 * H, :4 * H])
                mm.then_inc(s["ba_T"], 1)

            def cumulate():
                pe.wait_ge(s["consts"], 16)
                pe.wait_ge(s["ba_step"], BA_G)
                g = mgt[:, 0, 5 * NT * H:6 * NT * H]
                pe.matmul(A2[:, :NT * H], triu, g, start=True, stop=True)
                pe.matmul(A2[:, NT * H:2 * NT * H], ones[:], g, start=True, stop=True).then_inc(s["cg_mm"], 1)

            pe.wait_ge(s["ident_loaded"], 16)
            xbank = (G0, G1, G2, A0)

            def x_turn(t):
                for q in range(4):
                    g = 4 * t + q
                    if q in (0, 3):
                        pe.wait_ge((s["x_scaled_a"], s["x_scaled_b"])[q // 3], t + 1)
                    if g >= 4:
                        pe.wait_ge(s["x_lo"], g - 3)
                    for k in range(4):
                        mm = pe.transpose(xbank[q][:, tile4(k)], xt[:, t, (4 * q + k) * P:(4 * q + k + 1) * P], ident)
                    mm.then_inc(s["x_T"], 1)

            x_turn(0)
            x_turn(1)
            x_turn(2)
            pe.wait_ge(s["rows_loaded"], 64)
            pe.transpose(A2[:, :P], rows[:], ident).then_inc(s["rows_T"], 1)
            pe.wait_ge(s["w16_lo"], 1)
            pe.wait_ge(s["x_lo"], 8)
            beta_alpha(0)
            x_turn(3)
            pe.wait_ge(s["lo_ready"], 1)
            products_half(0, 0)
            pe.wait_ge(s["x_lo"], 16)
            beta_alpha(1).then_inc(s["ba_mm"], 1)
            products_half(0, 1).then_inc(s["win_done"], 1)

            head(0, None)
            with pe.Fori(1, H) as i:
                head(i, i - 1)

            def gate(n, slot, a, b):
                if a == 0:
                    pe.wait_ge(s["lo_ready"], n + 1)
                products(slot, a, b)

            last = H - 1
            pe.wait_ge(s["win_evac"], N1 - 1)
            gate(N1, 0, 0, 4)
            scores(last, 0)
            gate(N1, 0, 4, 8)
            scores(last, 1)
            gate(N1, 0, 8, 11)
            pTs(last, 0)
            scores(last, 2)
            gate(N1, 0, 11, 16)
            pTs(last, 1)
            scores(last, 3)
            pe.wait_ge(s["win_evac"], N1)
            gate(N1 + 1, 1, 0, 4)
            pTs(last, 2)
            gate(N1 + 1, 1, 4, 8)
            pTs(last, 3)
            gate(N1 + 1, 1, 8, 11)
            pv(last)
            gate(N1 + 1, 1, 11, 16)
            for c in range(2):
                pe.wait_ge(s["g_evac"], c + 1)
                gate(N1 + 2 + c, c, 0, 16)

            ybank = ((G0, G1), (A0, A1))

            def y(n, slot, u):
                pe.wait_ge(s["lo_ready"], n + 1)
                for b in range(2):
                    pe.wait_ge(s["act_lo"], 2 * b + 2)
                    ps = ybank[u][b]
                    for k in range(H):
                        c = slice((b * H + k) * P, (b * H + k + 1) * P)
                        o = b * H + k
                        pe.matmul(ps[:], w_hi[slot][:, c], o_hi(o), start=(k == 0), stop=False)
                        pe.matmul(ps[:], w_hi[slot][:, c], o_lo(o), start=False, stop=False)
                        mm = pe.matmul(ps[:], w_lo[slot][:, c], o_hi(o), start=False, stop=(k == H - 1))
                mm.then_inc(s["win_done"], 1)

            with pe.Fori(0, (KT - 2) // 2) as jj:
                j = jj * 2
                for u in range(2):
                    n = j * 3 + (N2 + 3 * u)
                    y(n, u, u)
                    pe.wait_ge(s["g_evac"], 2 * j + (2 * u + 4))
                    gate(n + 1, (u + 1) % 2, 0, 16)
                    gate(n + 2, u, 0, 16)
            for u in range(2):
                pe.wait_ge(s["yb"], KT - 2)
                y(N2 + 3 * (KT - 2) + u, u, u)

            def p3(n, slot, kc, banks):
                pe.wait_ge(s["lo_ready"], n + 1)
                for t in range(NT):
                    for k in range(4):
                        kt = 4 * kc + k
                        c = slice(k * 512, (k + 1) * 512)
                        pe.matmul(banks[t][:], h_hi[:, kt, tile4(t)], w_hi[slot][:, c],
                                  start=(kt == 0), stop=False)
                        pe.matmul(banks[t][:], h_hi[:, kt, tile4(t)], w_lo[slot][:, c], start=False, stop=False)
                        mm = pe.matmul(banks[t][:], h_lo[:, kt, tile4(t)], w_hi[slot][:, c],
                                       start=False, stop=(kt == KT - 1))
                    if kc == 3 and t < NT - 1:
                        mm.then_inc(s["p3_done"], 1)
                mm.then_inc(s["win_done"], 1)

            with pe.Fori(0, D // 512, 2) as eb:
                for e in range(2):
                    pe.wait_ge(s["resid"], eb * NT + (1, NT + 1)[e])
                    pe.wait_ge(s["g_evac"], 2 * KT)
                    pe.wait_ge(s["yb"], (KT - 1, KT)[e])
                    for kc in range(4):
                        pe.wait_ge(s["act_lo"], OCH + kc + 1)
                        if kc == 3:
                            pe.wait_ge(s["last_lo"], 2)
                        p3(eb * 4 + (N3 + 4 * e + kc), kc % 2, kc, (bank[0:4], bank[4:8])[e])

        @block.scalar
        def _(act):
            loaded = (s["raw_loaded0"], s["raw_loaded1"])
            act.preload_act_table_set("natural_log_exp_and_others")

            def split(n, slot, at, halves=None):
                if not (isinstance(n, int) and n < 2):
                    act.wait_ge(s["win_done"], n - 1)
                act.wait_ge(loaded[slot], 16 * at)
                if halves is not None:
                    act.wait_ge((s["y_loaded0"], s["y_loaded1"])[slot], 16 * halves)
                act.activation(w_hi[slot][:], raw[slot][:], ACT.Copy).then_inc(s["hi_ready"], 1)

            def sigmoid(ap, sem, n):
                act.activation(ap, ap, ACT.Exp, scale=-1.0).then_inc(sem, 1)
                act.wait_ge(sem, n + 1)
                act.activation(ap, ap, ACT.Ln, bias=1.0).then_inc(sem, 1)
                act.wait_ge(sem, n + 2)
                act.activation(ap, ap, ACT.Exp, scale=-1.0).then_inc(sem, 1)

            def evac(h, w):
                name = STRIPES[w][0]
                act.wait_ge(s["win_done"], h * NW + w + 1)
                if not (isinstance(h, int) and h == 0):
                    if name in ("gk", "gq"):
                        act.wait_ge(s["norm"], 2 * h + w - 1)
                    elif name == "gv":
                        act.wait_ge(s["silu"], 3 * h)
                    elif name == "gz":
                        act.wait_ge(s["o_2"], h)
                    elif name == "bk":
                        act.wait_ge(s["pv_mm"], h)
                    elif name == "bv":
                        act.wait_ge(s["pT_mm"], 4 * h)
                act.activation(dest[name], PJ[w % 2][:], ACT.Copy).then_inc(s["win_evac"], 1)

            def cgrow(h):
                act.wait_ge(s["cg_arg"], 4 * h + 4)
                act.wait_ge(s["mb_mm"], 3 * h)
                act.activation(Eg[:], G2[:], ACT.Exp).then_inc(s["cg_eg"], 1)
                act.activation(dT[:], dT[:], ACT.Exp).then_inc(s["cg_dt"], 1)

            def silu(h, c):
                act.wait_ge(s["clampd"], 3 * h + c + 1)
                sigmoid(rawc[("gk", "gq", "gv")[c]][:, 4:], s["sig"], 9 * h + 3 * c)

            def sq(h, c):
                k = ("gk", "gq")[c]
                act.wait_ge(s["silu"], 3 * h + c + 1)
                act.activation(rawc[k][:, 4:], cv[k][:], ACT.Square).then_inc(s["sqd"], 1)

            def rnorm(h, c):
                r = rawc[("gk", "gq")[c]][:, 4:]
                act.wait_ge(s["ss_mm"], 2 * h + c + 1)
                act.activation(r, (G0, G1)[c][:], ACT.Ln, bias=eps[:, 0:1]).then_inc(s["rn_ln"], 1)
                act.wait_ge(s["rn_ln"], 2 * h + c + 1)
                if c == 0:
                    act.activation(r, r, ACT.Exp, scale=-0.5).then_inc(s["rn"], 1)
                else:
                    act.activation(r, r, ACT.Exp, scale=-0.5, bias=lnscale[:, 0:1]).then_inc(s["rn"], 1)

            def n1(h):
                act.wait_ge(s["n1_mm"], h + 1)
                act.wait_ge(s["qdec"], h + 1)
                act.activation(L2[:], G0[:], ACT.Copy).then_inc(s["L2"], 1)

            def n2(h):
                act.wait_ge(s["n2_mm"], h + 1)
                act.activation(L4[:], G0[:], ACT.Copy).then_inc(s["L4"], 1)
                act.activation(U4[:], G1[:], ACT.Copy).then_inc(s["U4"], 1)

            def n3(h):
                act.wait_ge(s["n3_mm"], h + 1)
                act.activation(L8[:], G0[:], ACT.Copy).then_inc(s["L8"], 1)

            def ma(h, k):
                act.wait_ge(s["ma_mm"], 3 * h + k + 1)
                if k < 2:
                    act.activation(Yt[:], G0[:], ACT.Copy).then_inc(s["Y"], 1)
                else:
                    act.activation(corner(Yt, 1), corner(G0, 1), ACT.Copy).then_inc(s["Y"], 1)

            def vnew(h, t):
                act.wait_ge(s["vn_mm"], 4 * h + t + 1)
                act.activation(vn[:, tile4(t)], G1[:, :P], ACT.Copy).then_inc(s["vn"], 1)

            def gnorm_sq(h):
                act.wait_ge(s["o_mm"], 4 * h + 4)
                act.activation(onorm[:], G0[:], ACT.Square).then_inc(s["o_sq"], 1)

            def gnorm(h):
                act.wait_ge(s["o_ss"], h + 1)
                act.activation(onorm[:], G1[:], ACT.Ln, bias=eps[:, 0:1]).then_inc(s["o_ln"], 1)
                act.wait_ge(s["o_ln"], h + 1)
                act.activation(onorm[:], onorm[:], ACT.Exp, scale=-0.5).then_inc(s["o_rn"], 1)

            def zsig(h, b):
                act.wait_ge(s["zclamp"], 2 * h + b + 1)
                sigmoid(zt[:], s["zsig"], 6 * h + 3 * b)

            def b_sq(h, c):
                act.wait_ge(s["win_evac"], NW * h + 5 + c)
                if c == 0:
                    act.wait_ge(s["pv_mm"], h)
                else:
                    act.wait_ge(s["b_n"], 2 * h + 1)
                act.activation(pt[:, 2, :], pt[:, c, :], ACT.Square).then_inc(s["b_sq"], 1)

            def b_rn(h, c):
                act.wait_ge(s["b_ss"], 2 * h + c + 1)
                act.activation(pt[:, 2, :], A2[:], ACT.Ln, bias=eps[:, 0:1]).then_inc(s["b_ln"], 1)
                act.wait_ge(s["b_ln"], 2 * h + c + 1)
                act.activation(pt[:, 2, :], pt[:, 2, :], ACT.Exp, scale=-0.5).then_inc(s["b_rn"], 1)

            def softmax(h, t):
                act.wait_ge(s["s_nmax"], 4 * h + t + 1)
                if t >= 2:
                    act.wait_ge(s["pT_mm"], 4 * h + t - 1)
                elif t == 0:
                    act.wait_ge(s["bvT_mm"], h + 1)
                n = (t + 1) * P
                act.activation(probs[t % 2][:, :n], (A0, A1)[t % 2][:, :n], ACT.Exp, scale=SCALE,
                               bias=stat[:, 1, t:t + 1], accum_out=stat[:, 2, t:t + 1]).then_inc(s["s_exp"], 1)

            def pTc(h, t):
                act.wait_ge(s["pT_mm"], 4 * h + t + 1)
                act.activation(pt[:, 0:t + 1, tile4(t)],
                               A2[:, :(t + 1) * P].rearrange("p (k c) -> p k c", c=P), ACT.Copy).then_inc(s["pT"], 1)

            def at(i, w):
                return i * (NW // 2) + (w // 2 + 1)

            def split_next(i, w):
                if w + 1 < NW:
                    split(i * NW + (w + 1), (w + 1) % 2, at(i, w + 1))
                else:
                    split(i * NW + NW, 0, i * (NW // 2) + (NW // 2 + 1))

            def head(h, p):
                if p is not None:
                    evac(p, NW - 1)
                    split_next(h, 0)
                    cgrow(h)
                if p is not None:
                    softmax(p, 0)
                    zsig(p, 1)
                    softmax(p, 1)
                    pTc(p, 0)
                    softmax(p, 2)
                    pTc(p, 1)
                    softmax(p, 3)
                    evac(h, 0)
                    split_next(h, 1)
                    pTc(p, 2)
                    pTc(p, 3)
                    silu(h, 0)
                    sq(h, 0)
                else:
                    evac(h, 0)
                    decay_steps()
                    split_next(h, 1)
                    silu(h, 0)
                    decay_exps()
                    sq(h, 0)
                    cgrow(h)
                evac(h, 1)
                split_next(h, 2)
                rnorm(h, 0)
                silu(h, 1)
                sq(h, 1)
                rnorm(h, 1)
                evac(h, 2)
                split_next(h, 3)
                n1(h)
                n2(h)
                silu(h, 2)
                n3(h)
                evac(h, 3)
                split_next(h, 4)
                ma(h, 0)
                zsig(h, 0)
                ma(h, 1)
                ma(h, 2)
                evac(h, 4)
                split_next(h, 5)
                b_sq(h, 0)
                vnew(h, 0)
                b_rn(h, 0)
                vnew(h, 1)
                evac(h, 5)
                vnew(h, 2)
                split_next(h, 6)
                b_sq(h, 1)
                b_rn(h, 1)
                vnew(h, 3)
                if p is not None:
                    act.wait_ge(s["ob_out"], 16 * h)
                gnorm_sq(h)
                gnorm(h)
                evac(h, 6)
                split_next(h, 7)

            act.wait_ge(s["ones_set"], 4)

            def x_rstd(t):
                act.wait_ge((s["x_loaded0"], s["x_loaded1"], s["x_loaded2"], s["x_loaded3"])[t], 16)
                if t > 0:
                    act.wait_ge(s["x_sq"], t)
                act.activation(xsq[:], xt[:, t, :], ACT.Square, accum_out=ssx[:, t:t + 1]).then_inc(s["x_sq"], 1)
                act.wait_ge(s["x_sq"], t + 1)
                act.activation(rsx[:, t:t + 1], ssx[:, t:t + 1], ACT.Ln, scale=1.0 / D, bias=eps[:, 0:1])\
                    .then_inc(s["x_ln"], 1)
                act.wait_ge(s["x_ln"], t + 1)
                act.activation(rsx[:, t:t + 1], rsx[:, t:t + 1], ACT.Exp, scale=-0.5).then_inc(s["x_rstd"], 1)

            def x_hi(t):
                for q in range(4):
                    act.wait_ge(s["x_T"], 4 * t + q + 1)
                    act.activation(h_hi[:, 4 * q:4 * q + 4, tile4(t)], q4((G0, G1, G2, A0)[q]), ACT.Copy)\
                        .then_inc(s["x_hi"], 1)

            x_rstd(0)
            x_rstd(1)
            x_hi(0)
            x_rstd(2)
            x_hi(1)
            act.wait_ge(s["w16_loaded"], 16)
            act.activation(w16s[:, :, 0, :], w16[:], ACT.Copy).then_inc(s["w16_hi"], 1)
            x_rstd(3)
            x_hi(2)
            split(0, 0, 1)
            x_hi(3)
            split(1, 1, 1)

            def decay_steps():
                act.wait_ge(s["ba_step"], 2)
                sigmoid(ba[:, 0], s["ba_step"], 2)
                act.wait_ge(s["ba_step"], 5)
                act.activation(ba[:, 2], ba[:, 1], ACT.Abs).then_inc(s["ba_step"], 1)
                act.wait_ge(s["ba_step"], 6)
                act.activation(ba[:, 2], ba[:, 2], ACT.Exp, scale=-1.0).then_inc(s["ba_step"], 1)
                act.wait_ge(s["ba_step"], 7)
                act.activation(ba[:, 2], ba[:, 2], ACT.Ln, bias=1.0).then_inc(s["ba_step"], 1)
                act.activation(alog, alog, ACT.Exp).then_inc(s["ba_step"], 1)

            def decay_exps():
                act.wait_ge(s["ba_step"], BA_G + 3)
                act.activation(ba[:, 3], ba[:, 3], ACT.Exp).then_inc(s["ba_step"], 1)
                act.activation(ba[:, 4], ba[:, 1], ACT.Exp).then_inc(s["ba_step"], 1)
                act.activation(ba[:, 2], ba[:, 2], ACT.Exp).then_inc(s["ba_step"], 1)

            act.wait_ge(s["ba_mm"], 1)
            act.activation(baT, A1[:4 * H, :], ACT.Copy).then_inc(s["ba_copied"], 1)
            act.wait_ge(s["ab_loaded"], 32)

            head(0, None)
            with act.Fori(1, H) as i:
                head(i, i - 1)

            last = H - 1
            evac(last, NW - 1)
            split(N1 + 1, 1, (N1 + 1) // 2 + 1)
            softmax(last, 0)
            zsig(last, 1)
            softmax(last, 1)
            pTc(last, 0)
            softmax(last, 2)
            pTc(last, 1)
            softmax(last, 3)

            def gate_sigmoid(u, which, count):
                act.wait_ge(s["g_evac"], count + 1)
                sigmoid(sg[:, u, which, :], s["g_sig"], 3 * count)

            def act_split(c, dst, count=4):
                act.wait_ge((s["act_loaded0"], s["act_loaded1"])[c % 2], 16 * (c // 2 + 1))
                act.activation(dst.rearrange("p k t -> p (k t)"), act_raw[:, c % 2, :count * T],
                               ACT.Copy).then_inc(s["act_hi"], 1)

            act_split(0, o_split[:, 0, 0])
            split(N1 + 2, 0, (N1 + 2) // 2 + 1)
            pTc(last, 2)
            pTc(last, 3)
            act_split(1, o_split[:, 1, 0])
            gate_sigmoid(0, 0, 0)
            split(N1 + 3, 1, (N1 + 3) // 2 + 1)
            act.wait_ge(s["ob_out"], 16 * H)
            act_split(2, o_split[:, 2, 0])
            gate_sigmoid(0, 1, 1)
            act_split(3, o_split[:, 3, 0])
            split(N2, 0, N2 // 2 + 1, 1)
            gate_sigmoid(1, 0, 2)

            with act.Fori(0, (KT - 2) // 2) as jj:
                for u in range(2):
                    def nth(k):
                        c = 3 * u + k
                        return jj * 6 + (N2 + c), c % 2, jj * 3 + ((N2 + c) // 2 + 1)
                    split(*nth(1))
                    gate_sigmoid((u + 1) % 2, 1, 4 * jj + (2 * u + 3))
                    split(*nth(2))
                    split(*nth(3), jj + (u + 1))
                    gate_sigmoid(u, 0, 4 * jj + (2 * u + 4))
            n = N3 - 2
            split(n + 1, 1, (n + 1) // 2 + 1, KT // 2)
            gate_sigmoid(1, 1, 2 * KT - 1)
            act.wait_ge(s["win_done"], N3 - 2)
            def last_hi(u):
                act.wait_ge(s["mg"], KT - 1 + u)
                act.activation(h_hi[:, KT - 2 + u, :], mgt[:, u, :], ACT.Copy).then_inc(s["last_hi"], 1)

            act_split(OCH, h_hi[:, 0:4])
            act_split(OCH + 1, h_hi[:, 4:8])
            split(N3, 0, N3 // 2 + 1)
            last_hi(0)
            act_split(OCH + 2, h_hi[:, 8:12])
            act_split(OCH + 3, h_hi[:, 12:14], 2)
            split(N3 + 1, 1, (N3 + 1) // 2 + 1)
            last_hi(1)
            with act.Fori(0, 3) as eb:
                for k in range(2, 6):
                    split(eb * 4 + (N3 + k), k % 2, eb * 2 + ((N3 + k) // 2 + 1))
            for k in range(14, 16):
                split(N3 + k, k % 2, (N3 + k) // 2 + 1)

        @block.vector
        def _(dve):
            def split(n, slot):
                dve.wait_ge(s["hi_ready"], n + 1)
                dve.tensor_tensor(w_lo[slot][:], raw[slot][:], w_hi[slot][:].bitcast(F32), ALU.subtract)\
                    .then_inc(s["lo_ready"], 1)

            def columns(h):
                dve.tensor_copy(hcol[:].rearrange("p k t -> p (k t)"),
                                hc[:, bass.ds(h, 1), :, :].rearrange("p h k t -> p (h k t)")).then_inc(s["hcol"], 1)

            def cgrow(h):
                dve.wait_ge(s["cgrow_mm"], h + 1)
                dve.wait_ge(s["cg_dts"], h)
                for t in range(NT):
                    dve.scalar_tensor_tensor(dT[:, tile4(t)], G2[:, tile4(t)], hcol[:, HC_CG, t:t + 1],
                                             cst[:, C_DMASK, :], ALU.subtract, ALU.add).then_inc(s["cg_arg"], 1)

            def conv(h, c):
                name, col = (("gk", H), ("gq", 0), ("gv", 2 * H))[c]
                r, y = rawc[name], cv[name]
                dve.wait_ge(s["win_evac"], h * NW + c + 1)
                dve.wait_ge((s["ks_mm"], s["qk_mm"], s["vT_mm"])[c], (3 * h, h, h)[c])

                def tap(j):
                    return chan[:, bass.ds(h + (R_CONV + 3 * H * j + col), 1)]

                n = 12 * h + 4 * c
                dve.tensor_scalar(y[:], r[:, 4:4 + T], tap(3), None, ALU.mult).then_inc(s["conv"], 1)
                for j in range(3):
                    dve.wait_ge(s["conv"], n + j + 1)
                    dve.scalar_tensor_tensor(y[:], r[:, 1 + j:1 + j + T], tap(j), y[:], ALU.mult, ALU.add)\
                        .then_inc(s["conv"], 1)
                dve.wait_ge(s["conv"], n + 4)
                dve.tensor_scalar(r[:, 4:], y[:], LEAST, None, ALU.max).then_inc(s["clampd"], 1)

            def silu(h, c):
                name = ("gk", "gq", "gv")[c]
                dve.wait_ge(s["sig"], 9 * h + 3 * c + 3)
                dve.tensor_tensor(cv[name][:], cv[name][:], rawc[name][:, 4:], ALU.mult).then_inc(s["silu"], 1)

            def norm(h, c):
                name = ("gk", "gq")[c]
                dve.wait_ge(s["rn"], 2 * h + c + 1)
                dve.tensor_tensor(cv[name][:], cv[name][:], rawc[name][:, 4:], ALU.mult).then_inc(s["norm"], 1)

            def kT(h):
                dve.wait_ge(s["kT_mm"], h + 1)
                dve.wait_ge(s["st_mm"], 3 * h)
                dve.tensor_tensor(q4(kdec), q4(G0), hcb(HC_KD), ALU.mult).then_inc(s["kdec"], 1)

            def kk(h):
                dve.wait_ge(s["kk_mm"], h + 1)
                dve.wait_ge(s["cg_dts"], h + 1)
                dve.wait_ge(s["mb_mm"], 3 * h)
                dve.tensor_tensor(Up[:], G2[:], dTs[:], ALU.mult).then_inc(s["kkd"], 1)

            def UT(h):
                dve.wait_ge(s["UT_mm"], h + 1)
                dve.wait_ge(s["ma_mm"], 3 * h)
                dve.tensor_tensor(q4(Ln), q4(G0), hcb(HC_NB), ALU.mult).then_inc(s["Ln"], 1)

            def LT(h):
                dve.wait_ge(s["LT_mm"], h + 1)
                dve.wait_ge(s["o_mm"], 4 * h)
                dve.tensor_tensor(q4(Ud), q4(G2), over(cst[:, C_M16, :]), ALU.mult).then_inc(s["Ud"], 1)
                dve.wait_ge(s["o_out"], 16 * h)
                dve.tensor_tensor(q4(Ld), q4(Ln), over(cst[:, C_M16, :]), ALU.mult).then_inc(s["Ld"], 1)
                dve.wait_ge(s["Ud"], h + 1)
                dve.tensor_tensor(q4(xa), q4(Ud), over(ident), ALU.add).then_inc(s["X1"], 1)

            def qk(h):
                dve.wait_ge(s["cg_dt"], h + 1)
                dve.wait_ge(s["qk_mm"], h + 1)
                dve.tensor_tensor(qkT[:], G1[:], dT[:], ALU.mult).then_inc(s["qkd"], 1)
                dve.wait_ge(s["cg_eg"], h + 1)
                dve.wait_ge(s["norm"], 2 * h + 2)
                dve.tensor_tensor(qdec[:], cv["gq"][:], Eg[:], ALU.mult).then_inc(s["qdec"], 1)

            def n1(h):
                dve.wait_ge(s["n1_mm"], h + 1)
                dve.tensor_copy(U2[:], G1[:]).then_inc(s["U2"], 1)

            def n2(h):
                dve.wait_ge(s["n2_mm"], h + 1)
                dve.wait_ge(s["X1"], h + 1)
                dve.wait_ge(s["vn_mm"], 4 * h)
                dve.tensor_tensor(xb[:], G2[:], xa[:], ALU.add).then_inc(s["X2"], 1)

            def n3(h):
                dve.wait_ge(s["n3_mm"], h + 1)
                dve.wait_ge(s["X2"], h + 1)
                dve.tensor_tensor(xa[:], G2[:], xb[:], ALU.add).then_inc(s["X4"], 1)

            def n4(h):
                dve.wait_ge(s["n4_mm"], h + 1)
                dve.wait_ge(s["X4"], h + 1)
                dve.tensor_tensor(xb[:], G2[:], xa[:], ALU.add).then_inc(s["X8"], 1)

            def vTs(h):
                dve.wait_ge(s["vT_mm"], h + 1)
                dve.tensor_tensor(q4(vb), q4(G1), hcb(HC_B), ALU.mult).then_inc(s["vb"], 1)

            def ma(h, k):
                dve.wait_ge(s["ma_mm"], 3 * h + k + 1)
                if k < 2:
                    dve.tensor_copy(XTt[:], G1[:]).then_inc(s["XT"], 1)
                else:
                    dve.tensor_copy(corner(XTt, 0), corner(G1, 0)).then_inc(s["XT"], 1)

            def mb(h, k):
                a, b = ((xb, xa), (xa, xb), (corner(xb, 1), corner(xb, 1)))[k]
                dve.wait_ge(s["mb_mm"], 3 * h + k + 1)
                if k == 0:
                    dve.wait_ge(s["X8"], h + 1)
                else:
                    dve.wait_ge(s["X"], 3 * h + k)
                g = G2[:] if k < 2 else corner(G2, 1)
                dve.tensor_tensor(b[:], g, a[:], ALU.add).then_inc(s["X"], 1)

            def kS(h, t):
                dve.wait_ge(s["ks_mm"], 3 * h + t)
                dve.wait_ge(s["vb"], h + 1)
                dve.scalar_tensor_tensor(vb[:, tile4(t)], G1[:, :P], hcol[:, HC_NBE, t:t + 1], vb[:, tile4(t)],
                                         ALU.mult, ALU.add).then_inc(s["vbk"], 1)

            def state(h, t):
                dve.wait_ge(s["st_mm"], 3 * h + t + 1)
                if t == 0:
                    dve.tensor_copy(st[0][:], G2[:, :P]).then_inc(s["st"], 1)
                else:
                    dve.wait_ge(s["st"], 3 * h + t)
                    dve.scalar_tensor_tensor(st[t % 2][:], st[(t - 1) % 2][:], hcol[:, HC_GL, t:t + 1], G2[:, :P],
                                             ALU.mult, ALU.add).then_inc(s["st"], 1)

            def gnorm(h):
                dve.wait_ge(s["o_rn"], h + 1)
                dve.scalar_tensor_tensor(o1[:], G0[:], chan[:, R_GW:R_GW + 1], onorm[:], ALU.mult, ALU.mult)\
                    .then_inc(s["o_1"], 1)
                dve.wait_ge(s["o_1"], h + 1)
                dve.wait_ge(s["zs"], 2 * h + 1)
                dve.tensor_tensor(o1[:], o1[:], zA[:], ALU.mult).then_inc(s["o_2"], 1)

            def zclamp(h, b):
                dve.wait_ge(s["win_evac"], h * NW + (4, 8)[b])
                dve.tensor_scalar(zt[:], (zA, zB)[b][:], LEAST, None, ALU.max).then_inc(s["zclamp"], 1)

            def zmul(h, b):
                z = (zA, zB)[b]
                dve.wait_ge(s["zsig"], 6 * h + 3 * b + 3)
                dve.tensor_tensor(z[:], z[:], zt[:], ALU.mult).then_inc(s["zs"], 1)

            def b_norm(h, c):
                r, w = ((kr, R_KW), (qr, R_QW))[c]
                x_ = pt[:, c, :]
                lo, hi = slice(0, P // 2), slice(P // 2, P)
                dve.wait_ge(s["b_rn"], 2 * h + c + 1)
                dve.scalar_tensor_tensor(x_, x_, chan[:, w:w + 1], pt[:, 2, :], ALU.mult, ALU.mult)\
                    .then_inc(s["b_n"], 1)
                dve.wait_ge(s["b_n"], 2 * h + c + 1)
                dve.wait_ge(s["rope_loaded"], 16)
                if c == 0:
                    dve.wait_ge(s["pv_mm"], h)
                dve.tensor_tensor(pt[lo, 3, :], pt[hi, c, :], cossin[hi, 1, :], ALU.mult).then_inc(s["b_sinlo"], 1)
                dve.tensor_tensor(pt[hi, 3, :], pt[lo, c, :], cossin[lo, 1, :], ALU.mult).then_inc(s["b_sinhi"], 1)
                dve.wait_ge(s["b_sinlo"], 2 * h + c + 1)
                dve.wait_ge(s["b_sinhi"], 2 * h + c + 1)
                dve.wait_ge(s["b_cos"], 2 * h + c + 1)
                dve.tensor_tensor(r[:], r[:], pt[:, 3, :], ALU.add).then_inc(s["b_rope"], 1)

            def bvTs(h):
                dve.wait_ge(s["bvT_mm"], h + 1)
                dve.wait_ge(s["pv_mm"], h)
                dve.tensor_copy(vT[:], A2[:]).then_inc(s["bvT"], 1)

            def softmax_max(h, t):
                ps = (A0, A1)[t % 2]
                dve.wait_ge(s["s_mm"], 4 * h + t + 1)
                dve.tensor_tensor(ps[:, tile4(t)], ps[:, tile4(t)], cst[:, C_CMASK, :], ALU.add)\
                    .then_inc(s["s_mask"], 1)
                dve.wait_ge(s["s_mask"], 4 * h + t + 1)
                dve.tensor_reduce(stat[:, 0, t:t + 1], ps[:, :(t + 1) * P], AX_X, ALU.max).then_inc(s["s_max"], 1)
                dve.wait_ge(s["s_max"], 4 * h + t + 1)
                dve.tensor_scalar(stat[:, 1, t:t + 1], stat[:, 0, t:t + 1], -SCALE, None, ALU.mult)\
                    .then_inc(s["s_nmax"], 1)

            def softmax_norm(h, t):
                pr = probs[t % 2][:, :(t + 1) * P]
                dve.wait_ge(s["s_exp"], 4 * h + t + 1)
                dve.reciprocal(stat[:, 3, t:t + 1], stat[:, 2, t:t + 1]).then_inc(s["s_rec"], 1)
                dve.wait_ge(s["s_rec"], 4 * h + t + 1)
                dve.tensor_scalar(pr, pr, stat[:, 3, t:t + 1], None, ALU.mult).then_inc(s["s_norm"], 1)

            def attn_out(h):
                dve.wait_ge(s["pv_mm"], h + 1)
                dve.wait_ge(s["zs"], 2 * h + 2)
                dve.tensor_tensor(pr1[:], A0[:], zB[:], ALU.mult).then_inc(s["ob"], 1)

            def head(h, p):
                n = h * NW
                if p is None:
                    decays()
                    dve.wait_ge(s["pads"], 3)
                    conv(h, 0)
                    cumulated()
                    silu(h, 0)
                    head_columns()
                    columns(h)
                    cgrow(h)
                    split(n + 2, 0)
                else:
                    columns(h)
                    split(n + 1, 1)
                    cgrow(h)
                    softmax_max(p, 0)
                    zclamp(p, 1)
                    softmax_max(p, 1)
                    softmax_norm(p, 0)
                    zmul(p, 1)
                    softmax_max(p, 2)
                    softmax_norm(p, 1)
                    softmax_max(p, 3)
                    softmax_norm(p, 2)
                    softmax_norm(p, 3)
                    conv(h, 0)
                    split(n + 2, 0)
                    silu(h, 0)
                    attn_out(p)
                conv(h, 1)
                norm(h, 0)
                split(n + 3, 1)
                kT(h)
                silu(h, 1)
                kk(h)
                UT(h)
                norm(h, 1)
                LT(h)
                qk(h)
                split(n + 4, 0)
                n1(h)
                conv(h, 2)
                n2(h)
                silu(h, 2)
                n3(h)
                n4(h)
                vTs(h)
                zclamp(h, 0)
                ma(h, 0)
                split(n + 5, 1)
                zmul(h, 0)
                mb(h, 0)
                ma(h, 1)
                mb(h, 1)
                ma(h, 2)
                mb(h, 2)
                split(n + 6, 0)
                state(h, 0)
                kS(h, 1)
                b_norm(h, 0)
                state(h, 1)
                kS(h, 2)
                state(h, 2)
                split(n + 7, 1)
                kS(h, 3)
                b_norm(h, 1)
                gnorm(h)
                split(n + 8, 0)
                bvTs(h)

            dve.sem_inc(s["resid"], NT + 1)
            dve.wait_ge(s["nw_loaded"], 16)

            def x_scale(t):
                dve.wait_ge(s["x_rstd"], t + 1)
                dve.scalar_tensor_tensor(xt[:, t, :X_SPLIT], xt[:, t, :X_SPLIT], rsx[:, t:t + 1],
                                         nw[:, :X_SPLIT], ALU.mult, ALU.mult).then_inc(s["x_scaled_a"], 1)

            def x_lo(t):
                for q in range(4):
                    dve.wait_ge(s["x_hi"], 4 * t + q + 1)
                    dve.tensor_tensor(h_lo[:, 4 * q:4 * q + 4, tile4(t)], q4((G0, G1, G2, A0)[q]),
                                      h_hi[:, 4 * q:4 * q + 4, tile4(t)].bitcast(F32), ALU.subtract)\
                        .then_inc(s["x_lo"], 1)

            x_scale(0)
            x_scale(1)
            x_lo(0)
            x_scale(2)
            x_lo(1)
            dve.wait_ge(s["w16_hi"], 1)
            dve.tensor_tensor(w16s[:, :, 1, :], w16[:], w16s[:, :, 0, :].bitcast(F32), ALU.subtract).then_inc(s["w16_lo"], 1)
            x_scale(3)
            x_lo(2)
            dve.wait_ge(s["rows_T"], 1)
            dve.tensor_copy(chan[:], A2[:, :P]).then_inc(s["rows_ready"], 1)
            split(0, 0)
            x_lo(3)
            split(1, 1)
            dve.wait_ge(s["rows_ready"], 1)

            def decays():
                dve.wait_ge(s["ba_T"], 1)
                dve.wait_ge(s["ab_loaded"], 32)
                parts = A0[:, :NT * 4 * H].rearrange("p (t b c) -> p t b c", t=NT, b=2)
                dve.tensor_copy(ab, parts[:, :, 0, :]).then_inc(s["ab_sum"], 1)
                dve.wait_ge(s["ab_sum"], 1)
                dve.tensor_tensor(ab, ab, parts[:, :, 1, :], ALU.add).then_inc(s["ab_sum"], 1)
                dve.wait_ge(s["ab_sum"], 2)
                dve.tensor_scalar(ba[:, 0], ab[:, :, 0:H], LEAST, None, ALU.max).then_inc(s["ba_step"], 1)
                dve.tensor_tensor(ba[:, 1], ab[:, :, H:2 * H], dtb.unsqueeze(1).broadcast_to([P, NT, H]), ALU.add)\
                    .then_inc(s["ba_step"], 1)
                dve.wait_ge(s["ba_step"], 9)
                dve.scalar_tensor_tensor(ba[:, 3], ba[:, 1], 0.0, ba[:, 2], ALU.max, ALU.add)\
                    .then_inc(s["ba_step"], 1)
                dve.wait_ge(s["ba_step"], 10)
                dve.scalar_tensor_tensor(ba[:, 5], ba[:, 3], -1.0, alog.unsqueeze(1).broadcast_to([P, NT, H]),
                                         ALU.mult, ALU.mult).then_inc(s["ba_step"], 1)

            def cumulated():
                dve.wait_ge(s["cg_mm"], 1)
                cg = A2[:, :NT * H].rearrange("p (t h) -> p t h", t=NT)
                gl = A2[:, NT * H:2 * NT * H].rearrange("p (t h) -> p t h", t=NT)
                dve.tensor_copy(ba[:, 1], cg).then_inc(s["ba_step"], 1)
                dve.tensor_copy(ba[:, 2], gl).then_inc(s["ba_step"], 1)
                dve.wait_ge(s["ba_step"], 13)
                dve.tensor_tensor(ba[:, 3], ba[:, 2], ba[:, 1], ALU.subtract).then_inc(s["ba_step"], 1)

            def head_columns():
                dve.wait_ge(s["ba_step"], 17)
                dve.tensor_tensor(ba[:, 4], ba[:, 4], ba[:, 0], ALU.mult).then_inc(s["ba_step"], 1)
                dve.wait_ge(s["ba_step"], 18)
                for kind, b in ((HC_G, 5), (HC_CG, 1), (HC_B, 0), (HC_KD, 3), (HC_GL, 2)):
                    dve.tensor_copy(hc[:, :, kind, :], ba[:, b].rearrange("p t h -> p h t")).then_inc(s["hc_set"], 1)
                for kind, b in ((HC_NB, 0), (HC_NBE, 4)):
                    dve.tensor_scalar(hc[:, :, kind, :], ba[:, b].rearrange("p t h -> p h t"), -1.0, None, ALU.mult)\
                        .then_inc(s["hc_set"], 1)
                dve.wait_ge(s["hc_set"], NHC)

            head(0, None)
            with dve.Fori(1, H) as i:
                head(i, i - 1)

            def gate_evac(n, slot, u, which):
                dve.wait_ge(s["win_done"], n + 1)
                dve.tensor_scalar(sg[:, u, which, :], PJ[slot][:], LEAST, None, ALU.max).then_inc(s["g_evac"], 1)

            def act_split(c, src, dst, count=4):
                dve.wait_ge(s["act_hi"], c + 1)
                dve.tensor_tensor(dst.rearrange("p k t -> p (k t)"), act_raw[:, c % 2, :count * T],
                                  src.rearrange("p k t -> p (k t)").bitcast(F32), ALU.subtract)\
                    .then_inc(s["act_lo"], 1)

            def merge(n, u, j):
                dve.wait_ge(s["win_done"], n + 1)
                dve.wait_ge(s["g_sig"], 6 * j + 6)
                a, b = ((G0, G1), (A0, A1))[u]
                dve.tensor_tensor(sg[:, u, 0, :], a[:], sg[:, u, 0, :], ALU.mult).then_inc(s["ya"], 1)
                dve.tensor_tensor(sg[:, u, 1, :], b[:], sg[:, u, 1, :], ALU.mult).then_inc(s["yb"], 1)
                dve.wait_ge(s["ya"], j + 1)
                dve.wait_ge(s["yb"], j + 1)
                dve.tensor_tensor(mgt[:, u, :], sg[:, u, 0, :], sg[:, u, 1, :], ALU.add).then_inc(s["mg"], 1)

            last = H - 1
            split(N1 + 1, 1)
            softmax_max(last, 0)
            zclamp(last, 1)
            softmax_max(last, 1)
            softmax_norm(last, 0)
            zmul(last, 1)
            softmax_max(last, 2)
            softmax_norm(last, 1)
            softmax_max(last, 3)
            softmax_norm(last, 2)
            softmax_norm(last, 3)
            gate_evac(N1, 0, 0, 0)
            split(N1 + 2, 0)
            act_split(0, o_split[:, 0, 0], o_split[:, 0, 1])
            attn_out(last)
            act_split(1, o_split[:, 1, 0], o_split[:, 1, 1])
            gate_evac(N1 + 1, 1, 0, 1)
            split(N1 + 3, 1)
            act_split(2, o_split[:, 2, 0], o_split[:, 2, 1])
            act_split(3, o_split[:, 3, 0], o_split[:, 3, 1])
            gate_evac(N1 + 2, 0, 1, 0)
            split(N2, 0)
            with dve.Fori(0, (KT - 2) // 2) as jj:
                j = jj * 2
                for u in range(2):
                    n = j * 3 + (N2 + 3 * u)
                    gate_evac(n - 1, (u + 1) % 2, (u + 1) % 2, 1)
                    split(n + 1, (u + 1) % 2)
                    split(n + 2, u)
                    merge(n, u, j + u)
                    split(n + 3, (u + 1) % 2)
                    dve.wait_ge(s["mg"], j + (u + 1))
                    gate_evac(n + 1, (u + 1) % 2, u, 0)
                dve.wait_ge(s["mg_out"], 16 * (j + 2))
            gate_evac(N3 - 3, 1, 1, 1)
            split(N3 - 1, 1)
            def last_lo(u):
                dve.wait_ge(s["last_hi"], u + 1)
                dve.tensor_tensor(h_lo[:, KT - 2 + u, :], mgt[:, u, :], h_hi[:, KT - 2 + u, :].bitcast(F32),
                                  ALU.subtract).then_inc(s["last_lo"], 1)

            act_split(OCH, h_hi[:, 0:4], h_lo[:, 0:4])
            act_split(OCH + 1, h_hi[:, 4:8], h_lo[:, 4:8])
            merge(N3 - 2, 0, KT - 2)
            split(N3, 0)
            last_lo(0)
            act_split(OCH + 2, h_hi[:, 8:12], h_lo[:, 8:12])
            act_split(OCH + 3, h_hi[:, 12:14], h_lo[:, 12:14], 2)
            merge(N3 - 1, 1, KT - 1)
            split(N3 + 1, 1)
            last_lo(1)

            def residual(eb):
                dve.wait_ge(s["x3_loaded"], 16 * (eb + 1))
                dve.wait_ge(s["out_stored"], 16 * NT * eb)
                for t in range(NT):
                    if t < NT - 1:
                        dve.wait_ge(s["p3_done"], eb * (NT - 1) + (t + 1))
                    else:
                        dve.wait_ge(s["win_done"], eb * 4 + (N3 + 4))
                    dve.tensor_tensor(y3[:, t, :], bank[4 * (eb % 2) + t][:], x3[:, t, :], ALU.add).then_inc(s["resid"], 1)

            for eb in range(D // 512):
                for k in range(4 * eb + 2, min(4 * eb + 6, 16)):
                    split(N3 + k, k % 2)
                residual(eb)


_INS = ["x", "norm_w", "w_in", "gdn_conv_w", "gdn_a_log", "gdn_dt_bias", "gdn_norm_w", "moba_q_norm_w",
        "moba_k_norm_w", "w_out_gdn", "w_out_moba", "w_o"]


def shape_constants():
    r, c = np.arange(P)[:, None], np.arange(P)[None, :]
    cst = np.zeros((P, NCONST, P), np.float32)
    cst[:, C_ID] = r == c
    cst[:, C_TRIU] = r <= c
    cst[:, C_DMASK] = np.where(r <= c, 0.0, NEG)
    cst[:, C_CMASK] = np.where(c <= r, 0.0, NEG)
    cst[:, C_STRICT] = r < c
    cst[:, C_M16] = r // 16 == c // 16
    for col, b in ((C_L32, 16), (C_L64, 32)):
        cst[:, col] = (r // b == c // b + 1) & (r // (2 * b) == c // (2 * b))
    freq = np.float32(10000.0) ** (-np.arange(0, P, 2, dtype=np.float32) / np.float32(P))
    ang = np.arange(T, dtype=np.float32)[None, :] * freq.astype(np.float32)[:, None]
    rope = np.empty((P, 2, T), np.float32)
    rope[:P // 2, 0] = rope[P // 2:, 0] = np.cos(ang)
    rope[:P // 2, 1] = np.sin(ang)
    rope[P // 2:, 1] = -np.sin(ang)
    return cst, rope


def kernel(**inputs):
    import concourse.bacc as _bacc
    from concourse.bass_utils import run_bass_kernel_spmd as _run

    nc = _bacc.Bacc("TRN2", target_bir_lowering=False, num_devices=1)
    arrays, args = {}, []
    for name in _INS:
        arrays[f"in_{name}_dram"] = np.ascontiguousarray(inputs[name])
    arrays["const_masks"], arrays["const_rope"] = shape_constants()
    for name, a in arrays.items():
        args.append(nc.dram_tensor(name, a.shape, mybir.dt.from_np(a.dtype), kind="ExternalInput").ap())
    args.append(nc.dram_tensor("out_0_dram", (1, T, D), F32, kind="ExternalOutput").ap())
    hybrid_layer(nc, *args)
    r = _run(nc, [arrays], core_ids=[0])
    return r.results[0]["out_0_dram"]
```

```python
from contextlib import ExitStack

import numpy as np

import concourse.bass as bass
from concourse import mybir

F32 = mybir.dt.float32
F32R = mybir.dt.float32r
ALU = mybir.AluOpType
ACT = mybir.ActivationFunctionType
AX_X = mybir.AxisListType.X

P = 128
D = 2048
T = 512
NT = T // P
KT = D // P
H = 8
W = H * P
EPS = 1e-6
NEG = -1e30
LEAST = -43.0
COL_GDN = 0
COL_BETA = 4 * W
COL_MOBA = COL_BETA + 2 * H
COL_GATE = COL_MOBA + 4 * W
IN_COLS = COL_GATE + 2 * D
SCALE = float(P) ** -0.5
LNSCALE = float(np.log(SCALE))

STRIPES = (("gk", COL_GDN + W), ("gq", COL_GDN), ("gv", COL_GDN + 2 * W), ("gz", COL_GDN + 3 * W),
           ("bk", COL_MOBA + W), ("bq", COL_MOBA), ("bv", COL_MOBA + 2 * W), ("bz", COL_MOBA + 3 * W))
NW = len(STRIPES)
N1 = NW * H
N2 = N1 + 4
N3 = N2 + 3 * KT - 4
BA_G = 11
X_SPLIT = 3 * D // 4
OCH = 2 * H * T // D
MCH = KT * T // D

(C_ID, C_TRIU, C_DMASK, C_CMASK, C_STRICT, C_M16, C_L32, C_L64) = range(8)
NCONST = 8
(HC_G, HC_CG, HC_B, HC_NB, HC_NBE, HC_KD, HC_GL) = range(7)
NHC = 7
RING = 4
R_CONV, R_GW, R_QW, R_KW = 0, 96, 97, 98

SEMS = """
 ident_loaded consts rope_loaded nw_loaded rows_loaded rows_set rows_T rows_ready
 x_loaded0 x_loaded1 x_loaded2 x_loaded3 x_sq x_ln x_rstd x_rs x_scaled_a x_scaled_b
 x_T x_hi x_lo w16_loaded w16_hi w16_lo ba_mm ba_copied ba_T ab_sum ba_step cg_mm hc_set ones_set pads
 raw_loaded0 raw_loaded1 raw_loaded2 raw_loaded3 y_loaded0 y_loaded1
 hi_ready lo_ready win_done win_evac
 hcol cgrow_mm cg_arg cg_eg cg_dt cg_dts
 conv clampd sig silu sqd sq_hi sq_lo ss_mm rn_ln rn norm
 kT_mm kdec kk_mm kkd qk_mm qkd qdec UT_mm Ln LT_mm Ud Ld X1 L32m L64m
 n1_mm L2 U2 n2_mm X2 L4 U4 n3_mm X4 L8 n4_mm X8 ma_mm Y XT mb_mm X
 vT_mm vb ks_mm vbk vn_mm vn st_mm st o_mm o_sq o_hi o_lo o_ss o_ln o_rn o_1 o_2 o_out
 zclamp zsig zs
 b_sq b_hi b_lo b_ss b_ln b_rn b_n b_cos b_sinlo b_sinhi b_rope bvT_mm bvT
 s_mm s_mask s_max s_nmax s_exp s_rec s_norm pT_mm pT pv_mm ob ob_out
 g_evac g_sig ya yb mg mg_out
 act_loaded0 act_loaded1 act_hi act_lo last_hi last_lo
 p3_done resid x3_loaded out_stored
""".split()


def hybrid_layer(nc, x, norm_w, w_in, gdn_conv_w, gdn_a_log, gdn_dt_bias, gdn_norm_w, moba_q_norm_w,
                 moba_k_norm_w, w_out_gdn, w_out_moba, w_o, consts, rope, out):
    xs = x[0]
    outs = out[0]
    w_in3 = w_in[0].rearrange("(k p) c -> p k c", p=P)
    wg3 = w_out_gdn[0].rearrange("(k p) c -> p k c", p=P)
    wm3 = w_out_moba[0].rearrange("(k p) c -> p k c", p=P)
    wo3 = w_o[0].rearrange("(k p) c -> p k c", p=P)
    o_dram = nc.dram_tensor("branch_outputs", (2 * H, P, T), F32, kind="Internal").ap()
    m_dram = nc.dram_tensor("merged", (KT, P, T), F32, kind="Internal").ap()

    ctx = ExitStack()
    with ctx:
        def sb(name, shape, dt=F32, at=ctx):
            return at.enter_context(nc.sbuf_tensor(name, shape, dt))

        s = {n: ctx.enter_context(nc.semaphore(n)) for n in SEMS}
        bank = [ctx.enter_context(nc.psum_tensor(f"bank{i}", [P, 512], F32)) for i in range(8)]
        PJ = bank[0:2]
        G0, G1, G2 = bank[2:5]
        A0, A1, A2 = bank[5:8]

        h_hi = sb("h_hi", [P, KT, T], F32R)
        h_lo = sb("h_lo", [P, KT, T], F32R)
        def sb_both(name, shape, at):
            rounded = ExitStack()
            r = sb(name + "_r", shape, F32R, at=rounded)
            rounded.close()
            return sb(name, shape, at=at), r

        raw, w_lo = zip(*[sb_both(f"w_raw{i}", [P, D], ctx) for i in range(RING)])
        w_hi = [sb(f"w_hi{i}", [P, D], F32R) for i in range(2)]
        ones_f = sb("ones_f", [P, P])
        ones = sb("ones", [P, P], F32R)
        mean = sb("mean", [P, P], F32R)
        chan = sb("chan", [P, P])
        hc = sb("hc", [P, H, NHC, NT])
        eps = sb("eps", [P, 1])
        lnscale = sb("lnscale", [P, 1])
        sg = sb("sg", [P, 2, 2, T])
        mgt = sb("mgt", [P, 2, T])
        baT = sg[:4 * H, 0, 0, :]
        ab = mgt[:, 1, P:P + NT * 2 * H].rearrange("p (t c) -> p t c", t=NT)
        ba = mgt[:, 0, :6 * NT * H].rearrange("p (b t h) -> p b t h", b=6, t=NT)
        alog, dtb = mgt[:, 1, 0:H], mgt[:, 1, H:2 * H]
        ssx, rsx = mgt[:, 1, 2 * H:2 * H + NT], mgt[:, 1, 2 * H + NT:2 * H + 2 * NT]

        area = ExitStack()
        tmp = ExitStack()
        w16 = sb("w16", [P, KT, 2 * H], at=tmp)
        w16s = sb("w16_split", [P, KT, 2, 2 * H], F32R, at=tmp)
        rows = sb("rows", [P, P], at=tmp)
        xt = sb("x_tiles", [P, NT, D], at=tmp)
        nw = sb("norm_w_rows", [P, D], at=tmp)
        xsq = sb("x_square", [P, D], at=tmp)
        tmp.close()

        rawc, rawc_r = {}, {}
        for k in ("gk", "gq", "gv"):
            rawc[k], rawc_r[k] = sb_both(f"raw_{k}", [P, T + 4], area)
        cv = {k: sb(f"conv_{k}", [P, T], at=area) for k in ("gk", "gq", "gv")}
        dT = sb("decayT", [P, T], at=area)
        w0_ = sb("work0", [P, T], at=area)
        w1_, w1_r = sb_both("work1", [P, T], area)
        w2_, w3_, w4_ = [sb(f"work{i}", [P, T], at=area) for i in range(2, 5)]
        xa = sb("inv_a", [P, T], at=area)
        xb = sb("inv_b", [P, T], at=area)
        lm = [sb(f"lower{i}", [P, T], at=area) for i in range(3)]
        onorm, onorm_r = sb_both("out_norm", [P, T], area)
        kdec = sb("k_decay", [P, T], at=area)
        vb = sb("v_beta", [P, T], at=area)
        qdec = sb("q_decay", [P, T], at=area)
        qkT = sb("qkT", [P, T], at=area)
        st = [sb(f"state{i}", [P, P], at=area) for i in range(2)]
        zA = sb("zA", [P, T], at=area)
        hcol = sb("hcol", [P, NHC, NT], at=area)
        cossin = sb("cossin", [P, 2, T], at=area)
        zB = sb("zB", [P, T], at=area)
        zt = sb("z_tmp", [P, T], at=area)
        pt, pt_r = sb_both("pt", [P, 4, T], area)
        bv = sb("bv", [P, T], at=area)
        pr1 = sb("probs1", [P, T], at=area)
        kr = sb("k_rope", [P, T], at=area)
        qr = sb("q_rope", [P, T], at=area)
        vT = sb("vT", [P, T], at=area)
        stat = sb("softmax_stats", [P, 4, NT], at=area)
        cst = sb("cst", [P, NCONST, P], at=area)
        area.close()

        late = ExitStack()
        act_raw = sb("act_raw", [P, 2, D], at=ctx)
        o_split = sb("o_split", [P, OCH, 2, 4, T], F32R, at=late)
        late.close()
        x3 = sb("x_residual", [P, NT, 512], at=ctx)
        y3 = sb("out_tiles", [P, NT, 512], at=ctx)

        def o_hi(o):
            return o_split[:, o // 4, 0, o % 4, :]

        def o_lo(o):
            return o_split[:, o // 4, 1, o % 4, :]

        ident, triu = cst[:, C_ID, :], cst[:, C_TRIU, :]
        cos, sin = cossin[:, 0, :], cossin[:, 1, :]
        Eg, L2, Yt = w2_, w2_, w2_
        dTs, L4 = w0_, w0_
        Up, U2, XTt = w1_, w1_, w1_
        Ud, U4, vn = w3_, w3_, w3_
        Ld, L8, o1 = w4_, w4_, w4_
        Ln = lm[0]
        probs = [bv, pr1]
        dest = {"gk": rawc["gk"][:, 4:], "gq": rawc["gq"][:, 4:], "gv": rawc["gv"][:, 4:], "gz": zA[:],
                "bk": pt[:, 0, :], "bq": pt[:, 1, :], "bv": bv[:], "bz": zB[:]}

        def tile4(t):
            return slice(t * P, (t + 1) * P)

        def tile4h(t):
            return slice(t * P, t * P + P // 2), slice(t * P + P // 2, (t + 1) * P)

        def corner(ap, half):
            return q4(ap)[:P // 2, :, half * P // 2:(half + 1) * P // 2]

        def q4(ap):
            return ap[:].rearrange("p (t c) -> p t c", t=NT)

        def over(ap):
            return ap.unsqueeze(1).broadcast_to([P, NT, P])

        def hcb(kind):
            return hcol[:, kind, :].unsqueeze(2).broadcast_to([P, NT, P])

        block = ctx.enter_context(nc.Block())

        @block.sync
        def _(sp):
            x_loaded = (s["x_loaded0"], s["x_loaded1"], s["x_loaded2"], s["x_loaded3"])

            def load_x(t):
                sp.dma_start(xt[:, t, :], xs[t * P:(t + 1) * P, :]).then_inc(x_loaded[t], 16)

            load_x(0)
            sp.dma_start(nw[:], norm_w.broadcast_to([P, D])).then_inc(s["nw_loaded"], 16)
            sp.dma_start(cst[:, C_ID, :], consts[:, C_ID, :]).then_inc(s["ident_loaded"], 16)
            load_x(1)
            load_x(2)
            sp.dma_start(w16[:], w_in3[:, :, COL_BETA:COL_BETA + 2 * H]).then_inc(s["w16_loaded"], 16)
            load_x(3)

            loaded = (s["raw_loaded0"], s["raw_loaded1"], s["raw_loaded2"], s["raw_loaded3"])
            y_loaded = (s["y_loaded0"], s["y_loaded1"])

            def slot_free(n):
                sp.wait_ge(s["win_done"], n - RING + 1)

            def load(n, slot, src):
                sp.dma_start(raw[slot][:].rearrange("p (k c) -> p k c", k=src.shape[1]), src)\
                    .then_inc(loaded[slot], 16)

            def head_loads(i):
                for w, (_, col) in enumerate(STRIPES):
                    if w == 0:
                        slot_free(i * NW + 1)
                    elif w > 1:
                        slot_free(i * NW + w)
                    load(i * NW + w, w % RING, w_in3[:, :, bass.ds(i * P + col, P)])

            load(0, 0, w_in3[:, :, STRIPES[0][1]:STRIPES[0][1] + P])
            sp.wait_ge(s["rows_set"], 1)
            for row, src in ((R_CONV, gdn_conv_w[0].rearrange("j (c p) -> (j c) p", p=P)),
                             (R_GW, gdn_norm_w), (R_QW, moba_q_norm_w), (R_KW, moba_k_norm_w)):
                sp.dma_start(rows[row:row + src.shape[0], :], src).then_inc(s["rows_loaded"], 16)
            sp.dma_start(alog, gdn_a_log.broadcast_to([P, H])).then_inc(s["rows_loaded"], 16)
            sp.dma_start(dtb, gdn_dt_bias.broadcast_to([P, H])).then_inc(s["rows_loaded"], 16)
            load(1, 1, w_in3[:, :, STRIPES[1][1]:STRIPES[1][1] + P])
            sp.dma_start(cst[:, C_ID + 1:, :], consts[:, C_ID + 1:, :]).then_inc(s["consts"], 16)
            for w in range(2, RING):
                load(w, w, w_in3[:, :, STRIPES[w][1]:STRIPES[w][1] + P])
            sp.wait_ge(s["x_T"], 4 * NT)
            sp.dma_start(cossin[:], rope).then_inc(s["rope_loaded"], 16)
            for w in range(RING, NW):
                slot_free(w)
                load(w, w % RING, w_in3[:, :, STRIPES[w][1]:STRIPES[w][1] + P])
            with sp.Fori(1, H) as i:
                head_loads(i)

            def gate_load(n, slot, j, which):
                load(n, slot, w_in3[:, :, bass.ds(j * P + (COL_GATE + which * D), P)])

            def y_load(n, slot, j, u):
                half = raw[slot][:].rearrange("p (b k c) -> p b k c", b=2, k=H)
                sp.dma_start(half[:, 0], wg3[:, :, bass.ds(j * P, P)]).then_inc(loaded[slot], 16)
                sp.dma_start(half[:, 1], wm3[:, :, bass.ds(j * P, P)])\
                    .then_inc(y_loaded[u % 2], 16)

            for c in range(4):
                slot_free(N1 + c)
                gate_load(N1 + c, c % RING, c // 2, c % 2)
            slot_free(N2)

            def tile_loads(jj, u):
                n, j = jj * 12 + (N2 + 3 * u), jj * 4 + u
                y_load(n, 3 * u % RING, j, u)
                slot_free(n + 1)
                gate_load(n + 1, (3 * u + 1) % RING, j + 2, 0)
                slot_free(n + 3)
                gate_load(n + 2, (3 * u + 2) % RING, j + 2, 1)

            with sp.Fori(0, (KT - 2) // 4) as jj:
                for u in range(4):
                    tile_loads(jj, u)
            for u in range((KT - 2) % 4):
                tile_loads((KT - 2) // 4, u)
            for u in range(2):
                slot_free(N3 - 2 + u)
                y_load(N3 - 2 + u, (N3 - 2 + u) % RING, KT - 2 + u, u)

            def wo_load(n, slot, eb, kc):
                slot_free(n)
                load(n, slot, wo3[:, 4 * kc:4 * kc + 4, bass.ds(eb * 512, 512)])

            with sp.Fori(0, D // 512) as eb:
                for kc in range(4):
                    wo_load(eb * 4 + (N3 + kc), kc % RING, eb, kc)
                    if kc == 1:
                        sp.wait_ge(s["win_done"], N3)
                        sp.wait_ge(s["resid"], eb * NT + (NT + 1))
                        sp.dma_start(x3[:], xs.rearrange("(t p) d -> p t d", p=P)[:, :, bass.ds(eb * 512, 512)])\
                            .then_inc(s["x3_loaded"], 16)

        @block.gpsimd
        def _(pool):
            pool.memset(rows[:], 0.0).then_inc(s["rows_set"], 1)
            for tile, value in ((ones_f, 1.0), (eps, EPS), (lnscale, LNSCALE)):
                pool.memset(tile[:], value).then_inc(s["ones_set"], 1)
            pool.wait_ge(s["nw_loaded"], 16)
            for t in range(NT):
                part = xt[:, t, X_SPLIT:]
                pool.wait_ge(s["x_rstd"], t + 1)
                pool.tensor_scalar(part, part, rsx[:, t:t + 1], None, ALU.mult).then_inc(s["x_rs"], 1)
                pool.wait_ge(s["x_rs"], t + 1)
                pool.tensor_tensor(part, part, nw[:, X_SPLIT:], ALU.mult).then_inc(s["x_scaled_b"], 1)
            pool.wait_ge(s["ba_mm"], 1)
            for k in ("gk", "gq", "gv"):
                pool.memset(rawc[k][:, 0:4], 0.0).then_inc(s["pads"], 1)

            def head(h, p):
                pool.wait_ge(s["cg_dt"], h + 1)
                pool.wait_ge(s["n3_mm"], h)
                pool.tensor_tensor(q4(dTs), q4(dT), over(cst[:, C_STRICT, :]), ALU.mult).then_inc(s["cg_dts"], 1)
                if p is not None:
                    pool.wait_ge(s["ob"], h)
                    pool.dma_start(o_dram[bass.ds(p + H, 1)].rearrange("o p t -> p (o t)"), pr1[:])\
                        .then_inc(s["ob_out"], 16)
                pool.wait_ge(s["Ln"], h + 1)
                pool.wait_ge(s["ma_mm"], 3 * h)
                pool.tensor_tensor(q4(lm[1]), q4(Ln), over(cst[:, C_L32, :]), ALU.mult).then_inc(s["L32m"], 1)
                pool.tensor_tensor(q4(lm[2]), q4(Ln), over(cst[:, C_L64, :]), ALU.mult).then_inc(s["L64m"], 1)
                pool.wait_ge(s["rope_loaded"], 16)
                for c, r in ((0, kr), (1, qr)):
                    pool.wait_ge(s["b_n"], 2 * h + c + 1)
                    pool.wait_ge(s["s_mm"], 4 * h)
                    pool.tensor_tensor(r[:], pt[:, c, :], cos, ALU.mult).then_inc(s["b_cos"], 1)
                pool.wait_ge(s["o_2"], h + 1)
                pool.dma_start(o_dram[bass.ds(h, 1)].rearrange("o p t -> p (o t)"), o1[:]).then_inc(s["o_out"], 16)

            head(0, None)
            with pool.Fori(1, H) as i:
                head(i, i - 1)

            act_loaded = (s["act_loaded0"], s["act_loaded1"])

            def act_load(c, dram, first, count=4):
                if c >= 2:
                    pool.wait_ge(s["act_lo"], c - 1)
                pool.dma_start(act_raw[:, c % 2, :count * T].rearrange("p (k t) -> p k t", t=T),
                               dram[first:first + count].rearrange("k p t -> p k t"))\
                    .then_inc(act_loaded[c % 2], 16)

            pool.wait_ge(s["o_out"], 16 * H)
            for c in range(2):
                act_load(c, o_dram, 4 * c)
            pool.wait_ge(s["ob"], H)
            pool.dma_start(o_dram[2 * H - 1], pr1[:]).then_inc(s["ob_out"], 16)
            pool.wait_ge(s["ob_out"], 16 * H)
            for c in range(2, OCH):
                act_load(c, o_dram, 4 * c)

            def store_merged(j, u, wait):
                pool.wait_ge(s["mg"], wait)
                pool.dma_start(m_dram[bass.ds(j, 1)].rearrange("o p t -> p (o t)"), mgt[:, u, :])\
                    .then_inc(s["mg_out"], 16)

            with pool.Fori(0, (KT - 2) // 2) as jj:
                j = jj * 2
                for u in range(2):
                    store_merged(j + u, u, j + (u + 1))
            pool.wait_ge(s["mg_out"], 16 * (KT - 2))
            for c in range(MCH):
                act_load(OCH + c, m_dram, 4 * c, 4 if c < MCH - 1 else 2)

            with pool.Fori(0, D // 512) as eb:
                for t in range(NT):
                    pool.wait_ge(s["resid"], eb * NT + (NT + t + 2))
                    pool.dma_start(outs[t * P:(t + 1) * P, bass.ds(eb * 512, 512)], y3[:, t, :])\
                        .then_inc(s["out_stored"], 16)
            pool.wait_ge(s["out_stored"], 16 * NT * (D // 512))

        @block.tensor
        def _(pe):
            def products(slot, k0, k1):
                for k in range(k0, k1):
                    c = slice(k * P, (k + 1) * P)
                    pe.matmul(PJ[slot % 2][:], w_hi[slot % 2][:, c], h_hi[:, k, :], start=(k == 0), stop=False,
                              skip_group_check=True)
                    pe.matmul(PJ[slot % 2][:], w_hi[slot % 2][:, c], h_lo[:, k, :], start=False, stop=False,
                              skip_group_check=True)
                    mm = pe.matmul(PJ[slot % 2][:], w_lo[slot][:, c], h_hi[:, k, :], start=False, stop=(k == KT - 1),
                                   skip_group_check=True)
                if k1 == KT:
                    mm.then_inc(s["win_done"], 1)

            def products_half(slot, half):
                tok = slice(half * T // 2, (half + 1) * T // 2)
                for k in range(KT):
                    c = slice(k * P, (k + 1) * P)
                    pe.matmul(PJ[slot % 2][:, tok], w_hi[slot % 2][:, c], h_hi[:, k, tok], start=(k == 0), stop=False)
                    pe.matmul(PJ[slot % 2][:, tok], w_hi[slot % 2][:, c], h_lo[:, k, tok], start=False, stop=False)
                    mm = pe.matmul(PJ[slot % 2][:, tok], w_lo[slot][:, c], h_hi[:, k, tok], start=False,
                                   stop=(k == KT - 1))
                return mm

            def window(n, slot, k0, k1):
                if k0 == 0:
                    pe.wait_ge(s["lo_ready"], n + 1)
                    if not (isinstance(n, int) and n < 2):
                        pe.wait_ge(s["win_evac"], n - 1)
                products(slot, k0, k1)

            def four(ps, lhsT, rhs):
                for t in range(NT):
                    mm = pe.matmul(ps[:, tile4(t)], lhsT[:, tile4(t)], rhs[:, tile4(t)], start=True, stop=True)
                return mm

            def turn(ps, src):
                for t in range(NT):
                    mm = pe.transpose(ps[:, tile4(t)], src[:, tile4(t)], ident)
                return mm

            def cgrow(h):
                pe.wait_ge(s["hcol"], h + 1)
                pe.wait_ge(s["st"], 3 * h)
                for t in range(NT):
                    mm = pe.matmul(G2[:, tile4(t)], hcol[:, HC_G, t:t + 1].broadcast_to([P, P]), triu,
                                   start=True, stop=True)
                mm.then_inc(s["cgrow_mm"], 1)

            def channel_sum(ps, factor, hi, lo):
                pe.matmul(ps[:], factor[:], hi, start=True, stop=False)
                return pe.matmul(ps[:], factor[:], lo, start=False, stop=True)

            def ss(h, c):
                pe.wait_ge(s["sq_lo"], 2 * h + c + 1)
                pe.wait_ge((s["o_1"], s["o_ln"])[c], h)
                channel_sum((G0, G1)[c], ones, onorm_r[:], rawc_r[("gk", "gq")[c]][:, 4:]).then_inc(s["ss_mm"], 1)

            def kT(h):
                pe.wait_ge(s["norm"], 2 * h + 1)
                turn(G0, cv["gk"]).then_inc(s["kT_mm"], 1)

            def kk(h):
                pe.wait_ge(s["cg_eg"], h + 1)
                four(G2, cv["gk"], cv["gk"]).then_inc(s["kk_mm"], 1)

            def qk(h):
                pe.wait_ge(s["norm"], 2 * h + 2)
                four(G1, cv["gk"], cv["gq"]).then_inc(s["qk_mm"], 1)

            def UT(h):
                pe.wait_ge(s["kkd"], h + 1)
                pe.wait_ge(s["kdec"], h + 1)
                turn(G0, Up).then_inc(s["UT_mm"], 1)

            def LT(h):
                pe.wait_ge(s["Ln"], h + 1)
                turn(G2, Ln).then_inc(s["LT_mm"], 1)

            def n1(h):
                pe.wait_ge(s["Ud"], h + 1)
                pe.wait_ge(s["Ld"], h + 1)
                pe.wait_ge(s["qkd"], h + 1)
                four(G0, Ud, Ld)
                four(G1, Ld, Ud).then_inc(s["n1_mm"], 1)

            def n2(h):
                pe.wait_ge(s["L2"], h + 1)
                pe.wait_ge(s["U2"], h + 1)
                pe.wait_ge(s["X1"], h + 1)
                four(G0, U2, L2)
                four(G1, L2, U2)
                four(G2, L2, xa).then_inc(s["n2_mm"], 1)

            def n3(h):
                pe.wait_ge(s["X2"], h + 1)
                pe.wait_ge(s["L4"], h + 1)
                pe.wait_ge(s["U4"], h + 1)
                four(G0, U4, L4)
                four(G2, L4, xb).then_inc(s["n3_mm"], 1)

            def n4(h):
                pe.wait_ge(s["X4"], h + 1)
                pe.wait_ge(s["L8"], h + 1)
                four(G2, L8, xa).then_inc(s["n4_mm"], 1)

            def vTs(h):
                pe.wait_ge(s["silu"], 3 * h + 3)
                pe.wait_ge(s["U4"], h + 1)
                turn(G1, cv["gv"]).then_inc(s["vT_mm"], 1)

            def ma(h, k):
                src = (xb, xa, xb)[k]
                if k == 0:
                    pe.wait_ge(s["X8"], h + 1)
                    pe.wait_ge(s["L8"], h + 1)
                    pe.wait_ge(s["vb"], h + 1)
                elif k == 1:
                    pe.wait_ge(s["X"], 3 * h + k)
                if k < 2:
                    pe.wait_ge((s["L32m"], s["L64m"])[k], h + 1)
                    four(G0, lm[k + 1], src)
                    mm = turn(G1, src)
                else:
                    for t in range(NT):
                        a, b = tile4h(t)
                        pe.matmul(G0[:P // 2, b], Ln[P // 2:, a], src[P // 2:, b], start=True, stop=True)
                    for t in range(NT):
                        a, b = tile4h(t)
                        mm = pe.transpose(G1[:P // 2, a], src[:P // 2, a], ident[:P // 2, :P // 2])
                mm.then_inc(s["ma_mm"], 1)

            def mb(h, k):
                if k < 2:
                    pe.wait_ge(s["Y"], 3 * h + k + 1)
                    pe.wait_ge(s["XT"], 3 * h + k + 1)
                    mm = four(G2, XTt, Yt)
                else:
                    for t in range(NT):
                        a, b = tile4h(t)
                        mm = pe.matmul(G2[:P // 2, b], XTt[:P // 2, a], Yt[:P // 2, b], start=True, stop=True)
                mm.then_inc(s["mb_mm"], 1)

            def kS(h, t):
                pe.wait_ge(s["st"], 3 * h + t)
                pe.matmul(G1[:, :P], cv["gk"][:, tile4(t)], st[(t - 1) % 2][:], start=True, stop=True)\
                    .then_inc(s["ks_mm"], 1)

            def vnew(h, t):
                if t == 0:
                    pe.wait_ge(s["vb"], h + 1)
                    pe.wait_ge(s["X"], 3 * h + 3)
                else:
                    pe.wait_ge(s["vbk"], 3 * h + t)
                pe.matmul(G1[:, :P], xb[:, tile4(t)], vb[:, tile4(t)], start=True, stop=True).then_inc(s["vn_mm"], 1)

            def outs_(h, t):
                pe.wait_ge(s["vn"], 4 * h + t + 1)
                if t < NT - 1:
                    pe.wait_ge(s["kdec"], h + 1)
                    pe.matmul(G2[:, :P], kdec[:, tile4(t)], vn[:, tile4(t)], start=True, stop=True)\
                        .then_inc(s["st_mm"], 1)
                if t == 0:
                    pe.wait_ge(s["qkd"], h + 1)
                    pe.wait_ge(s["qdec"], h + 1)
                else:
                    pe.matmul(G0[:, tile4(t)], st[(t - 1) % 2][:], qdec[:, tile4(t)], start=True, stop=False)
                pe.matmul(G0[:, tile4(t)], vn[:, tile4(t)], qkT[:, tile4(t)], start=(t == 0), stop=True)\
                    .then_inc(s["o_mm"], 1)

            def gnorm(h):
                pe.wait_ge(s["o_lo"], h + 1)
                channel_sum(G1, mean, w1_r[:], onorm_r[:]).then_inc(s["o_ss"], 1)

            def b_ss(h, c):
                pe.wait_ge(s["b_lo"], 2 * h + c + 1)
                if c == 0:
                    pe.wait_ge(s["pT"], 4 * h)
                channel_sum(A2, mean, pt_r[:, 3, :], pt_r[:, 2, :]).then_inc(s["b_ss"], 1)

            def bvTs(h):
                pe.wait_ge(s["win_evac"], NW * h + 7)
                pe.wait_ge(s["b_ln"], 2 * h + 2)
                turn(A2, bv).then_inc(s["bvT_mm"], 1)

            def scores(h, t):
                pe.wait_ge(s["b_rope"], 2 * h + 2)
                if t >= 2:
                    pe.wait_ge(s["s_exp"], 4 * h + t - 1)
                n = (t + 1) * P
                pe.matmul((A0, A1)[t % 2][:, :n], qr[:, tile4(t)], kr[:, :n], start=True, stop=True)\
                    .then_inc(s["s_mm"], 1)

            def pTs(h, t):
                pe.wait_ge(s["s_norm"], 4 * h + t + 1)
                if t == 0:
                    pe.wait_ge(s["bvT"], h + 1)
                else:
                    pe.wait_ge(s["pT"], 4 * h + t)
                for k in range(t + 1):
                    mm = pe.transpose(A2[:, tile4(k)], probs[t % 2][:, tile4(k)], ident)
                mm.then_inc(s["pT_mm"], 1)

            def pv(h):
                pe.wait_ge(s["pT"], 4 * h + 4)
                for k in range(NT):
                    mm = pe.matmul(A0[:, k * P:], vT[:, tile4(k)], pt[:, k, k * P:],
                                   start=(k == 0), stop=(k == NT - 1))
                mm.then_inc(s["pv_mm"], 1)

            def head(h, p):
                def win(w, a, b):
                    window(h * NW + w, w % RING, a, b)
                if p is not None:
                    win(0, 0, 4)
                    cgrow(h)
                    scores(p, 0)
                    win(0, 4, 8)
                    scores(p, 1)
                    win(0, 8, 11)
                    pTs(p, 0)
                    scores(p, 2)
                    win(0, 11, 16)
                    pTs(p, 1)
                    scores(p, 3)
                    win(1, 0, 4)
                    pTs(p, 2)
                    win(1, 4, 8)
                    pTs(p, 3)
                    win(1, 8, 11)
                    pv(p)
                    win(1, 11, 16)
                else:
                    beta_alpha_T()
                    win(1, 0, 7)
                    cumulate()
                    win(1, 7, 16)
                    cgrow(h)
                win(2, 0, 3)
                ss(h, 0)
                win(2, 3, 9)
                kT(h)
                kk(h)
                win(2, 9, 12)
                UT(h)
                win(2, 12, 14)
                ss(h, 1)
                win(2, 14, 15)
                LT(h)
                win(2, 15, 16)
                win(3, 0, 1)
                qk(h)
                win(3, 1, 4)
                n1(h)
                win(3, 4, 7)
                n2(h)
                win(3, 7, 10)
                n3(h)
                win(3, 10, 13)
                n4(h)
                win(3, 13, 16)
                vTs(h)
                win(4, 0, 2)
                ma(h, 0)
                win(4, 2, 5)
                mb(h, 0)
                win(4, 5, 8)
                ma(h, 1)
                win(4, 8, 11)
                mb(h, 1)
                win(4, 11, 13)
                pe.wait_ge(s["X"], 3 * h + 2)
                win(4, 13, 14)
                ma(h, 2)
                win(4, 14, 16)
                pe.wait_ge(s["Y"], 3 * h + 3)
                pe.wait_ge(s["XT"], 3 * h + 3)
                win(5, 0, 1)
                mb(h, 2)
                win(5, 1, 4)
                vnew(h, 0)
                win(5, 4, 7)
                outs_(h, 0)
                b_ss(h, 0)
                win(5, 7, 9)
                kS(h, 1)
                win(5, 9, 11)
                vnew(h, 1)
                win(5, 11, 14)
                outs_(h, 1)
                win(5, 14, 16)
                kS(h, 2)
                win(6, 0, 2)
                vnew(h, 2)
                win(6, 2, 4)
                outs_(h, 2)
                win(6, 4, 7)
                kS(h, 3)
                win(6, 7, 10)
                vnew(h, 3)
                b_ss(h, 1)
                win(6, 10, 13)
                outs_(h, 3)
                win(6, 13, 16)
                win(7, 0, 1)
                gnorm(h)
                win(7, 1, 4)
                bvTs(h)
                win(7, 4, 16)

            def beta_alpha(half):
                tok = slice(half * T // 2, (half + 1) * T // 2)
                for k in range(KT):
                    wk = w16s[:, k, :, :].rearrange("p b c -> p (b c)")
                    pe.matmul(A1[:4 * H, tok], wk, h_hi[:, k, tok], start=(k == 0), stop=False)
                    mm = pe.matmul(A1[:4 * H, tok], wk, h_lo[:, k, tok], start=False, stop=(k == KT - 1))
                return mm

            def beta_alpha_T():
                pe.wait_ge(s["ba_copied"], 1)
                for t in range(NT):
                    mm = pe.transpose(A0[:, t * 4 * H:(t + 1) * 4 * H], baT[:, tile4(t)], ident[:4 * H, :4 * H])
                mm.then_inc(s["ba_T"], 1)

            def cumulate():
                pe.wait_ge(s["consts"], 16)
                pe.wait_ge(s["ba_step"], BA_G)
                g = mgt[:, 0, 5 * NT * H:6 * NT * H]
                pe.matmul(A2[:, :NT * H], triu, g, start=True, stop=True)
                pe.matmul(A2[:, NT * H:2 * NT * H], ones_f[:], g, start=True, stop=True).then_inc(s["cg_mm"], 1)

            pe.wait_ge(s["ident_loaded"], 16)
            xbank = (G0, G1, G2, A0)

            def x_turn(t):
                for q in range(4):
                    g = 4 * t + q
                    if q in (0, 3):
                        pe.wait_ge((s["x_scaled_a"], s["x_scaled_b"])[q // 3], t + 1)
                    if g >= 4:
                        pe.wait_ge(s["x_lo"], g - 3)
                    for k in range(4):
                        mm = pe.transpose(xbank[q][:, tile4(k)], xt[:, t, (4 * q + k) * P:(4 * q + k + 1) * P], ident)
                    mm.then_inc(s["x_T"], 1)

            x_turn(0)
            x_turn(1)
            x_turn(2)
            pe.wait_ge(s["rows_loaded"], 96)
            pe.transpose(A2[:, :P], rows[:], ident).then_inc(s["rows_T"], 1)
            pe.wait_ge(s["w16_lo"], 1)
            pe.wait_ge(s["x_lo"], 8)
            beta_alpha(0)
            x_turn(3)
            pe.wait_ge(s["lo_ready"], 1)
            products_half(0, 0)
            pe.wait_ge(s["x_lo"], 16)
            beta_alpha(1).then_inc(s["ba_mm"], 1)
            products_half(0, 1).then_inc(s["win_done"], 1)

            head(0, None)
            with pe.Fori(1, H) as i:
                head(i, i - 1)

            def gate(n, slot, a, b):
                if a == 0:
                    pe.wait_ge(s["lo_ready"], n + 1)
                products(slot, a, b)

            last = H - 1
            pe.wait_ge(s["win_evac"], N1 - 1)
            gate(N1, 0, 0, 4)
            scores(last, 0)
            gate(N1, 0, 4, 8)
            scores(last, 1)
            gate(N1, 0, 8, 11)
            pTs(last, 0)
            scores(last, 2)
            gate(N1, 0, 11, 16)
            pTs(last, 1)
            scores(last, 3)
            pe.wait_ge(s["win_evac"], N1)
            gate(N1 + 1, 1, 0, 4)
            pTs(last, 2)
            gate(N1 + 1, 1, 4, 8)
            pTs(last, 3)
            gate(N1 + 1, 1, 8, 11)
            pv(last)
            gate(N1 + 1, 1, 11, 16)
            for c in range(2):
                pe.wait_ge(s["g_evac"], c + 1)
                gate(N1 + 2 + c, 2 + c, 0, 16)

            ybank = ((G0, G1), (A0, A1))

            def y(n, slot, u):
                pe.wait_ge(s["lo_ready"], n + 1)
                for b in range(2):
                    pe.wait_ge(s["act_lo"], 2 * b + 2)
                    ps = ybank[u][b]
                    for k in range(H):
                        c = slice((b * H + k) * P, (b * H + k + 1) * P)
                        o = b * H + k
                        pe.matmul(ps[:], w_hi[slot % 2][:, c], o_hi(o), start=(k == 0), stop=False)
                        pe.matmul(ps[:], w_hi[slot % 2][:, c], o_lo(o), start=False, stop=False)
                        mm = pe.matmul(ps[:], w_lo[slot][:, c], o_hi(o), start=False, stop=(k == H - 1))
                mm.then_inc(s["win_done"], 1)

            def tile_windows(jj, u):
                n = jj * 12 + (N2 + 3 * u)
                y(n, 3 * u % RING, u % 2)
                pe.wait_ge(s["g_evac"], 8 * jj + (2 * u + 4))
                gate(n + 1, (3 * u + 1) % RING, 0, 16)
                gate(n + 2, (3 * u + 2) % RING, 0, 16)

            with pe.Fori(0, (KT - 2) // 4) as jj:
                for u in range(4):
                    tile_windows(jj, u)
            for u in range((KT - 2) % 4):
                tile_windows((KT - 2) // 4, u)
            for u in range(2):
                pe.wait_ge(s["yb"], KT - 2)
                y(N3 - 2 + u, (N3 - 2 + u) % RING, u)

            def p3(n, slot, kc, banks):
                pe.wait_ge(s["lo_ready"], n + 1)
                for t in range(NT):
                    for k in range(4):
                        kt = 4 * kc + k
                        c = slice(k * 512, (k + 1) * 512)
                        pe.matmul(banks[t][:], h_hi[:, kt, tile4(t)], w_hi[slot % 2][:, c],
                                  start=(kt == 0), stop=False)
                        pe.matmul(banks[t][:], h_hi[:, kt, tile4(t)], w_lo[slot][:, c], start=False, stop=False)
                        mm = pe.matmul(banks[t][:], h_lo[:, kt, tile4(t)], w_hi[slot % 2][:, c],
                                       start=False, stop=(kt == KT - 1))
                    if kc == 3 and t < NT - 1:
                        mm.then_inc(s["p3_done"], 1)
                mm.then_inc(s["win_done"], 1)

            with pe.Fori(0, D // 512, 2) as eb:
                for e in range(2):
                    pe.wait_ge(s["resid"], eb * NT + (1, NT + 1)[e])
                    pe.wait_ge(s["g_evac"], 2 * KT)
                    pe.wait_ge(s["yb"], (KT - 1, KT)[e])
                    for kc in range(4):
                        pe.wait_ge(s["act_lo"], OCH + kc + 1)
                        if kc == 3:
                            pe.wait_ge(s["last_lo"], 2)
                        p3(eb * 4 + (N3 + 4 * e + kc), kc % RING, kc, (bank[0:4], bank[4:8])[e])

        @block.scalar
        def _(act):
            loaded = (s["raw_loaded0"], s["raw_loaded1"], s["raw_loaded2"], s["raw_loaded3"])
            y_loaded = (s["y_loaded0"], s["y_loaded1"])
            act.preload_act_table_set("natural_log_exp_and_others")

            def split(n, slot, at, y=None):
                if not (isinstance(n, int) and n < 2):
                    act.wait_ge(s["win_done"], n - 1)
                act.wait_ge(loaded[slot], 16 * at)
                if y is not None:
                    act.wait_ge(y_loaded[y[0]], 16 * y[1])
                act.activation(w_hi[slot % 2][:], raw[slot][:], ACT.Copy).then_inc(s["hi_ready"], 1)

            def split_at(n, y=None):
                split(n, n % RING, n // RING + 1, y)

            def sigmoid(ap, sem, n):
                act.activation(ap, ap, ACT.Exp, scale=-1.0).then_inc(sem, 1)
                act.wait_ge(sem, n + 1)
                act.activation(ap, ap, ACT.Ln, bias=1.0).then_inc(sem, 1)
                act.wait_ge(sem, n + 2)
                act.activation(ap, ap, ACT.Exp, scale=-1.0).then_inc(sem, 1)

            def evac(h, w):
                name = STRIPES[w][0]
                act.wait_ge(s["win_done"], h * NW + w + 1)
                if not (isinstance(h, int) and h == 0):
                    if name in ("gk", "gq"):
                        act.wait_ge(s["norm"], 2 * h + w - 1)
                    elif name == "gv":
                        act.wait_ge(s["silu"], 3 * h)
                    elif name == "gz":
                        act.wait_ge(s["o_2"], h)
                    elif name == "bk":
                        act.wait_ge(s["pv_mm"], h)
                    elif name == "bv":
                        act.wait_ge(s["pT_mm"], 4 * h)
                act.activation(dest[name], PJ[w % 2][:], ACT.Copy).then_inc(s["win_evac"], 1)

            def cgrow(h):
                act.wait_ge(s["cg_arg"], 4 * h + 4)
                act.wait_ge(s["mb_mm"], 3 * h)
                act.activation(Eg[:], G2[:], ACT.Exp).then_inc(s["cg_eg"], 1)
                act.activation(dT[:], dT[:], ACT.Exp).then_inc(s["cg_dt"], 1)

            def silu(h, c):
                act.wait_ge(s["clampd"], 3 * h + c + 1)
                sigmoid(rawc[("gk", "gq", "gv")[c]][:, 4:], s["sig"], 9 * h + 3 * c)

            def sq(h, c):
                k = ("gk", "gq")[c]
                act.wait_ge(s["silu"], 3 * h + c + 1)
                act.activation(rawc[k][:, 4:], cv[k][:], ACT.Square).then_inc(s["sqd"], 1)
                if c == 0:
                    act.wait_ge(s["o_1"], h)
                else:
                    act.wait_ge(s["ss_mm"], 2 * h + 1)
                act.wait_ge(s["sqd"], 2 * h + c + 1)
                act.activation(onorm_r[:], rawc[k][:, 4:], ACT.Copy).then_inc(s["sq_hi"], 1)

            def rnorm(h, c):
                r = rawc[("gk", "gq")[c]][:, 4:]
                act.wait_ge(s["ss_mm"], 2 * h + c + 1)
                act.activation(r, (G0, G1)[c][:], ACT.Ln, bias=eps[:, 0:1]).then_inc(s["rn_ln"], 1)
                act.wait_ge(s["rn_ln"], 2 * h + c + 1)
                if c == 0:
                    act.activation(r, r, ACT.Exp, scale=-0.5).then_inc(s["rn"], 1)
                else:
                    act.activation(r, r, ACT.Exp, scale=-0.5, bias=lnscale[:, 0:1]).then_inc(s["rn"], 1)

            def n1(h):
                act.wait_ge(s["n1_mm"], h + 1)
                act.wait_ge(s["qdec"], h + 1)
                act.activation(L2[:], G0[:], ACT.Copy).then_inc(s["L2"], 1)

            def n2(h):
                act.wait_ge(s["n2_mm"], h + 1)
                act.activation(L4[:], G0[:], ACT.Copy).then_inc(s["L4"], 1)
                act.activation(U4[:], G1[:], ACT.Copy).then_inc(s["U4"], 1)

            def n3(h):
                act.wait_ge(s["n3_mm"], h + 1)
                act.activation(L8[:], G0[:], ACT.Copy).then_inc(s["L8"], 1)

            def ma(h, k):
                act.wait_ge(s["ma_mm"], 3 * h + k + 1)
                if k < 2:
                    act.activation(Yt[:], G0[:], ACT.Copy).then_inc(s["Y"], 1)
                else:
                    act.activation(corner(Yt, 1), corner(G0, 1), ACT.Copy).then_inc(s["Y"], 1)

            def vnew(h, t):
                act.wait_ge(s["vn_mm"], 4 * h + t + 1)
                act.activation(vn[:, tile4(t)], G1[:, :P], ACT.Copy).then_inc(s["vn"], 1)

            def gnorm_sq(h):
                act.wait_ge(s["o_mm"], 4 * h + 4)
                act.activation(onorm[:], G0[:], ACT.Square).then_inc(s["o_sq"], 1)
                act.wait_ge(s["o_sq"], h + 1)
                act.activation(w1_r[:], onorm[:], ACT.Copy).then_inc(s["o_hi"], 1)

            def gnorm(h):
                act.wait_ge(s["o_ss"], h + 1)
                act.activation(onorm[:], G1[:], ACT.Ln, bias=eps[:, 0:1]).then_inc(s["o_ln"], 1)
                act.wait_ge(s["o_ln"], h + 1)
                act.activation(onorm[:], onorm[:], ACT.Exp, scale=-0.5).then_inc(s["o_rn"], 1)

            def zsig(h, b):
                act.wait_ge(s["zclamp"], 2 * h + b + 1)
                sigmoid(zt[:], s["zsig"], 6 * h + 3 * b)

            def b_sq(h, c):
                act.wait_ge(s["win_evac"], NW * h + 5 + c)
                if c == 0:
                    act.wait_ge(s["pv_mm"], h)
                else:
                    act.wait_ge(s["b_n"], 2 * h + 1)
                act.activation(pt[:, 2, :], pt[:, c, :], ACT.Square).then_inc(s["b_sq"], 1)

            def b_hi(h, c):
                act.wait_ge(s["b_sq"], 2 * h + c + 1)
                if c == 1:
                    act.wait_ge(s["b_rope"], 2 * h + 1)
                act.activation(pt_r[:, 3, :], pt[:, 2, :], ACT.Copy).then_inc(s["b_hi"], 1)

            def b_rn(h, c):
                act.wait_ge(s["b_ss"], 2 * h + c + 1)
                act.activation(pt[:, 2, :], A2[:], ACT.Ln, bias=eps[:, 0:1]).then_inc(s["b_ln"], 1)
                act.wait_ge(s["b_ln"], 2 * h + c + 1)
                act.activation(pt[:, 2, :], pt[:, 2, :], ACT.Exp, scale=-0.5).then_inc(s["b_rn"], 1)

            def softmax(h, t):
                act.wait_ge(s["s_nmax"], 4 * h + t + 1)
                if t >= 2:
                    act.wait_ge(s["pT_mm"], 4 * h + t - 1)
                elif t == 0:
                    act.wait_ge(s["bvT_mm"], h + 1)
                n = (t + 1) * P
                act.activation(probs[t % 2][:, :n], (A0, A1)[t % 2][:, :n], ACT.Exp, scale=SCALE,
                               bias=stat[:, 1, t:t + 1], accum_out=stat[:, 2, t:t + 1]).then_inc(s["s_exp"], 1)

            def pTc(h, t):
                act.wait_ge(s["pT_mm"], 4 * h + t + 1)
                act.activation(pt[:, 0:t + 1, tile4(t)],
                               A2[:, :(t + 1) * P].rearrange("p (k c) -> p k c", c=P), ACT.Copy).then_inc(s["pT"], 1)

            def split_next(i, w):
                c = w + 1
                split(i * NW + c, c % RING, i * (NW // RING) + (c // RING + 1))

            def head(h, p):
                if p is not None:
                    evac(p, NW - 1)
                    split_next(h, 0)
                    cgrow(h)
                if p is not None:
                    softmax(p, 0)
                    zsig(p, 1)
                    softmax(p, 1)
                    pTc(p, 0)
                    softmax(p, 2)
                    pTc(p, 1)
                    softmax(p, 3)
                    evac(h, 0)
                    split_next(h, 1)
                    pTc(p, 2)
                    pTc(p, 3)
                    silu(h, 0)
                    sq(h, 0)
                else:
                    evac(h, 0)
                    decay_steps()
                    split_next(h, 1)
                    silu(h, 0)
                    decay_exps()
                    sq(h, 0)
                evac(h, 1)
                split_next(h, 2)
                if p is None:
                    cgrow(h)
                rnorm(h, 0)
                silu(h, 1)
                sq(h, 1)
                rnorm(h, 1)
                evac(h, 2)
                split_next(h, 3)
                n1(h)
                n2(h)
                silu(h, 2)
                n3(h)
                evac(h, 3)
                split_next(h, 4)
                ma(h, 0)
                zsig(h, 0)
                ma(h, 1)
                ma(h, 2)
                evac(h, 4)
                split_next(h, 5)
                b_sq(h, 0)
                vnew(h, 0)
                b_hi(h, 0)
                b_rn(h, 0)
                vnew(h, 1)
                evac(h, 5)
                vnew(h, 2)
                split_next(h, 6)
                b_sq(h, 1)
                b_hi(h, 1)
                vnew(h, 3)
                b_rn(h, 1)
                if p is not None:
                    act.wait_ge(s["ob_out"], 16 * h)
                gnorm_sq(h)
                evac(h, 6)
                gnorm(h)
                split_next(h, 7)

            act.wait_ge(s["ones_set"], 3)
            act.activation(ones[:], ones_f[:], ACT.Copy)
            act.activation(mean[:], ones_f[:], ACT.Copy, scale=1.0 / P)

            def x_rstd(t):
                act.wait_ge((s["x_loaded0"], s["x_loaded1"], s["x_loaded2"], s["x_loaded3"])[t], 16)
                if t > 0:
                    act.wait_ge(s["x_sq"], t)
                act.activation(xsq[:], xt[:, t, :], ACT.Square, accum_out=ssx[:, t:t + 1]).then_inc(s["x_sq"], 1)
                act.wait_ge(s["x_sq"], t + 1)
                act.activation(rsx[:, t:t + 1], ssx[:, t:t + 1], ACT.Ln, scale=1.0 / D, bias=eps[:, 0:1])\
                    .then_inc(s["x_ln"], 1)
                act.wait_ge(s["x_ln"], t + 1)
                act.activation(rsx[:, t:t + 1], rsx[:, t:t + 1], ACT.Exp, scale=-0.5).then_inc(s["x_rstd"], 1)

            def x_hi(t):
                for q in range(4):
                    act.wait_ge(s["x_T"], 4 * t + q + 1)
                    act.activation(h_hi[:, 4 * q:4 * q + 4, tile4(t)], q4((G0, G1, G2, A0)[q]), ACT.Copy)\
                        .then_inc(s["x_hi"], 1)

            x_rstd(0)
            x_rstd(1)
            x_hi(0)
            x_rstd(2)
            x_hi(1)
            act.wait_ge(s["w16_loaded"], 16)
            act.activation(w16s[:, :, 0, :], w16[:], ACT.Copy).then_inc(s["w16_hi"], 1)
            x_rstd(3)
            x_hi(2)
            split_at(0)
            x_hi(3)
            split_at(1)

            def decay_steps():
                act.wait_ge(s["ba_step"], 2)
                sigmoid(ba[:, 0], s["ba_step"], 2)
                act.wait_ge(s["ba_step"], 5)
                act.activation(ba[:, 2], ba[:, 1], ACT.Abs).then_inc(s["ba_step"], 1)
                act.wait_ge(s["ba_step"], 6)
                act.activation(ba[:, 2], ba[:, 2], ACT.Exp, scale=-1.0).then_inc(s["ba_step"], 1)
                act.wait_ge(s["ba_step"], 7)
                act.activation(ba[:, 2], ba[:, 2], ACT.Ln, bias=1.0).then_inc(s["ba_step"], 1)
                act.activation(alog, alog, ACT.Exp).then_inc(s["ba_step"], 1)

            def decay_exps():
                act.wait_ge(s["ba_step"], BA_G + 3)
                act.activation(ba[:, 3], ba[:, 3], ACT.Exp).then_inc(s["ba_step"], 1)
                act.activation(ba[:, 4], ba[:, 1], ACT.Exp).then_inc(s["ba_step"], 1)
                act.activation(ba[:, 2], ba[:, 2], ACT.Exp).then_inc(s["ba_step"], 1)

            act.wait_ge(s["ba_mm"], 1)
            act.activation(baT, A1[:4 * H, :], ACT.Copy).then_inc(s["ba_copied"], 1)
            act.wait_ge(s["rows_loaded"], 96)

            head(0, None)
            with act.Fori(1, H) as i:
                head(i, i - 1)

            last = H - 1
            evac(last, NW - 1)
            split_at(N1 + 1)
            softmax(last, 0)
            zsig(last, 1)
            softmax(last, 1)
            pTc(last, 0)
            softmax(last, 2)
            pTc(last, 1)
            softmax(last, 3)

            def gate_sigmoid(u, which, count):
                act.wait_ge(s["g_evac"], count + 1)
                sigmoid(sg[:, u, which, :], s["g_sig"], 3 * count)

            def act_split(c, dst, count=4):
                act.wait_ge((s["act_loaded0"], s["act_loaded1"])[c % 2], 16 * (c // 2 + 1))
                act.activation(dst.rearrange("p k t -> p (k t)"), act_raw[:, c % 2, :count * T],
                               ACT.Copy).then_inc(s["act_hi"], 1)

            act_split(0, o_split[:, 0, 0])
            split_at(N1 + 2)
            pTc(last, 2)
            pTc(last, 3)
            act_split(1, o_split[:, 1, 0])
            gate_sigmoid(0, 0, 0)
            split_at(N1 + 3)
            act.wait_ge(s["ob_out"], 16 * H)
            act_split(2, o_split[:, 2, 0])
            gate_sigmoid(0, 1, 1)
            act_split(3, o_split[:, 3, 0])
            split_at(N2, (0, 1))
            gate_sigmoid(1, 0, 2)

            def tile_splits(jj, u):
                def nth(k):
                    c = 3 * u + k
                    return jj * 12 + (N2 + c), c % RING, jj * 3 + ((N2 + c) // RING + 1)
                split(*nth(1))
                gate_sigmoid((u + 1) % 2, 1, 8 * jj + (2 * u + 3))
                split(*nth(2))
                split(*nth(3), ((u + 1) % 2, jj * 2 + ((u + 1) // 2 + 1)))
                gate_sigmoid(u % 2, 0, 8 * jj + (2 * u + 4))

            with act.Fori(0, (KT - 2) // 4) as jj:
                for u in range(4):
                    tile_splits(jj, u)
            for u in range((KT - 2) % 4):
                tile_splits((KT - 2) // 4, u)
            split_at(N3 - 1, (1, KT // 2))
            gate_sigmoid(1, 1, 2 * KT - 1)
            act.wait_ge(s["win_done"], N3 - 2)
            def last_hi(u):
                act.wait_ge(s["mg"], KT - 1 + u)
                act.activation(h_hi[:, KT - 2 + u, :], mgt[:, u, :], ACT.Copy).then_inc(s["last_hi"], 1)

            act_split(OCH, h_hi[:, 0:4])
            act_split(OCH + 1, h_hi[:, 4:8])
            split_at(N3)
            last_hi(0)
            act_split(OCH + 2, h_hi[:, 8:12])
            act_split(OCH + 3, h_hi[:, 12:14], 2)
            split_at(N3 + 1)
            last_hi(1)
            with act.Fori(0, 3) as eb:
                for k in range(2, 6):
                    split(eb * 4 + (N3 + k), k % RING, eb + ((N3 + k) // RING + 1))
            for k in range(14, 16):
                split_at(N3 + k)

        @block.vector
        def _(dve):
            def split(n, slot):
                dve.wait_ge(s["hi_ready"], n + 1)
                dve.tensor_tensor(w_lo[slot][:], raw[slot][:], w_hi[slot % 2][:].bitcast(F32), ALU.subtract)\
                    .then_inc(s["lo_ready"], 1)

            def columns(h):
                dve.tensor_copy(hcol[:].rearrange("p k t -> p (k t)"),
                                hc[:, bass.ds(h, 1), :, :].rearrange("p h k t -> p (h k t)")).then_inc(s["hcol"], 1)

            def cgrow(h):
                dve.wait_ge(s["cgrow_mm"], h + 1)
                dve.wait_ge(s["cg_dts"], h)
                for t in range(NT):
                    dve.scalar_tensor_tensor(dT[:, tile4(t)], G2[:, tile4(t)], hcol[:, HC_CG, t:t + 1],
                                             cst[:, C_DMASK, :], ALU.subtract, ALU.add).then_inc(s["cg_arg"], 1)

            def conv(h, c):
                name, col = (("gk", H), ("gq", 0), ("gv", 2 * H))[c]
                r, y = rawc[name], cv[name]
                dve.wait_ge(s["win_evac"], h * NW + c + 1)
                dve.wait_ge((s["ks_mm"], s["qk_mm"], s["vT_mm"])[c], (3 * h, h, h)[c])

                def tap(j):
                    return chan[:, bass.ds(h + (R_CONV + 3 * H * j + col), 1)]

                n = 12 * h + 4 * c
                dve.tensor_scalar(y[:], r[:, 4:4 + T], tap(3), None, ALU.mult).then_inc(s["conv"], 1)
                for j in range(3):
                    dve.wait_ge(s["conv"], n + j + 1)
                    dve.scalar_tensor_tensor(y[:], r[:, 1 + j:1 + j + T], tap(j), y[:], ALU.mult, ALU.add)\
                        .then_inc(s["conv"], 1)
                dve.wait_ge(s["conv"], n + 4)
                dve.tensor_scalar(r[:, 4:], y[:], LEAST, None, ALU.max).then_inc(s["clampd"], 1)

            def silu(h, c):
                name = ("gk", "gq", "gv")[c]
                dve.wait_ge(s["sig"], 9 * h + 3 * c + 3)
                dve.tensor_tensor(cv[name][:], cv[name][:], rawc[name][:, 4:], ALU.mult).then_inc(s["silu"], 1)

            def sq_lo(h, c):
                k = ("gk", "gq")[c]
                dve.wait_ge(s["sq_hi"], 2 * h + c + 1)
                dve.tensor_tensor(rawc_r[k][:, 4:], rawc[k][:, 4:], onorm_r[:].bitcast(F32), ALU.subtract).then_inc(s["sq_lo"], 1)

            def norm(h, c):
                name = ("gk", "gq")[c]
                dve.wait_ge(s["rn"], 2 * h + c + 1)
                dve.tensor_tensor(cv[name][:], cv[name][:], rawc[name][:, 4:], ALU.mult).then_inc(s["norm"], 1)

            def kT(h):
                dve.wait_ge(s["kT_mm"], h + 1)
                dve.wait_ge(s["st_mm"], 3 * h)
                dve.tensor_tensor(q4(kdec), q4(G0), hcb(HC_KD), ALU.mult).then_inc(s["kdec"], 1)

            def kk(h):
                dve.wait_ge(s["kk_mm"], h + 1)
                dve.wait_ge(s["cg_dts"], h + 1)
                dve.wait_ge(s["mb_mm"], 3 * h)
                dve.tensor_tensor(Up[:], G2[:], dTs[:], ALU.mult).then_inc(s["kkd"], 1)

            def UT(h):
                dve.wait_ge(s["UT_mm"], h + 1)
                dve.wait_ge(s["ma_mm"], 3 * h)
                dve.tensor_tensor(q4(Ln), q4(G0), hcb(HC_NB), ALU.mult).then_inc(s["Ln"], 1)

            def LT(h):
                dve.wait_ge(s["LT_mm"], h + 1)
                dve.wait_ge(s["o_mm"], 4 * h)
                dve.tensor_tensor(q4(Ud), q4(G2), over(cst[:, C_M16, :]), ALU.mult).then_inc(s["Ud"], 1)
                dve.wait_ge(s["o_out"], 16 * h)
                dve.tensor_tensor(q4(Ld), q4(Ln), over(cst[:, C_M16, :]), ALU.mult).then_inc(s["Ld"], 1)
                dve.wait_ge(s["Ud"], h + 1)
                dve.tensor_tensor(q4(xa), q4(Ud), over(ident), ALU.add).then_inc(s["X1"], 1)

            def qk(h):
                dve.wait_ge(s["cg_dt"], h + 1)
                dve.wait_ge(s["qk_mm"], h + 1)
                dve.tensor_tensor(qkT[:], G1[:], dT[:], ALU.mult).then_inc(s["qkd"], 1)
                dve.wait_ge(s["cg_eg"], h + 1)
                dve.wait_ge(s["norm"], 2 * h + 2)
                dve.tensor_tensor(qdec[:], cv["gq"][:], Eg[:], ALU.mult).then_inc(s["qdec"], 1)

            def n1(h):
                dve.wait_ge(s["n1_mm"], h + 1)
                dve.tensor_copy(U2[:], G1[:]).then_inc(s["U2"], 1)

            def n2(h):
                dve.wait_ge(s["n2_mm"], h + 1)
                dve.wait_ge(s["X1"], h + 1)
                dve.wait_ge(s["vn_mm"], 4 * h)
                dve.tensor_tensor(xb[:], G2[:], xa[:], ALU.add).then_inc(s["X2"], 1)

            def n3(h):
                dve.wait_ge(s["n3_mm"], h + 1)
                dve.wait_ge(s["X2"], h + 1)
                dve.tensor_tensor(xa[:], G2[:], xb[:], ALU.add).then_inc(s["X4"], 1)

            def n4(h):
                dve.wait_ge(s["n4_mm"], h + 1)
                dve.wait_ge(s["X4"], h + 1)
                dve.tensor_tensor(xb[:], G2[:], xa[:], ALU.add).then_inc(s["X8"], 1)

            def vTs(h):
                dve.wait_ge(s["vT_mm"], h + 1)
                dve.tensor_tensor(q4(vb), q4(G1), hcb(HC_B), ALU.mult).then_inc(s["vb"], 1)

            def ma(h, k):
                dve.wait_ge(s["ma_mm"], 3 * h + k + 1)
                if k < 2:
                    dve.tensor_copy(XTt[:], G1[:]).then_inc(s["XT"], 1)
                else:
                    dve.tensor_copy(corner(XTt, 0), corner(G1, 0)).then_inc(s["XT"], 1)

            def mb(h, k):
                a, b = ((xb, xa), (xa, xb), (corner(xb, 1), corner(xb, 1)))[k]
                dve.wait_ge(s["mb_mm"], 3 * h + k + 1)
                if k == 0:
                    dve.wait_ge(s["X8"], h + 1)
                else:
                    dve.wait_ge(s["X"], 3 * h + k)
                g = G2[:] if k < 2 else corner(G2, 1)
                dve.tensor_tensor(b[:], g, a[:], ALU.add).then_inc(s["X"], 1)

            def kS(h, t):
                dve.wait_ge(s["ks_mm"], 3 * h + t)
                dve.wait_ge(s["vb"], h + 1)
                dve.scalar_tensor_tensor(vb[:, tile4(t)], G1[:, :P], hcol[:, HC_NBE, t:t + 1], vb[:, tile4(t)],
                                         ALU.mult, ALU.add).then_inc(s["vbk"], 1)

            def state(h, t):
                dve.wait_ge(s["st_mm"], 3 * h + t + 1)
                if t == 0:
                    dve.tensor_copy(st[0][:], G2[:, :P]).then_inc(s["st"], 1)
                else:
                    dve.wait_ge(s["st"], 3 * h + t)
                    dve.scalar_tensor_tensor(st[t % 2][:], st[(t - 1) % 2][:], hcol[:, HC_GL, t:t + 1], G2[:, :P],
                                             ALU.mult, ALU.add).then_inc(s["st"], 1)

            def o_lo_(h):
                dve.wait_ge(s["o_hi"], h + 1)
                dve.tensor_tensor(onorm_r[:], onorm[:], w1_r[:].bitcast(F32), ALU.subtract).then_inc(s["o_lo"], 1)

            def gnorm(h):
                dve.wait_ge(s["o_rn"], h + 1)
                dve.scalar_tensor_tensor(o1[:], G0[:], chan[:, R_GW:R_GW + 1], onorm[:], ALU.mult, ALU.mult)\
                    .then_inc(s["o_1"], 1)
                dve.wait_ge(s["o_1"], h + 1)
                dve.wait_ge(s["zs"], 2 * h + 1)
                dve.tensor_tensor(o1[:], o1[:], zA[:], ALU.mult).then_inc(s["o_2"], 1)

            def zclamp(h, b):
                dve.wait_ge(s["win_evac"], h * NW + (4, 8)[b])
                dve.tensor_scalar(zt[:], (zA, zB)[b][:], LEAST, None, ALU.max).then_inc(s["zclamp"], 1)

            def zmul(h, b):
                z = (zA, zB)[b]
                dve.wait_ge(s["zsig"], 6 * h + 3 * b + 3)
                dve.tensor_tensor(z[:], z[:], zt[:], ALU.mult).then_inc(s["zs"], 1)

            def b_lo(h, c):
                dve.wait_ge(s["b_hi"], 2 * h + c + 1)
                dve.tensor_tensor(pt_r[:, 2, :], pt[:, 2, :], pt_r[:, 3, :].bitcast(F32), ALU.subtract)\
                    .then_inc(s["b_lo"], 1)

            def b_norm(h, c):
                r, w = ((kr, R_KW), (qr, R_QW))[c]
                x_ = pt[:, c, :]
                lo, hi = slice(0, P // 2), slice(P // 2, P)
                dve.wait_ge(s["b_rn"], 2 * h + c + 1)
                dve.scalar_tensor_tensor(x_, x_, chan[:, w:w + 1], pt[:, 2, :], ALU.mult, ALU.mult)\
                    .then_inc(s["b_n"], 1)
                dve.wait_ge(s["b_n"], 2 * h + c + 1)
                dve.wait_ge(s["rope_loaded"], 16)
                if c == 0:
                    dve.wait_ge(s["pv_mm"], h)
                dve.tensor_tensor(pt[lo, 3, :], pt[hi, c, :], cossin[hi, 1, :], ALU.mult).then_inc(s["b_sinlo"], 1)
                dve.tensor_tensor(pt[hi, 3, :], pt[lo, c, :], cossin[lo, 1, :], ALU.mult).then_inc(s["b_sinhi"], 1)
                dve.wait_ge(s["b_sinlo"], 2 * h + c + 1)
                dve.wait_ge(s["b_sinhi"], 2 * h + c + 1)
                dve.wait_ge(s["b_cos"], 2 * h + c + 1)
                dve.tensor_tensor(r[:], r[:], pt[:, 3, :], ALU.add).then_inc(s["b_rope"], 1)

            def bvTs(h):
                dve.wait_ge(s["bvT_mm"], h + 1)
                dve.wait_ge(s["pv_mm"], h)
                dve.tensor_copy(vT[:], A2[:]).then_inc(s["bvT"], 1)

            def softmax_max(h, t):
                ps = (A0, A1)[t % 2]
                dve.wait_ge(s["s_mm"], 4 * h + t + 1)
                dve.tensor_tensor(ps[:, tile4(t)], ps[:, tile4(t)], cst[:, C_CMASK, :], ALU.add)\
                    .then_inc(s["s_mask"], 1)
                dve.wait_ge(s["s_mask"], 4 * h + t + 1)
                dve.tensor_reduce(stat[:, 0, t:t + 1], ps[:, :(t + 1) * P], AX_X, ALU.max).then_inc(s["s_max"], 1)
                dve.wait_ge(s["s_max"], 4 * h + t + 1)
                dve.tensor_scalar(stat[:, 1, t:t + 1], stat[:, 0, t:t + 1], -SCALE, None, ALU.mult)\
                    .then_inc(s["s_nmax"], 1)

            def softmax_norm(h, t):
                pr = probs[t % 2][:, :(t + 1) * P]
                dve.wait_ge(s["s_exp"], 4 * h + t + 1)
                dve.reciprocal(stat[:, 3, t:t + 1], stat[:, 2, t:t + 1]).then_inc(s["s_rec"], 1)
                dve.wait_ge(s["s_rec"], 4 * h + t + 1)
                dve.tensor_scalar(pr, pr, stat[:, 3, t:t + 1], None, ALU.mult).then_inc(s["s_norm"], 1)

            def attn_out(h):
                dve.wait_ge(s["pv_mm"], h + 1)
                dve.wait_ge(s["zs"], 2 * h + 2)
                dve.tensor_tensor(pr1[:], A0[:], zB[:], ALU.mult).then_inc(s["ob"], 1)

            def head(h, p):
                n = h * NW
                if p is None:
                    decays()
                    dve.wait_ge(s["pads"], 3)
                    conv(h, 0)
                    cumulated()
                    split(n + 2, 2)
                    silu(h, 0)
                    head_columns()
                    columns(h)
                    sq_lo(h, 0)
                    cgrow(h)
                else:
                    columns(h)
                    split(n + 1, 1)
                    cgrow(h)
                    softmax_max(p, 0)
                    zclamp(p, 1)
                    softmax_max(p, 1)
                    softmax_norm(p, 0)
                    zmul(p, 1)
                    softmax_max(p, 2)
                    softmax_norm(p, 1)
                    softmax_max(p, 3)
                    softmax_norm(p, 2)
                    softmax_norm(p, 3)
                    conv(h, 0)
                    split(n + 2, 2)
                    silu(h, 0)
                    attn_out(p)
                    sq_lo(h, 0)
                conv(h, 1)
                norm(h, 0)
                split(n + 3, 3)
                kT(h)
                silu(h, 1)
                kk(h)
                sq_lo(h, 1)
                UT(h)
                norm(h, 1)
                LT(h)
                qk(h)
                split(n + 4, 0)
                n1(h)
                conv(h, 2)
                n2(h)
                silu(h, 2)
                n3(h)
                n4(h)
                vTs(h)
                zclamp(h, 0)
                ma(h, 0)
                split(n + 5, 1)
                zmul(h, 0)
                mb(h, 0)
                ma(h, 1)
                mb(h, 1)
                ma(h, 2)
                mb(h, 2)
                split(n + 6, 2)
                b_lo(h, 0)
                state(h, 0)
                kS(h, 1)
                b_norm(h, 0)
                state(h, 1)
                kS(h, 2)
                state(h, 2)
                split(n + 7, 3)
                b_lo(h, 1)
                kS(h, 3)
                o_lo_(h)
                b_norm(h, 1)
                gnorm(h)
                split(n + 8, 0)
                bvTs(h)

            dve.sem_inc(s["resid"], NT + 1)
            dve.wait_ge(s["nw_loaded"], 16)

            def x_scale(t):
                dve.wait_ge(s["x_rstd"], t + 1)
                dve.scalar_tensor_tensor(xt[:, t, :X_SPLIT], xt[:, t, :X_SPLIT], rsx[:, t:t + 1],
                                         nw[:, :X_SPLIT], ALU.mult, ALU.mult).then_inc(s["x_scaled_a"], 1)

            def x_lo(t):
                for q in range(4):
                    dve.wait_ge(s["x_hi"], 4 * t + q + 1)
                    dve.tensor_tensor(h_lo[:, 4 * q:4 * q + 4, tile4(t)], q4((G0, G1, G2, A0)[q]),
                                      h_hi[:, 4 * q:4 * q + 4, tile4(t)].bitcast(F32), ALU.subtract)\
                        .then_inc(s["x_lo"], 1)

            x_scale(0)
            x_scale(1)
            x_lo(0)
            x_scale(2)
            x_lo(1)
            dve.wait_ge(s["w16_hi"], 1)
            dve.tensor_tensor(w16s[:, :, 1, :], w16[:], w16s[:, :, 0, :].bitcast(F32), ALU.subtract).then_inc(s["w16_lo"], 1)
            x_scale(3)
            x_lo(2)
            split(0, 0)
            dve.wait_ge(s["rows_T"], 1)
            dve.tensor_copy(chan[:], A2[:, :P]).then_inc(s["rows_ready"], 1)
            x_lo(3)
            split(1, 1)
            dve.wait_ge(s["rows_ready"], 1)

            def decays():
                dve.wait_ge(s["ba_T"], 1)
                dve.wait_ge(s["rows_loaded"], 96)
                parts = A0[:, :NT * 4 * H].rearrange("p (t b c) -> p t b c", t=NT, b=2)
                dve.tensor_copy(ab, parts[:, :, 0, :]).then_inc(s["ab_sum"], 1)
                dve.wait_ge(s["ab_sum"], 1)
                dve.tensor_tensor(ab, ab, parts[:, :, 1, :], ALU.add).then_inc(s["ab_sum"], 1)
                dve.wait_ge(s["ab_sum"], 2)
                dve.tensor_scalar(ba[:, 0], ab[:, :, 0:H], LEAST, None, ALU.max).then_inc(s["ba_step"], 1)
                dve.tensor_tensor(ba[:, 1], ab[:, :, H:2 * H], dtb.unsqueeze(1).broadcast_to([P, NT, H]), ALU.add)\
                    .then_inc(s["ba_step"], 1)
                dve.wait_ge(s["ba_step"], 9)
                dve.scalar_tensor_tensor(ba[:, 3], ba[:, 1], 0.0, ba[:, 2], ALU.max, ALU.add)\
                    .then_inc(s["ba_step"], 1)
                dve.wait_ge(s["ba_step"], 10)
                dve.scalar_tensor_tensor(ba[:, 5], ba[:, 3], -1.0, alog.unsqueeze(1).broadcast_to([P, NT, H]),
                                         ALU.mult, ALU.mult).then_inc(s["ba_step"], 1)

            def cumulated():
                dve.wait_ge(s["cg_mm"], 1)
                cg = A2[:, :NT * H].rearrange("p (t h) -> p t h", t=NT)
                gl = A2[:, NT * H:2 * NT * H].rearrange("p (t h) -> p t h", t=NT)
                dve.tensor_copy(ba[:, 1], cg).then_inc(s["ba_step"], 1)
                dve.tensor_copy(ba[:, 2], gl).then_inc(s["ba_step"], 1)
                dve.wait_ge(s["ba_step"], 13)
                dve.tensor_tensor(ba[:, 3], ba[:, 2], ba[:, 1], ALU.subtract).then_inc(s["ba_step"], 1)

            def head_columns():
                dve.wait_ge(s["ba_step"], 17)
                dve.tensor_tensor(ba[:, 4], ba[:, 4], ba[:, 0], ALU.mult).then_inc(s["ba_step"], 1)
                dve.wait_ge(s["ba_step"], 18)
                for kind, b in ((HC_G, 5), (HC_CG, 1), (HC_B, 0), (HC_KD, 3), (HC_GL, 2)):
                    dve.tensor_copy(hc[:, :, kind, :], ba[:, b].rearrange("p t h -> p h t")).then_inc(s["hc_set"], 1)
                for kind, b in ((HC_NB, 0), (HC_NBE, 4)):
                    dve.tensor_scalar(hc[:, :, kind, :], ba[:, b].rearrange("p t h -> p h t"), -1.0, None, ALU.mult)\
                        .then_inc(s["hc_set"], 1)
                dve.wait_ge(s["hc_set"], NHC)

            head(0, None)
            with dve.Fori(1, H) as i:
                head(i, i - 1)

            def gate_evac(n, slot, u, which):
                dve.wait_ge(s["win_done"], n + 1)
                dve.tensor_scalar(sg[:, u, which, :], PJ[slot][:], LEAST, None, ALU.max).then_inc(s["g_evac"], 1)

            def act_split(c, src, dst, count=4):
                dve.wait_ge(s["act_hi"], c + 1)
                dve.tensor_tensor(dst.rearrange("p k t -> p (k t)"), act_raw[:, c % 2, :count * T],
                                  src.rearrange("p k t -> p (k t)").bitcast(F32), ALU.subtract)\
                    .then_inc(s["act_lo"], 1)

            def merge(n, u, j):
                dve.wait_ge(s["win_done"], n + 1)
                dve.wait_ge(s["g_sig"], 6 * j + 6)
                a, b = ((G0, G1), (A0, A1))[u]
                dve.tensor_tensor(sg[:, u, 0, :], a[:], sg[:, u, 0, :], ALU.mult).then_inc(s["ya"], 1)
                dve.tensor_tensor(sg[:, u, 1, :], b[:], sg[:, u, 1, :], ALU.mult).then_inc(s["yb"], 1)
                dve.wait_ge(s["ya"], j + 1)
                dve.wait_ge(s["yb"], j + 1)
                dve.tensor_tensor(mgt[:, u, :], sg[:, u, 0, :], sg[:, u, 1, :], ALU.add).then_inc(s["mg"], 1)

            last = H - 1
            split(N1 + 1, 1)
            softmax_max(last, 0)
            zclamp(last, 1)
            softmax_max(last, 1)
            softmax_norm(last, 0)
            zmul(last, 1)
            softmax_max(last, 2)
            softmax_norm(last, 1)
            softmax_max(last, 3)
            softmax_norm(last, 2)
            softmax_norm(last, 3)
            gate_evac(N1, 0, 0, 0)
            split(N1 + 2, 2)
            act_split(0, o_split[:, 0, 0], o_split[:, 0, 1])
            attn_out(last)
            act_split(1, o_split[:, 1, 0], o_split[:, 1, 1])
            gate_evac(N1 + 1, 1, 0, 1)
            split(N1 + 3, 3)
            act_split(2, o_split[:, 2, 0], o_split[:, 2, 1])
            act_split(3, o_split[:, 3, 0], o_split[:, 3, 1])
            gate_evac(N1 + 2, 0, 1, 0)
            split(N2, 0)
            def tile_steps(jj, u):
                n, j = jj * 12 + (N2 + 3 * u), jj * 4 + u
                gate_evac(n - 1, (u + 1) % 2, (u + 1) % 2, 1)
                split(n + 1, (3 * u + 1) % RING)
                split(n + 2, (3 * u + 2) % RING)
                merge(n, u % 2, j)
                split(n + 3, (3 * u + 3) % RING)
                dve.wait_ge(s["mg"], j + 1)
                gate_evac(n + 1, (u + 1) % 2, u % 2, 0)
                if u % 2 == 1:
                    dve.wait_ge(s["mg_out"], 16 * (j + 1))

            with dve.Fori(0, (KT - 2) // 4) as jj:
                for u in range(4):
                    tile_steps(jj, u)
            for u in range((KT - 2) % 4):
                tile_steps((KT - 2) // 4, u)
            gate_evac(N3 - 3, 1, 1, 1)
            split(N3 - 1, 3)
            def last_lo(u):
                dve.wait_ge(s["last_hi"], u + 1)
                dve.tensor_tensor(h_lo[:, KT - 2 + u, :], mgt[:, u, :], h_hi[:, KT - 2 + u, :].bitcast(F32),
                                  ALU.subtract).then_inc(s["last_lo"], 1)

            act_split(OCH, h_hi[:, 0:4], h_lo[:, 0:4])
            act_split(OCH + 1, h_hi[:, 4:8], h_lo[:, 4:8])
            merge(N3 - 2, 0, KT - 2)
            split(N3, 0)
            last_lo(0)
            act_split(OCH + 2, h_hi[:, 8:12], h_lo[:, 8:12])
            act_split(OCH + 3, h_hi[:, 12:14], h_lo[:, 12:14], 2)
            merge(N3 - 1, 1, KT - 1)
            split(N3 + 1, 1)
            last_lo(1)

            def residual(eb):
                dve.wait_ge(s["x3_loaded"], 16 * (eb + 1))
                dve.wait_ge(s["out_stored"], 16 * NT * eb)
                for t in range(NT):
                    if t < NT - 1:
                        dve.wait_ge(s["p3_done"], eb * (NT - 1) + (t + 1))
                    else:
                        dve.wait_ge(s["win_done"], eb * 4 + (N3 + 4))
                    dve.tensor_tensor(y3[:, t, :], bank[4 * (eb % 2) + t][:], x3[:, t, :], ALU.add).then_inc(s["resid"], 1)

            for eb in range(D // 512):
                for k in range(4 * eb + 2, min(4 * eb + 6, 16)):
                    split(N3 + k, k % RING)
                residual(eb)


_INS = ["x", "norm_w", "w_in", "gdn_conv_w", "gdn_a_log", "gdn_dt_bias", "gdn_norm_w", "moba_q_norm_w",
        "moba_k_norm_w", "w_out_gdn", "w_out_moba", "w_o"]


def shape_constants():
    r, c = np.arange(P)[:, None], np.arange(P)[None, :]
    cst = np.zeros((P, NCONST, P), np.float32)
    cst[:, C_ID] = r == c
    cst[:, C_TRIU] = r <= c
    cst[:, C_DMASK] = np.where(r <= c, 0.0, NEG)
    cst[:, C_CMASK] = np.where(c <= r, 0.0, NEG)
    cst[:, C_STRICT] = r < c
    cst[:, C_M16] = r // 16 == c // 16
    for col, b in ((C_L32, 16), (C_L64, 32)):
        cst[:, col] = (r // b == c // b + 1) & (r // (2 * b) == c // (2 * b))
    freq = np.float32(10000.0) ** (-np.arange(0, P, 2, dtype=np.float32) / np.float32(P))
    ang = np.arange(T, dtype=np.float32)[None, :] * freq.astype(np.float32)[:, None]
    rope = np.empty((P, 2, T), np.float32)
    rope[:P // 2, 0] = rope[P // 2:, 0] = np.cos(ang)
    rope[:P // 2, 1] = np.sin(ang)
    rope[P // 2:, 1] = -np.sin(ang)
    return cst, rope


def kernel(**inputs):
    import concourse.bacc as _bacc
    from concourse.bass_utils import run_bass_kernel_spmd as _run

    nc = _bacc.Bacc("TRN2", target_bir_lowering=False, num_devices=1)
    arrays, args = {}, []
    for name in _INS:
        arrays[f"in_{name}_dram"] = np.ascontiguousarray(inputs[name])
    arrays["const_masks"], arrays["const_rope"] = shape_constants()
    for name, a in arrays.items():
        args.append(nc.dram_tensor(name, a.shape, mybir.dt.from_np(a.dtype), kind="ExternalInput").ap())
    args.append(nc.dram_tensor("out_0_dram", (1, T, D), F32, kind="ExternalOutput").ap())
    hybrid_layer(nc, *args)
    r = _run(nc, [arrays], core_ids=[0])
    return r.results[0]["out_0_dram"]
```
